# Optimizing a Trainium2 kernel written in Bass

```python
import math
import jax
import jax.numpy as jnp
from jax import lax
import numpy as np
import jax, jax.numpy as jnp

D_MODEL = 1024
BATCH = 1
SEQ = 256
DEPTH = 2

HEAD_DIM = 64
GDN_WIDTH = 3 * D_MODEL // 8
CONV_WIDTH = D_MODEL // 4
FOX_WIDTH = D_MODEL - GDN_WIDTH - CONV_WIDTH
MIX_WIDTH = GDN_WIDTH + CONV_WIDTH + FOX_WIDTH
GDN_HEADS = GDN_WIDTH // HEAD_DIM
FOX_HEADS = FOX_WIDTH // HEAD_DIM
GDN_SHORT_CONV = 4
GDN_CHUNK = 64
CONV_KERNEL = 31
FOX_BLOCK = 128
FFN_DENSE = ((8 * D_MODEL // 3 + 127) // 128) * 128
N_EXPERTS = 8
TOP_K = 2
FFN_EXPERT = 7 * D_MODEL // 2
MOE_BLOCK = 128
N_DENSE = (DEPTH + 1) // 2
N_MOE = DEPTH // 2
DEEPNORM_ALPHA = (2 * DEPTH) ** 0.25
DEEPNORM_BETA = (8 * DEPTH) ** -0.25
LN_EPS = 1e-5
NORM_EPS = 1e-6
IN_SIZES = (GDN_WIDTH, GDN_WIDTH, GDN_WIDTH, GDN_HEADS, GDN_HEADS, GDN_WIDTH,
            2 * CONV_WIDTH,
            FOX_WIDTH, FOX_WIDTH, FOX_WIDTH, FOX_HEADS)
IN_COLS = sum(IN_SIZES)


def layer_norm(x, g, b):
    xf = x.astype(jnp.float32)
    mu = xf.mean(-1, keepdims=True)
    var = jnp.square(xf - mu).mean(-1, keepdims=True)
    return ((xf - mu) * lax.rsqrt(var + LN_EPS) * g.astype(jnp.float32) + b.astype(jnp.float32)).astype(x.dtype)

def rms_norm_f32(x, g):
    xf = x.astype(jnp.float32)
    return xf * lax.rsqrt(jnp.square(xf).mean(-1, keepdims=True) + NORM_EPS) * g.astype(jnp.float32)

def l2_normalize(x):
    return x * lax.rsqrt(jnp.sum(jnp.square(x), -1, keepdims=True) + NORM_EPS)

def split_columns(p, sizes):
    cuts = np.cumsum(np.array(sizes))[:-1].tolist()
    return jnp.split(p, cuts, axis=-1)

def causal_depthwise_conv(x, w):
    k_width, channels = w.shape
    return lax.conv_general_dilated(
        x, w[:, None, :], window_strides=(1,), padding=[(k_width - 1, 0)],
        dimension_numbers=('NWC', 'WIO', 'NWC'), feature_group_count=channels)

def gated_delta_rule(q, k, v, g, beta):
    B, T, H, dk = q.shape
    dv = v.shape[-1]
    C = GDN_CHUNK
    n = T // C
    f32 = jnp.float32
    q = l2_normalize(q.astype(f32)) * dk ** -0.5
    k = l2_normalize(k.astype(f32))
    v = v.astype(f32)

    def chunks(t):
        return t.reshape(B, n, C, H, -1).transpose(1, 0, 3, 2, 4)

    qc, kc, vc = chunks(q), chunks(k), chunks(v)
    gc = jnp.cumsum(chunks(g.astype(f32)[..., None])[..., 0], axis=-1)
    bc = chunks(beta.astype(f32)[..., None])
    causal = jnp.tril(jnp.ones((C, C), bool))
    strict = jnp.tril(jnp.ones((C, C), bool), -1)
    diff = gc[..., :, None] - gc[..., None, :]
    decay = jnp.where(causal, jnp.exp(jnp.where(causal, diff, 0.0)), 0.0)
    kb = kc * bc
    lower = jnp.where(strict, jnp.einsum('nbhcd,nbhsd->nbhcs', kb, kc) * decay, 0.0)
    eye = jnp.eye(C, dtype=f32)
    t_inv = lax.linalg.triangular_solve(lower + eye, jnp.broadcast_to(eye, lower.shape),
                                        left_side=True, lower=True, unit_diagonal=True)
    u = jnp.einsum('nbhcs,nbhsd->nbhcd', t_inv, vc * bc)
    w = jnp.einsum('nbhcs,nbhsd->nbhcd', t_inv, kb * jnp.exp(gc)[..., None])
    a_intra = jnp.where(causal, jnp.einsum('nbhcd,nbhsd->nbhcs', qc, kc) * decay, 0.0)

    def step(state, inp):
        q_i, k_i, u_i, w_i, a_i, g_i = inp
        v_new = u_i - jnp.einsum('bhck,bhkv->bhcv', w_i, state)
        o_i = (jnp.einsum('bhck,bhkv->bhcv', q_i * jnp.exp(g_i)[..., None], state)
               + jnp.einsum('bhcs,bhsv->bhcv', a_i, v_new))
        g_last = g_i[..., -1]
        state = (state * jnp.exp(g_last)[..., None, None]
                 + jnp.einsum('bhck,bhcv->bhkv', k_i * jnp.exp(g_last[..., None] - g_i)[..., None], v_new))
        return state, o_i

    s0 = jnp.zeros((B, H, dk, dv), f32)
    _, o = lax.scan(step, s0, (qc, kc, u, w, a_intra, gc))
    return o.transpose(1, 0, 3, 2, 4).reshape(B, T, H, dv)

def forgetting_attention(q, k, v, log_f):
    B, T, H, d = q.shape
    f32 = jnp.float32
    nb = T // FOX_BLOCK
    c = jnp.cumsum(log_f.astype(f32), axis=1)
    qb = (q.astype(f32) * d ** -0.5).reshape(B, nb, FOX_BLOCK, H, d).transpose(1, 0, 3, 2, 4)
    cq = c.reshape(B, nb, FOX_BLOCK, H).transpose(1, 0, 3, 2)
    kt = k.astype(f32).transpose(0, 2, 1, 3)
    vt = v.astype(f32).transpose(0, 2, 1, 3)
    ck = c.transpose(0, 2, 1)
    key_pos = jnp.arange(T)

    def block(args):
        q_blk, cq_blk, i = args
        q_pos = i * FOX_BLOCK + jnp.arange(FOX_BLOCK)
        s = jnp.einsum('bhqd,bhkd->bhqk', q_blk, kt) + cq_blk[..., None] - ck[:, :, None, :]
        s = jnp.where(key_pos[None, :] <= q_pos[:, None], s, -jnp.inf)
        p = jax.nn.softmax(s, axis=-1)
        return jnp.einsum('bhqk,bhkd->bhqd', p, vt)

    o = lax.map(block, (qb, cq, jnp.arange(nb)))
    return o.transpose(1, 0, 3, 2, 4).reshape(B, T, H, d)

def hybrid_mixer(x, w_in, mix_scale, w_out, gdn_conv_w, gdn_a_log, gdn_dt_bias, gdn_norm_w,
                 cnv_dw_w, cnv_dw_b, cnv_ln_g, cnv_ln_b, fox_f_bias):
    B, T, _ = x.shape
    dt = x.dtype
    f32 = jnp.float32
    proj = jnp.einsum('btd,de->bte', x, w_in)
    (a_q, a_k, a_v, a_decay, a_beta, a_gate, c_glu, f_q, f_k, f_v, f_forget) = split_columns(proj, IN_SIZES)

    def heads(t, h):
        return t.reshape(B, T, h, HEAD_DIM)

    qkv = jax.nn.silu(causal_depthwise_conv(jnp.concatenate([a_q, a_k, a_v], -1), gdn_conv_w))
    a_q, a_k, a_v = jnp.split(qkv, 3, axis=-1)
    log_decay = -jnp.exp(gdn_a_log.astype(f32)) * jax.nn.softplus(a_decay.astype(f32) + gdn_dt_bias.astype(f32))
    beta = jax.nn.sigmoid(a_beta.astype(f32))
    o_a = gated_delta_rule(heads(a_q, GDN_HEADS), heads(a_k, GDN_HEADS), heads(a_v, GDN_HEADS), log_decay, beta)
    o_a = (rms_norm_f32(o_a, gdn_norm_w) * jax.nn.silu(heads(a_gate, GDN_HEADS).astype(f32))).reshape(B, T, GDN_WIDTH).astype(dt)

    glu_a, glu_b = jnp.split(c_glu, 2, axis=-1)
    u = glu_a * jax.nn.sigmoid(glu_b)
    u = causal_depthwise_conv(u, cnv_dw_w) + cnv_dw_b
    o_b = jax.nn.silu(layer_norm(u, cnv_ln_g, cnv_ln_b))

    log_f = jax.nn.log_sigmoid(f_forget.astype(f32) + fox_f_bias.astype(f32))
    o_c = forgetting_attention(heads(f_q, FOX_HEADS), heads(f_k, FOX_HEADS), heads(f_v, FOX_HEADS), log_f)
    o_c = o_c.reshape(B, T, FOX_WIDTH).astype(dt)

    mixed = jnp.concatenate([o_a, o_b, o_c], axis=-1) * mix_scale
    return jnp.einsum('bte,ed->btd', mixed, w_out)

def swiglu(x, w1, w3, w2):
    h = jax.nn.silu(jnp.einsum('btd,df->btf', x, w1)) * jnp.einsum('btd,df->btf', x, w3)
    return jnp.einsum('btf,fd->btd', h, w2)

def moe_swiglu(x, w_router, w1, w3, w2):
    B, T, D = x.shape
    xf = x.reshape(-1, D)
    n_tok = xf.shape[0]
    n_asg = n_tok * TOP_K
    logits = jnp.einsum('nd,de->ne', xf, w_router).astype(jnp.float32)
    top_logits, top_idx = lax.top_k(logits, TOP_K)
    gates = jax.nn.softmax(top_logits, axis=-1)
    e_flat = top_idx.reshape(-1)
    order = jnp.argsort(e_flat)
    e_sorted = e_flat[order]
    sizes = jnp.bincount(e_flat, length=N_EXPERTS).astype(jnp.int32)
    padded = ((sizes + MOE_BLOCK - 1) // MOE_BLOCK) * MOE_BLOCK
    pad_end = jnp.cumsum(padded)
    pad_start = pad_end - padded
    start = jnp.cumsum(sizes) - sizes
    rank = jnp.arange(n_asg, dtype=jnp.int32) - start[e_sorted]
    dest = pad_start[e_sorted] + rank
    n_blocks = (n_asg + MOE_BLOCK - 1) // MOE_BLOCK + N_EXPERTS
    rows = n_blocks * MOE_BLOCK
    tok_pad = jnp.full((rows,), n_tok, jnp.int32).at[dest].set((order // TOP_K).astype(jnp.int32))
    gate_pad = jnp.zeros((rows,), jnp.float32).at[dest].set(gates.reshape(-1)[order])
    block_start = jnp.arange(n_blocks, dtype=jnp.int32) * MOE_BLOCK
    block_expert = jnp.minimum(jnp.searchsorted(pad_end, block_start, side='right'), N_EXPERTS - 1)
    x_ext = jnp.concatenate([xf, jnp.zeros((1, D), xf.dtype)], axis=0)
    x_blocks = x_ext[tok_pad].reshape(n_blocks, MOE_BLOCK, D)

    def expert_block(args):
        xb, e = args
        h = jax.nn.silu(xb @ w1[e]) * (xb @ w3[e])
        return h @ w2[e]

    y = lax.map(expert_block, (x_blocks, block_expert)).reshape(rows, D)
    y = y * gate_pad[:, None].astype(y.dtype)
    out = jnp.zeros((n_tok + 1, D), y.dtype).at[tok_pad].add(y)[:n_tok]
    return out.reshape(B, T, D)

def first_inputs(seed: int = 0) -> dict:
    key = jax.random.key(seed)
    ks = jax.random.split(key, 26)
    f32 = jnp.float32
    nrm = jax.random.normal
    x = nrm(ks[0], (BATCH, SEQ, D_MODEL), f32)
    w_in = nrm(ks[1], (DEPTH, D_MODEL, IN_COLS), f32) * D_MODEL ** -0.5
    mix_scale = 1.0 + 0.05 * nrm(ks[2], (DEPTH, MIX_WIDTH), f32)
    w_out = nrm(ks[3], (DEPTH, MIX_WIDTH, D_MODEL), f32) * (MIX_WIDTH ** -0.5 * DEEPNORM_BETA)
    gdn_conv_w = nrm(ks[4], (DEPTH, GDN_SHORT_CONV, 3 * GDN_WIDTH), f32) * GDN_SHORT_CONV ** -0.5
    gdn_a_log = jnp.log(jax.random.uniform(ks[5], (DEPTH, GDN_HEADS), f32, 1.0, 16.0))
    dt_init = jnp.exp(jax.random.uniform(ks[6], (DEPTH, GDN_HEADS), f32, math.log(1e-3), math.log(1e-1)))
    gdn_dt_bias = dt_init + jnp.log(-jnp.expm1(-dt_init))
    gdn_norm_w = 1.0 + 0.05 * nrm(ks[7], (DEPTH, HEAD_DIM), f32)
    cnv_dw_w = nrm(ks[8], (DEPTH, CONV_KERNEL, CONV_WIDTH), f32) * CONV_KERNEL ** -0.5
    cnv_dw_b = 0.02 * nrm(ks[9], (DEPTH, CONV_WIDTH), f32)
    cnv_ln_g = 1.0 + 0.05 * nrm(ks[10], (DEPTH, CONV_WIDTH), f32)
    cnv_ln_b = 0.02 * nrm(ks[11], (DEPTH, CONV_WIDTH), f32)
    fox_f_bias = 3.0 + 0.5 * nrm(ks[12], (DEPTH, FOX_HEADS), f32)
    ln_mix_g = 1.0 + 0.05 * nrm(ks[13], (DEPTH, D_MODEL), f32)
    ln_mix_b = 0.02 * nrm(ks[14], (DEPTH, D_MODEL), f32)
    ln_ffn_g = 1.0 + 0.05 * nrm(ks[15], (DEPTH, D_MODEL), f32)
    ln_ffn_b = 0.02 * nrm(ks[16], (DEPTH, D_MODEL), f32)
    ffn_w1 = nrm(ks[17], (N_DENSE, D_MODEL, FFN_DENSE), f32) * D_MODEL ** -0.5
    ffn_w3 = nrm(ks[18], (N_DENSE, D_MODEL, FFN_DENSE), f32) * D_MODEL ** -0.5
    ffn_w2 = nrm(ks[19], (N_DENSE, FFN_DENSE, D_MODEL), f32) * (FFN_DENSE ** -0.5 * DEEPNORM_BETA)
    moe_router = nrm(ks[20], (N_MOE, D_MODEL, N_EXPERTS), f32) * D_MODEL ** -0.5
    moe_w1 = nrm(ks[21], (N_MOE, N_EXPERTS, D_MODEL, FFN_EXPERT), f32) * D_MODEL ** -0.5
    moe_w3 = nrm(ks[22], (N_MOE, N_EXPERTS, D_MODEL, FFN_EXPERT), f32) * D_MODEL ** -0.5
    moe_w2 = nrm(ks[23], (N_MOE, N_EXPERTS, FFN_EXPERT, D_MODEL), f32) * (FFN_EXPERT ** -0.5 * DEEPNORM_BETA)
    return {'x': x, 'w_in': w_in, 'mix_scale': mix_scale, 'w_out': w_out,
            'gdn_conv_w': gdn_conv_w, 'gdn_a_log': gdn_a_log, 'gdn_dt_bias': gdn_dt_bias, 'gdn_norm_w': gdn_norm_w,
            'cnv_dw_w': cnv_dw_w, 'cnv_dw_b': cnv_dw_b, 'cnv_ln_g': cnv_ln_g, 'cnv_ln_b': cnv_ln_b,
            'fox_f_bias': fox_f_bias,
            'ln_mix_g': ln_mix_g, 'ln_mix_b': ln_mix_b, 'ln_ffn_g': ln_ffn_g, 'ln_ffn_b': ln_ffn_b,
            'ffn_w1': ffn_w1, 'ffn_w3': ffn_w3, 'ffn_w2': ffn_w2,
            'moe_router': moe_router, 'moe_w1': moe_w1, 'moe_w3': moe_w3, 'moe_w2': moe_w2}

def first_block(x, w_in, mix_scale, w_out, gdn_conv_w, gdn_a_log, gdn_dt_bias, gdn_norm_w,
              cnv_dw_w, cnv_dw_b, cnv_ln_g, cnv_ln_b, fox_f_bias,
              ln_mix_g, ln_mix_b, ln_ffn_g, ln_ffn_b,
              ffn_w1, ffn_w3, ffn_w2, moe_router, moe_w1, moe_w3, moe_w2):
    for l in range(DEPTH):
        mix = hybrid_mixer(x, w_in[l], mix_scale[l], w_out[l], gdn_conv_w[l], gdn_a_log[l], gdn_dt_bias[l],
                           gdn_norm_w[l], cnv_dw_w[l], cnv_dw_b[l], cnv_ln_g[l], cnv_ln_b[l], fox_f_bias[l])
        x = layer_norm(DEEPNORM_ALPHA * x + mix, ln_mix_g[l], ln_mix_b[l])
        if l % 2 == 0:
            ff = swiglu(x, ffn_w1[l // 2], ffn_w3[l // 2], ffn_w2[l // 2])
        else:
            ff = moe_swiglu(x, moe_router[l // 2], moe_w1[l // 2], moe_w3[l // 2], moe_w2[l // 2])
        x = layer_norm(DEEPNORM_ALPHA * x + ff, ln_ffn_g[l], ln_ffn_b[l])
    return x


DEPTH_2 = 1

CHUNK = 64
Q_BLOCK = 128
A_HEADS = 8
A_HEAD_DIM = 64
A_WIDTH = A_HEADS * A_HEAD_DIM
IDX_HEADS = 4
IDX_DIM = 64
TOPK_MAX = 256
REL_BUCKETS = 32
REL_MAX_DIST = 128
SSM_GROUPS = 16
SSM_GROUP_CH = 16
SSM_WIDTH = SSM_GROUPS * SSM_GROUP_CH
SSM_STATE = 64
DT_MIN = 0.001
DT_MAX = 0.1
MEM_TOKENS = 256
MEM_HEADS = 4
MEM_HEAD_DIM = 64
MEM_WIDTH = MEM_HEADS * MEM_HEAD_DIM
N_BRANCHES = 3
FFN_DIM = 2816
IN_SPLITS = (A_WIDTH, A_HEAD_DIM, A_HEAD_DIM, IDX_HEADS * IDX_DIM, IDX_DIM, IDX_HEADS,
             SSM_WIDTH, MEM_WIDTH, N_BRANCHES * D_MODEL)
W_IN_COLS = (A_WIDTH + 2 * A_HEAD_DIM + IDX_HEADS * IDX_DIM + IDX_DIM + IDX_HEADS
             + SSM_WIDTH + MEM_WIDTH + N_BRANCHES * D_MODEL)


def rms_norm(x, g):
    xf = x.astype(jnp.float32)
    y = xf * lax.rsqrt(jnp.mean(xf * xf, axis=-1, keepdims=True) + NORM_EPS)
    return (y * g.astype(jnp.float32)).astype(x.dtype)

def swiglu_ffn(h, w_in, w_out):
    gate, up = jnp.split(h @ w_in, 2, axis=-1)
    return (jax.nn.silu(gate) * up) @ w_out

def t5_bucket(rel):
    half = REL_BUCKETS // 2
    max_exact = half // 2
    n = jnp.abs(rel)
    nf = jnp.maximum(n, 1).astype(jnp.float32)
    large = max_exact + (jnp.log(nf / max_exact) / math.log(REL_MAX_DIST / max_exact)
                         * (half - max_exact)).astype(jnp.int32)
    large = jnp.minimum(large, half - 1)
    return jnp.where(rel > 0, half, 0) + jnp.where(n < max_exact, n, large)

def indexed_sparse_attention(q, k, v, q_idx, k_idx, w_idx, rel_bias):
    b_, s_ = q.shape[0], q.shape[1]
    topk = min(TOPK_MAX, s_ // 4)
    nblk = s_ // Q_BLOCK
    key_pos = jnp.arange(s_, dtype=jnp.int32)
    scale = A_HEAD_DIM ** -0.5
    idx_scale = IDX_DIM ** -0.5
    head_w_scale = IDX_HEADS ** -0.5

    def to_blocks(a):
        return a.reshape((b_, nblk, Q_BLOCK) + a.shape[2:]).swapaxes(0, 1)

    def block(args):
        qb, qib, wb, start = args
        t = start + jnp.arange(Q_BLOCK, dtype=jnp.int32)
        limit = (t // CHUNK + 1) * CHUNK
        rel = jax.nn.relu(jnp.einsum('bqhd,bsd->bqhs', qib, k_idx).astype(jnp.float32) * idx_scale)
        score = jnp.einsum('bqhs,bqh->bqs', rel, wb.astype(jnp.float32) * head_w_scale)
        score = jnp.where(key_pos[None, None, :] < limit[None, :, None], score, -jnp.inf)
        _, sel = lax.top_k(score, topk)
        valid = sel < limit[None, :, None]
        flat = sel.reshape(b_, Q_BLOCK * topk, 1)
        k_sel = jnp.take_along_axis(k, flat, axis=1).reshape(b_, Q_BLOCK, topk, A_HEAD_DIM)
        v_sel = jnp.take_along_axis(v, flat, axis=1).reshape(b_, Q_BLOCK, topk, A_HEAD_DIM)
        bias = rel_bias[t5_bucket(sel - t[None, :, None])]
        logits = (jnp.einsum('bqhd,bqkd->bqhk', qb, k_sel).astype(jnp.float32) * scale
                  + jnp.transpose(bias, (0, 1, 3, 2)).astype(jnp.float32))
        logits = jnp.where(valid[:, :, None, :], logits, -jnp.inf)
        p = jax.nn.softmax(logits, axis=-1).astype(v_sel.dtype)
        return jnp.einsum('bqhk,bqkd->bqhd', p, v_sel)

    starts = jnp.arange(nblk, dtype=jnp.int32) * Q_BLOCK
    out = lax.map(block, (to_blocks(q), to_blocks(q_idx), to_blocks(w_idx), starts))
    return out.swapaxes(0, 1).reshape(b_, s_, A_WIDTH)

def _complex_affine_combine(e1, e2):
    a1r, a1i, b1r, b1i = e1
    a2r, a2i, b2r, b2i = e2
    return (a2r * a1r - a2i * a1i,
            a2r * a1i + a2i * a1r,
            a2r * b1r - a2i * b1i + b2r,
            a2r * b1i + a2i * b1r + b2i)

def s5_layer(u, lam_re, lam_im, log_dt, b_re, b_im, c_re, c_im, d):
    b_, s_ = u.shape[0], u.shape[1]
    f32 = jnp.float32
    uf = u.astype(f32).reshape(b_, s_, SSM_GROUPS, SSM_GROUP_CH)
    lr, li = lam_re.astype(f32), lam_im.astype(f32)
    dt = jnp.exp(log_dt.astype(f32))[:, None]
    mag = jnp.exp(lr * dt)
    ar, ai = mag * jnp.cos(li * dt), mag * jnp.sin(li * dt)
    den = lr * lr + li * li
    fr = ((ar - 1.0) * lr + ai * li) / den
    fi = (ai * lr - (ar - 1.0) * li) / den
    br, bi = b_re.astype(f32), b_im.astype(f32)
    bbr = fr[..., None] * br - fi[..., None] * bi
    bbi = fr[..., None] * bi + fi[..., None] * br
    bur = jnp.einsum('bsgc,gpc->bsgp', uf, bbr)
    bui = jnp.einsum('bsgc,gpc->bsgp', uf, bbi)
    elems = (jnp.broadcast_to(ar, bur.shape), jnp.broadcast_to(ai, bur.shape), bur, bui)
    _, _, xr, xi = lax.associative_scan(_complex_affine_combine, elems, axis=1)
    y = (jnp.einsum('bsgp,gcp->bsgc', xr, c_re.astype(f32))
         - jnp.einsum('bsgp,gcp->bsgc', xi, c_im.astype(f32))
         + d.astype(f32).reshape(SSM_GROUPS, SSM_GROUP_CH) * uf)
    return y.reshape(b_, s_, SSM_WIDTH).astype(u.dtype)

def memory_attention(q, k, v):
    logits = jnp.einsum('bshd,bmhd->bhsm', q, k).astype(jnp.float32) * (MEM_HEAD_DIM ** -0.5)
    p = jax.nn.softmax(logits, axis=-1).astype(v.dtype)
    out = jnp.einsum('bhsm,bmhd->bshd', p, v)
    return out.reshape(q.shape[0], q.shape[1], MEM_WIDTH)

def second_inputs(seed: int = 0) -> dict:
    key = jax.random.key(seed)
    ks = jax.random.split(key, 32)
    f32 = jnp.float32
    L = DEPTH_2

    def nrm(k, shape, scale):
        return jax.random.normal(k, shape, f32) * scale

    def gain(k, shape):
        return 1.0 + 0.02 * jax.random.normal(k, shape, f32)

    n = jnp.arange(SSM_STATE, dtype=f32)
    return {
        'x': nrm(ks[0], (BATCH, SEQ, D_MODEL), 1.0),
        'mem': nrm(ks[1], (BATCH, MEM_TOKENS, D_MODEL), 1.0),
        'ffn1_norm': gain(ks[2], (L, D_MODEL)),
        'ffn1_w_in': nrm(ks[3], (L, D_MODEL, 2 * FFN_DIM), D_MODEL ** -0.5),
        'ffn1_w_out': nrm(ks[4], (L, FFN_DIM, D_MODEL), FFN_DIM ** -0.5),
        'mix_norm': gain(ks[5], (L, D_MODEL)),
        'w_in': nrm(ks[6], (L, D_MODEL, W_IN_COLS), D_MODEL ** -0.5),
        'a_q_gain': gain(ks[7], (L, A_HEAD_DIM)),
        'a_k_gain': gain(ks[8], (L, A_HEAD_DIM)),
        'rel_bias': nrm(ks[9], (REL_BUCKETS, A_HEADS), 0.5),
        'w_o_a': nrm(ks[10], (L, A_WIDTH, D_MODEL), A_WIDTH ** -0.5),
        'ssm_lambda_re': -0.5 + nrm(ks[11], (L, SSM_GROUPS, SSM_STATE), 0.01),
        'ssm_lambda_im': math.pi * n + nrm(ks[12], (L, SSM_GROUPS, SSM_STATE), 0.01),
        'ssm_log_dt': jax.random.uniform(ks[13], (L, SSM_GROUPS), f32,
                                         minval=math.log(DT_MIN), maxval=math.log(DT_MAX)),
        'ssm_b_re': nrm(ks[14], (L, SSM_GROUPS, SSM_STATE, SSM_GROUP_CH), (2 * SSM_GROUP_CH) ** -0.5),
        'ssm_b_im': nrm(ks[15], (L, SSM_GROUPS, SSM_STATE, SSM_GROUP_CH), (2 * SSM_GROUP_CH) ** -0.5),
        'ssm_c_re': nrm(ks[16], (L, SSM_GROUPS, SSM_GROUP_CH, SSM_STATE), SSM_STATE ** -0.5),
        'ssm_c_im': nrm(ks[17], (L, SSM_GROUPS, SSM_GROUP_CH, SSM_STATE), SSM_STATE ** -0.5),
        'ssm_d': nrm(ks[18], (L, SSM_WIDTH), 1.0),
        'w_glu': nrm(ks[19], (L, SSM_WIDTH, 2 * D_MODEL), SSM_WIDTH ** -0.5),
        'mem_norm': gain(ks[20], (L, D_MODEL)),
        'w_mem_kv': nrm(ks[21], (L, D_MODEL, 2 * MEM_WIDTH), D_MODEL ** -0.5),
        'm_q_gain': gain(ks[22], (L, MEM_HEAD_DIM)),
        'm_k_gain': gain(ks[23], (L, MEM_HEAD_DIM)),
        'w_o_m': nrm(ks[24], (L, MEM_WIDTH, D_MODEL), MEM_WIDTH ** -0.5),
        'w_out': nrm(ks[25], (L, D_MODEL, D_MODEL), D_MODEL ** -0.5),
        'ffn2_norm': gain(ks[26], (L, D_MODEL)),
        'ffn2_w_in': nrm(ks[27], (L, D_MODEL, 2 * FFN_DIM), D_MODEL ** -0.5),
        'ffn2_w_out': nrm(ks[28], (L, FFN_DIM, D_MODEL), FFN_DIM ** -0.5),
        'final_norm': gain(ks[29], (L, D_MODEL)),
    }

def second_block(x, mem, ffn1_norm, ffn1_w_in, ffn1_w_out, mix_norm, w_in, a_q_gain, a_k_gain,
              rel_bias, w_o_a, ssm_lambda_re, ssm_lambda_im, ssm_log_dt, ssm_b_re, ssm_b_im,
              ssm_c_re, ssm_c_im, ssm_d, w_glu, mem_norm, w_mem_kv, m_q_gain, m_k_gain, w_o_m,
              w_out, ffn2_norm, ffn2_w_in, ffn2_w_out, final_norm):
    b_, s_ = x.shape[0], x.shape[1]
    offsets = [sum(IN_SPLITS[:i + 1]) for i in range(len(IN_SPLITS) - 1)]
    for l in range(DEPTH_2):
        x = x + 0.5 * swiglu_ffn(rms_norm(x, ffn1_norm[l]), ffn1_w_in[l], ffn1_w_out[l])
        h = rms_norm(x, mix_norm[l])
        q_a, k_a, v_a, q_i, k_i, w_i, u_s, q_m, gates = jnp.split(h @ w_in[l], offsets, axis=-1)
        q_a = rms_norm(q_a.reshape(b_, s_, A_HEADS, A_HEAD_DIM), a_q_gain[l])
        k_a = rms_norm(k_a, a_k_gain[l])
        o_a = indexed_sparse_attention(q_a, k_a, v_a, q_i.reshape(b_, s_, IDX_HEADS, IDX_DIM),
                                       k_i, w_i, rel_bias) @ w_o_a[l]
        y_s = jax.nn.gelu(s5_layer(u_s, ssm_lambda_re[l], ssm_lambda_im[l], ssm_log_dt[l],
                                   ssm_b_re[l], ssm_b_im[l], ssm_c_re[l], ssm_c_im[l], ssm_d[l]))
        glu_a, glu_b = jnp.split(y_s @ w_glu[l], 2, axis=-1)
        o_b = glu_a * jax.nn.sigmoid(glu_b)
        mem_kv = rms_norm(mem, mem_norm[l]) @ w_mem_kv[l]
        m_k, m_v = jnp.split(mem_kv, 2, axis=-1)
        m_k = rms_norm(m_k.reshape(b_, MEM_TOKENS, MEM_HEADS, MEM_HEAD_DIM), m_k_gain[l])
        m_v = m_v.reshape(b_, MEM_TOKENS, MEM_HEADS, MEM_HEAD_DIM)
        q_m = rms_norm(q_m.reshape(b_, s_, MEM_HEADS, MEM_HEAD_DIM), m_q_gain[l])
        o_m = memory_attention(q_m, m_k, m_v) @ w_o_m[l]
        g = jax.nn.sigmoid(gates.reshape(b_, s_, N_BRANCHES, D_MODEL))
        merged = g[:, :, 0] * o_a + g[:, :, 1] * o_b + g[:, :, 2] * o_m
        x = x + merged @ w_out[l]
        x = x + 0.5 * swiglu_ffn(rms_norm(x, ffn2_norm[l]), ffn2_w_in[l], ffn2_w_out[l])
        x = rms_norm(x, final_norm[l])
    return x


def setup_inputs(seed=0):
    out = dict(first_inputs(seed))
    for name, value in second_inputs(seed + 1).items():
        if name != "x":
            out[name + "_2"] = value
    return out


def reference(
    x, w_in, mix_scale, w_out, gdn_conv_w, gdn_a_log, gdn_dt_bias, gdn_norm_w, cnv_dw_w,
    cnv_dw_b, cnv_ln_g, cnv_ln_b, fox_f_bias, ln_mix_g, ln_mix_b, ln_ffn_g, ln_ffn_b, ffn_w1,
    ffn_w3, ffn_w2, moe_router, moe_w1, moe_w3, moe_w2, mem_2, ffn1_norm_2, ffn1_w_in_2,
    ffn1_w_out_2, mix_norm_2, w_in_2, a_q_gain_2, a_k_gain_2, rel_bias_2, w_o_a_2,
    ssm_lambda_re_2, ssm_lambda_im_2, ssm_log_dt_2, ssm_b_re_2, ssm_b_im_2, ssm_c_re_2,
    ssm_c_im_2, ssm_d_2, w_glu_2, mem_norm_2, w_mem_kv_2, m_q_gain_2, m_k_gain_2, w_o_m_2,
    w_out_2, ffn2_norm_2, ffn2_w_in_2, ffn2_w_out_2, final_norm_2,
):
    x = first_block(
        x, w_in, mix_scale, w_out, gdn_conv_w, gdn_a_log, gdn_dt_bias, gdn_norm_w, cnv_dw_w,
        cnv_dw_b, cnv_ln_g, cnv_ln_b, fox_f_bias, ln_mix_g, ln_mix_b, ln_ffn_g, ln_ffn_b,
        ffn_w1, ffn_w3, ffn_w2, moe_router, moe_w1, moe_w3, moe_w2,
    )
    return second_block(
        x, mem_2, ffn1_norm_2, ffn1_w_in_2, ffn1_w_out_2, mix_norm_2, w_in_2, a_q_gain_2,
        a_k_gain_2, rel_bias_2, w_o_a_2, ssm_lambda_re_2, ssm_lambda_im_2, ssm_log_dt_2,
        ssm_b_re_2, ssm_b_im_2, ssm_c_re_2, ssm_c_im_2, ssm_d_2, w_glu_2, mem_norm_2,
        w_mem_kv_2, m_q_gain_2, m_k_gain_2, w_o_m_2, w_out_2, ffn2_norm_2, ffn2_w_in_2,
        ffn2_w_out_2, final_norm_2,
    )


_drawn_inputs = setup_inputs


def setup_inputs(seed=0):
    import zlib

    import numpy as np

    out = dict(_drawn_inputs(seed))
    spreads = {}
    factors = {'gdn_norm_w': 3.026,
     'cnv_dw_b': 3.656,
     'cnv_ln_g': 3.473,
     'cnv_ln_b': 7.7,
     'ffn1_norm_2': 4.639,
     'mix_norm_2': 3.427,
     'a_q_gain_2': 8.0,
     'a_k_gain_2': 8.0,
     'ssm_lambda_re_2': 64.0,
     'ssm_lambda_im_2': 27.8,
     'ssm_log_dt_2': 30.232,
     'ssm_b_re_2': 39.816,
     'ssm_b_im_2': 40.448,
     'ssm_c_re_2': 40.36,
     'ssm_c_im_2': 39.4,
     'mem_norm_2': 8.0,
     'm_q_gain_2': 8.0,
     'm_k_gain_2': 8.0,
     'ffn2_norm_2': 7.118,
     'final_norm_2': 7.762,
     'rel_bias_2': 4.414}
    for name, (base, spread) in spreads.items():
        noise = np.random.default_rng([zlib.crc32(name.encode()), seed]).standard_normal(out[name].shape)
        drawn = base * np.exp(spread * noise) if base else spread * noise
        out[name] = jnp.asarray(drawn.astype(out[name].dtype))
    for name, factor in factors.items():
        out[name] = (out[name] * factor).astype(out[name].dtype)
    return out
```

```python
from contextlib import ExitStack

import numpy as np

import concourse.bass as bass
from concourse import mybir

F32 = mybir.dt.float32
I32 = mybir.dt.int32
ALU = mybir.AluOpType
ACT = mybir.ActivationFunctionType
AX_X = mybir.AxisListType.X

P = 128
D = 1024
T = 256
TT = T // P
DT = D // P
DEPTH = 2
ALPHA = float((2 * DEPTH) ** 0.25)
LN_EPS, NORM_EPS = 1e-5, 1e-6
HD = 64
GW, CW, XW = 384, 256, 384
H = GW // HD
HP = H // 2
TAPS = 31
CHUNK = 64
FFN = 2816
E, FE = 8, 3584
CAP = P
FC = 256
RING = 6

C_QKV, C_DECAY, C_GATE = 0, 1152, 1164
C_GLUA, C_GLUB, C_FQ, C_FV, IN_COLS = 1548, 1804, 2060, 2828, 3218
PROJ = [(C_DECAY, 198, "tokA"), (C_FV, 195, "tokC"), (C_FV + 195, 195, "tokC")]
PROJ += [(C_QKV + 256 * i, 256 if i < 4 else 128, "qkv") for i in range(5)]
PROJ += [(C_GLUB, 256, "glub"), (C_GLUA, 256, "glua")]
PROJ += [(C_FQ + 256 * i, 256, "fqk") for i in range(3)]
PROJ += [(C_DECAY + 198, 198, "tokA")]
GLUA_LOAD = [k for _, _, k in PROJ].index("glua")
OUT_LOADS = 4
MIX_LOADS = len(PROJ) + OUT_LOADS
FFN_BODIES = FFN // FC // 2
FFN_LOADS = 3 * (FFN // FC)
MOE_BODIES = FE // FC // 2
MOE_LOADS = 6 * MOE_BODIES
LEVELS = 6
NEG = -1.0e30

HEADS1 = DEPTH * H
AH, IH, MH = 8, 4, 4
TOPK = 64
NS = 8
C_QA, C_KV, C_QI, C_KI, C_US, C_QM, C_G = 0, 512, 640, 896, 964, 1220, 1476
PROJ2 = [(C_QI, 256, "qi"), (C_KI, 68, "kiw"), (C_QA, 256, "qa"), (C_QA + 256, 256, "qa"), (C_KV, 128, "kv"),
         (C_US, 256, "us"), (C_QM, 256, "qm")] + [(C_G + 256 * i, 256, "gate") for i in range(12)]
N_MEM = 0
N_FFN1 = 2
N_PROJ2 = N_FFN1 + FFN_LOADS
N_OA = N_PROJ2 + len(PROJ2)
N_OM = N_OA + 2
N_GLU = N_OM + 1
N_OUT2 = N_GLU + 2
N_FFN2 = N_OUT2 + 4
N_END = N_FFN2 + FFN_LOADS
R2_LDT, R2_FFN1, R2_MIX, R2_MEM, R2_FFN2, R2_LRE, R2_LIM, R2_D, ROWS2 = 0, 8, 16, 24, 32, 40, 48, 56, 58
TWO_PI = (6.28125, 0.0019350051879882812, 3.0199157663446e-07)
ROUND = 12582912.0
PI_F = 3.1415925
ARENA = 27670

R_GCONV, R_DW, R_DWB, R_MIX, ROWS1 = 0, 36, 98, 100, 108


def bucket_of(rel):
    half, exact = 16, 8
    n = abs(rel)
    large = exact + int(np.float32(np.log(np.float32(max(n, 1)) / np.float32(exact))) / np.float32(np.log(128 / exact)) * np.float32(half - exact))
    return (half if rel > 0 else 0) + (n if n < exact else min(large, half - 1))


def shape_constants():
    i, j = np.arange(P)[:, None], np.arange(P)[None, :]
    same = (i // CHUNK) == (j // CHUNK)
    t = {}
    t["ident"] = i == j
    t["le"] = i <= j
    t["lt"] = i < j
    t["ones"] = np.ones((P, P))
    t["half"] = same
    t["le64"] = (i <= j) & same
    t["gt64"] = (i > j) & same
    t["inhalf"] = np.concatenate([(i // CHUNK == p) & (j >= 0) for p in range(2)], 1)
    t["gt256"] = np.concatenate([np.arange(P)[:, None] + P * a > np.arange(T)[None, :] for a in range(TT)], 1)
    b = [1 << n for n in range(LEVELS)]
    t["lvl"] = np.concatenate([(i // (2 * n) == j // (2 * n)) & (i % (2 * n) >= n) & (j % (2 * n) < n) for n in b], 1)
    diag = np.where(j > i, NEG, 0.0)
    t["foxmask"] = np.concatenate([diag, diag * 0, diag], 1)
    key = np.arange(T)[None, :]
    t["cap"] = np.concatenate([np.where(key < ((np.arange(P)[:, None] + P * a) // CHUNK + 1) * CHUNK, 3e38, -2e38) for a in range(TT)], 1)
    t["iota"] = np.broadcast_to(j, (P, P))
    t["lower8"] = np.broadcast_to((np.arange(8)[:, None] > np.arange(8)[None, :]).reshape(1, 64), (P, 64))
    t["parity"] = np.concatenate([(i // 16) % 2 == p for p in range(2)], 1)
    hot = np.zeros((P, 512))
    for c in range(511):
        hot[bucket_of(c - 255), c] = 1
    t["hot"] = hot
    return {k: np.ascontiguousarray(v, dtype=np.float32) for k, v in t.items()}


def constant_offsets():
    at, out = 0, {}
    for k, v in shape_constants().items():
        out[k] = (at, v.shape[1])
        at += v.shape[1]
    return out, at


class Steps:

    def __init__(self, eng, sem):
        self.eng, self.sem, self.n = eng, sem, 0

    def do(self, ins):
        self.n += 1
        ins.then_inc(self.sem, 1)

    def settle(self):
        self.eng.wait_ge(self.sem, self.n)


class Ring:

    def __init__(self, data, loaded, used, shift=0):
        self.data, self.loaded, self.used, self.shift = data, loaded, used, shift
        self.before = None

    def slot(self, n):
        return self.data[:, (n + self.shift) % RING, :]

    def load(self, sp, n, dst, src, more=0):
        if n + 1 > RING or not isinstance(more, int):
            sp.wait_ge(self.used, n + 1 - RING + more)
        elif self.before:
            self.before(n)
        sp.dma_start(dst, src).then_inc(self.loaded[n % RING], 16)

    def arrived(self, pe, n, rounds=0):
        pe.wait_ge(self.loaded[n % RING], 16 * (n // RING + 1) + 16 * rounds)


def cols(ap, c, w):
    return ap[:, c:c + w].rearrange("(k p) c -> p k c", p=P)


def two_block_kernel(nc, a, out):
    CO, CONST_W = constant_offsets()
    with ExitStack() as ctx:
        def sb(name, shape, dt=F32):
            return ctx.enter_context(nc.sbuf_tensor(name, shape, dt))

        S = {}

        def sem(name):
            if name not in S:
                S[name] = ctx.enter_context(nc.semaphore(name))
            return S[name]

        bank = [ctx.enter_context(nc.psum_tensor(f"bank{i}", [P, 512], F32)) for i in range(8)]

        def bk(i, *dims):
            n = int(np.prod(dims))
            v = bank[i][:, 0:n]
            if len(dims) == 2:
                v = v.rearrange("p (a b) -> p a b", a=dims[0])
            if len(dims) == 3:
                v = v.rearrange("p (a b c) -> p a b c", a=dims[0], b=dims[1])
            return v

        consts = sb("consts_sb", [P, CONST_W])

        def const(name, k=0, w=None):
            o, width = CO[name]
            w = w or width
            return consts[:, o + k * w:o + (k + 1) * w]

        ident, ones, half = const("ident"), const("ones"), const("half")

        ring_data = sb("ring_data", [P, RING, 8 * FC])
        ring = Ring(ring_data, [sem(f"loaded{i}") for i in range(RING)], sem("weights_used"))
        x = sb("x", [P, TT, D])
        actT = sb("actT", [P, DT, T])
        lnp = sb("lnp", [P, 2, D])
        prow = sb("prow", [P, DEPTH, P])
        pcol = sb("pcol", [P, DEPTH, P])
        hpar = sb("hpar", [P, DEPTH, 24])
        nrmw = sb("nrmw", [P, DEPTH, HD])
        cln = sb("cln", [P, DEPTH, 2, CW])
        router_sb = sb("router_sb", [P, DT, E])
        headg = sb("headg", [P, 4, HD])
        toep = nc.dram_tensor("toep", (AH, P, 512), F32, kind="Internal").ap()
        small = sb("small", [P, 1024])
        npass_i = sb("npass_i", [P, 1], I32)
        arena = sb("arena", [P, ARENA])

        class Area:

            def __init__(self, at=0):
                self.at = at

            def __call__(self, *dims):
                n = int(np.prod(dims))
                v = arena[:, self.at:self.at + n]
                self.at += n
                if self.at > ARENA:
                    raise ValueError(self.at)
                names = "abcd"[:len(dims)]
                if len(dims) > 1:
                    v = v.rearrange("p (" + " ".join(names) + ") -> p " + " ".join(names),
                                    **{k: d for k, d in zip(names[:-1], dims[:-1])})
                return v

        class Small(Area):
            def __call__(self, *dims):
                n = int(np.prod(dims))
                v = small[:, self.at:self.at + n]
                self.at += n
                if self.at > 1024:
                    raise ValueError(self.at)
                names = "abcd"[:len(dims)]
                if len(dims) > 1:
                    v = v.rearrange("p (" + " ".join(names) + ") -> p " + " ".join(names),
                                    **{k: d for k, d in zip(names[:-1], dims[:-1])})
                return v

        ar = Area()
        mixed = ar(TT, D)
        tokA, tokC = ar(TT, 396), ar(TT, 390)
        at_qkv_raw = ar.at
        qkv_raw = ar(9, 3 + T)
        qkv = ar(9, T)
        fqk = ar(6, T)
        uraw = ar(2, TAPS - 1 + T)
        sigb = ar(2, T)
        uconv = sigb
        at_gm = ar.at
        GM, GU = ar(TT, H, P), ar(TT, H, P)
        X, Y = GM, GU
        Dm, DTm = ar(TT, H, P), ar(TT, H, P)
        Lm, AT = Dm, DTm
        Cl = [ar(TT, H, P) for _ in range(2)]
        Zs = ar(TT, H, P)
        kend, vb = ar(TT, GW), ar(TT, GW)
        GF = ar(TT, H, T)
        over = Area(at_qkv_raw)
        kbe, u_sb, wT = over(TT, GW), over(TT, GW), over(TT, HP, P)
        over = Area(at_gm)
        fs, fp, fpT = ([over(3 * P) for _ in range(2)] for _ in range(3))
        S_st = ar(HP, HD)
        oq = ar(GW)
        sq = Zs
        rn = Cl[0].rearrange("p a b c -> p (a b c)").rearrange("p (a b) -> p a b", a=6)
        ar = Area()
        yacc = ar(TT, D)
        sil, hT = ar(4, T), ar(4, T)
        xgT, Ysb = ar(DT, CAP), ar(D)
        Pm, PG, PGT = ar(TT, CAP), ar(TT, CAP), ar(TT, P)
        sm = Small()
        s1, az, lg1, gs = sm(TT, 12), sm(TT, 12), sm(TT, 12), sm(TT, 12)
        beta, eg, cb, eglp = sm(TT, H), sm(TT, 24), sm(TT, H), sm(TT, 2, HP)
        ss12, rr12 = sm(TT * H), sm(TT * H)
        bst, mv, std, rstd = sm(TT, 2, 6), sm(TT, 2), sm(TT), sm(TT)
        fneg, fsum, frec = sm(H, TT), sm(H, TT), sm(H, TT)
        lgt, gtm, eqm = sm(TT, E), sm(TT, 64), sm(TT, 64)
        rank, sel, m1, ex, esum, gate = sm(TT, E), sm(TT, E), sm(TT), sm(TT, E), sm(TT), sm(TT, E)
        posx, cnt, poscol, gcol = sm(TT, 2, E), sm(2), sm(TT), sm(TT)

        ring2 = Ring(ring_data, [sem(f"loaded2_{i}") for i in range(RING)], sem("weights2_used"), (2 * MIX_LOADS + FFN_LOADS) % RING)
        prow2, pcol2 = prow[:, 0, :], pcol.rearrange("p a b -> p (a b)")
        hbuf = lnp
        ar = Area()
        gates = ar(TT, 3 * D)
        score, work = ar(3 * P), ar(3 * P)
        Ct, St = ar(NS, T), ar(NS, T)
        bu = ar(NS, 2, T)
        tstage = bu.rearrange("p a b c -> p (a b c)").rearrange("p (h c) -> p h c", h=AH)
        gl = bu.rearrange("p a b c -> p (a b c)")[:, 0:TT * D].rearrange("p (j d) -> p j d", j=TT)
        gl2 = bu.rearrange("p a b c -> p (a b c)")[:, TT * D:2 * TT * D].rearrange("p (j d) -> p j d", j=TT)
        bias = ar(AH, 3 * P)
        at_att = ar.at
        al = [ar(3 * P) for _ in range(2)]
        ap_ = [ar(512) for _ in range(2)]
        apT = [ar(512) for _ in range(2)]
        memx = arena[:, at_att:at_att + TT * D].rearrange("p (j d) -> p j d", j=TT)
        rel = arena[:, at_att:at_att + IH * 3 * P].rearrange("p (h c) -> p h c", h=IH)
        at_q = ar.at
        qa, qaT = ar(TT, 512), ar(4, T)
        qm, qmT = ar(TT, 256), ar(2, T)
        qiT, kiT, kaT = ar(2, T), ar(T), ar(T)
        kva, kd = ar(TT, P), ar(TT, P)
        uT = ar(2, T)
        mkT = ar(2, T)
        bT, cT = ar(2, 2, P), ar(2, 2, P)
        mkv = cln.rearrange("p a b c -> p (a b c)").rearrange("p (j c) -> p j c", j=TT)
        over = Area(at_q)
        relb, relb_bc = over(AH), over(AH, P)
        braw, blk = over(2, NS, 16), over(2, NS, 32)
        craw, cd = over(2, 2, HD), over(2, 2, 2, HD)
        btmp = over(2, NS, 16)
        pw = [over(NS * P) for _ in range(2)]
        memT = arena[:, 4096:6144].rearrange("p (k t) -> p k t", k=DT)
        oa, om = qa, qm
        sm = Small(sm.at)
        ss2, r2 = sm(TT), sm(TT)
        ssq, rq = sm(TT * 13), sm(TT * 13)
        q26 = [sm(NS) for _ in range(16)]
        wi, log_dt = sm(TT, IH), sm(2)
        max8 = sm(2, 8)
        aneg, asum, arec = sm(AH + MH, TT), sm(AH + MH, TT), sm(AH + MH, TT)

        def bc(ap, axis, n):
            v = ap.unsqueeze(axis)
            shape = list(v.shape)
            shape[axis] = n
            return v.broadcast_to(shape)

        def slots(ap):
            return ap.rearrange("p (t q) -> p q t", q=2)

        def slot(h):
            return HP * (h % 2) + h // 2

        def four(ap):
            return ap.rearrange("p (q t) c -> p q t c", q=2)

        def bc4(ap, n):
            v = slots(ap).unsqueeze(3)
            return v.broadcast_to([P, 2, HP, n])

        def taps(l, k, tile):
            return pcol[:, l, R_DW + 2 * k + tile:R_DW + 2 * k + tile + 1]

        def pick(h):
            return slice(HD * (h % 2), HD * (h % 2) + HD)

        proj_on_act = [m for m in range(len(PROJ)) if m != GLUA_LOAD]

        def act_proj(l, m):
            return l * len(proj_on_act) + proj_on_act.index(m) + 1

        block = ctx.enter_context(nc.Block())

        @block.sync
        def _(sp):
            sp.dma_start(x[:, :, :], a["x"][0].rearrange("(j p) d -> p j d", p=P)).then_inc(sem("x_loaded"), 16)

            def mixer(l):
                n0 = (MIX_LOADS + FFN_LOADS) * l
                for m, (c, w, _) in enumerate(PROJ):
                    ring.load(sp, n0 + m, ring.slot(n0 + m)[:, 0:8 * w].rearrange("p (k c) -> p k c", k=DT), cols(a["w_in"][l], c, w))
                for m in range(OUT_LOADS):
                    n = n0 + len(PROJ) + m
                    ring.load(sp, n, ring.slot(n).rearrange("p (k c) -> p k c", k=DT), cols(a["w_out"][l], FC * m, FC))

            def chunk_slots(ring, n, w1, w3, w2, c, order, more, rounds_more):
                for j in order[0:2]:
                    ring.load(sp, n + j, ring.slot(n + j).rearrange("p (k c) -> p k c", k=DT),
                              (w1, w3)[order.index(j)][:, bass.ds(c, FC)].rearrange("(k p) c -> p k c", p=P), rounds_more)

            def dense(ring, n0, w1, w3, w2):
                def up(n, c, more):
                    for j, w in enumerate((w1, w3)):
                        ring.load(sp, n + j, ring.slot(n + j).rearrange("p (k c) -> p k c", k=DT),
                                  w[:, bass.ds(c, FC)].rearrange("(k p) c -> p k c", p=P), more)

                def down(n, c, more):
                    ring.load(sp, n, ring.slot(n).rearrange("p (f d) -> p f d", f=2),
                              w2[bass.ds(c, FC), :].rearrange("(f p) d -> p f d", p=P), more)

                def body(i):
                    c, more = i * (2 * FC), i * 6
                    up(n0, c, more)
                    up(n0 + 2, c + FC, more)
                    down(n0 + 4, c, more)
                    down(n0 + 5, c + FC, more)

                if n0 < RING:
                    body(0)
                with sp.Fori(1 if n0 < RING else 0, FFN_BODIES) as i:
                    body(i)
                n, c = n0 + 6 * FFN_BODIES, 2 * FC * FFN_BODIES
                up(n, c, 0)
                down(n + 2, c, 0)

            mixer(0)
            dense(ring, MIX_LOADS, a["ffn_w1"][0], a["ffn_w3"][0], a["ffn_w2"][0])
            mixer(1)
            sp.wait_ge(sem("npass_ready"), 1)
            npass = sp.value_load(npass_i[0:1, 0:1], min_val=1, max_val=2)
            n0 = 2 * MIX_LOADS + FFN_LOADS
            w1, w3, w2 = (a[k].rearrange("o e d f -> (o e d) f") for k in ("moe_w1", "moe_w3", "moe_w2"))
            with sp.Fori(0, npass) as p, sp.Fori(0, E) as e, sp.Fori(0, MOE_BODIES) as k:
                more = (p * E + e) * MOE_LOADS + k * 6
                for s in range(2):
                    for j, w in enumerate((w1, w3)):
                        n = n0 + 2 * s + j
                        ring.load(sp, n, ring.slot(n).rearrange("p (k c) -> p k c", k=DT),
                                  w[bass.ds(e * D, D), bass.ds(k * (2 * FC) + s * FC, FC)].rearrange("(k p) c -> p k c", p=P), more)
                for s in range(2):
                    n = n0 + 4 + s
                    ring.load(sp, n, ring.slot(n).rearrange("p (f d) -> p f d", f=2),
                              w2[bass.ds(e * FE + k * (2 * FC) + s * FC, FC), :].rearrange("(f p) d -> p f d", p=P), more)
            ring2.before = lambda n: sp.wait_ge(ring.used, npass * (E * MOE_LOADS) + (n0 + n + 1 - RING))

            def slots_of(n, k):
                return ring2.slot(n).rearrange("p (k c) -> p k c", k=k)

            for m in range(2):
                ring2.load(sp, N_MEM + m, slots_of(N_MEM + m, DT), cols(a["w_mem_kv_2"][0], FC * m, FC))
            w = a["ffn1_w_in_2"][0]
            dense(ring2, N_FFN1, w[:, 0:FFN], w[:, FFN:2 * FFN], a["ffn1_w_out_2"][0])
            for m, (c, w, _) in enumerate(PROJ2):
                n = N_PROJ2 + m
                ring2.load(sp, n, ring2.slot(n)[:, 0:8 * w].rearrange("p (k c) -> p k c", k=DT), cols(a["w_in_2"][0], c, w))
            for m in range(2):
                ring2.load(sp, N_OA + m, slots_of(N_OA + m, 4), a["w_o_a_2"][0][:, 512 * m:512 * m + 512].rearrange("(k p) c -> p k c", p=P))
            ring2.load(sp, N_OM, slots_of(N_OM, 2), a["w_o_m_2"][0].rearrange("(k p) c -> p k c", p=P))
            for m in range(2):
                ring2.load(sp, N_GLU + m, slots_of(N_GLU + m, 2), a["w_glu_2"][0][:, D * (1 - m):D * (2 - m)].rearrange("(k p) c -> p k c", p=P))
            for m in range(4):
                ring2.load(sp, N_OUT2 + m, slots_of(N_OUT2 + m, DT), cols(a["w_out_2"][0], FC * m, FC))
            w = a["ffn2_w_in_2"][0]
            dense(ring2, N_FFN2, w[:, 0:FFN], w[:, FFN:2 * FFN], a["ffn2_w_out_2"][0])
            sp.wait_ge(sem("x_done"), 1)
            sp.dma_start(out[0].rearrange("(j p) d -> p j d", p=P), x[:, :, :]).then_inc(sem("out_stored"), 16)
            sp.wait_ge(sem("out_stored"), 16)

        @block.gpsimd
        def _(pool):
            st = Steps(pool, sem("pool_steps"))
            ld = sem("params_loaded")
            pool.dma_start(consts[:, :], a["consts"]).then_inc(sem("consts_loaded"), 16)
            for l in range(DEPTH):
                pool.dma_start(prow[R_GCONV:R_GCONV + 36, l, :], a["gdn_conv_w"][l].rearrange("k (t p) -> (k t) p", p=P)).then_inc(ld, 16)
                pool.dma_start(prow[R_DW:R_DW + 2 * TAPS, l, :], a["cnv_dw_w"][l].rearrange("k (t p) -> (k t) p", p=P)).then_inc(ld, 16)
                pool.dma_start(prow[R_DWB:R_DWB + 2, l, :], a["cnv_dw_b"][l].rearrange("(t p) -> t p", p=P)).then_inc(ld, 16)
                pool.dma_start(prow[R_MIX:R_MIX + 8, l, :], a["mix_scale"][l].rearrange("(t p) -> t p", p=P)).then_inc(ld, 16)
                pool.dma_start(hpar[:, l, 0:6], a["gdn_dt_bias"][l].partition_broadcast(P)).then_inc(ld, 16)
                pool.dma_start(hpar[:, l, 6:12], a["fox_f_bias"][l].partition_broadcast(P)).then_inc(ld, 16)
                pool.dma_start(hpar[:, l, 12:18], a["gdn_a_log"][l].partition_broadcast(P)).then_inc(ld, 16)
                pool.dma_start(nrmw[:, l, :], a["gdn_norm_w"][l].partition_broadcast(P)).then_inc(ld, 16)
                pool.dma_start(cln[:, l, 0, :], a["cnv_ln_g"][l].partition_broadcast(P)).then_inc(ld, 16)
                pool.dma_start(cln[:, l, 1, :], a["cnv_ln_b"][l].partition_broadcast(P)).then_inc(ld, 16)
            pool.dma_start(router_sb[:, :, :], a["moe_router"][0].rearrange("(k p) e -> p k e", p=P)).then_inc(ld, 16)
            pool.wait_ge(sem("consts_loaded"), 16)

            def layer_norm_params(u):
                g, b = [("ln_mix_g", "ln_mix_b"), ("ln_ffn_g", "ln_ffn_b")][u % 2]
                if u:
                    pool.wait_ge(sem("ln_done"), u)
                pool.dma_start(lnp[:, 0, :], a[g][u // 2].partition_broadcast(P)).then_inc(sem("lnp_loaded"), 16)
                pool.dma_start(lnp[:, 1, :], a[b][u // 2].partition_broadcast(P)).then_inc(sem("lnp_loaded"), 16)

            def mixer(l):
                pool.wait_ge(sem("logs_ready"), l + 1)
                for j in range(TT):
                    nc.gpsimd.tensor_tensor(four(GM[:, j]), bc(bc(const("gt64"), 1, HP), 1, 2), bc4(gs[:, j, 0:H], P), ALU.mult).then_inc(sem("masked_logs"), 1)
                    nc.gpsimd.tensor_tensor(four(GU[:, j]), bc(bc(const("le64"), 1, HP), 1, 2), bc4(gs[:, j, 0:H], P), ALU.mult).then_inc(sem("masked_logs"), 1)
                for j in range(TT):
                    nc.gpsimd.tensor_tensor(GF[:, j], bc(const("gt256", j, T), 1, H), bc(gs[:, j, H:2 * H], 2, T), ALU.mult).then_inc(sem("masked_forget"), 1)
                for j in range(TT):
                    pool.wait_ge(sem("gdn_act"), 12 * l + 1 + 2 * (j + 1))
                    nc.gpsimd.tensor_tensor(four(Dm[:, j]), four(Dm[:, j]), bc4(beta[:, j], P), ALU.mult).then_inc(sem("decay_beta"), 1)
                for j in range(TT):
                    pool.wait_ge(sem("gdn_act"), 12 * l + 5 + 2 * (j + 1))
                    nc.gpsimd.tensor_tensor(DTm[:, j], DTm[:, j], bc(const("le64"), 1, H), ALU.mult).then_inc(sem("decay_causal"), 1)
                for n in range(LEVELS):
                    for j in range(TT):
                        if n == 0:
                            pool.wait_ge(sem("lower_ready"), l * 4 + 2 * (j + 1))
                        if n >= 2:
                            pool.wait_ge(sem("inv_z"), l * 24 + (n - 2) * 4 + 4)
                        if n == 2:
                            pool.wait_ge(sem("inv_upd"), l * 24 + 4)
                        nc.gpsimd.tensor_tensor(Cl[n % 2][:, j], Lm[:, j], bc(const("lvl", n, P), 1, H), ALU.mult).then_inc(sem("coupling"), 1)

            for l in range(DEPTH):
                layer_norm_params(2 * l)
                mixer(l)
                layer_norm_params(2 * l + 1)

            pool.wait_ge(sem("ln_done"), 3)
            ld = sem("params2_loaded")
            for r, k, n in ((R2_FFN1, "ffn1_norm_2", 8), (R2_MIX, "mix_norm_2", 8), (R2_MEM, "mem_norm_2", 8), (R2_FFN2, "ffn2_norm_2", 8), (R2_D, "ssm_d_2", 2)):
                pool.dma_start(prow2[r:r + n, :], a[k][0].rearrange("(t p) -> t p", p=P)).then_inc(ld, 16)
            for r, k in ((R2_LRE, "ssm_lambda_re_2"), (R2_LIM, "ssm_lambda_im_2")):
                pool.dma_start(prow2[r:r + NS, :], a[k][0].rearrange("(j q) p -> j (q p)", q=2)).then_inc(ld, 16)
            pool.dma_start(log_dt[0:NS, :], a["ssm_log_dt_2"][0].rearrange("(j q) -> j q", q=2)).then_inc(sem("dt_loaded"), 16)
            for i, k in enumerate(("a_q_gain_2", "a_k_gain_2", "m_q_gain_2", "m_k_gain_2")):
                pool.dma_start(headg[:, i, :], a[k][0].partition_broadcast(P)).then_inc(ld, 16)
            for i, k in enumerate(("ssm_b_re_2", "ssm_b_im_2")):
                pool.dma_start(braw[:, i], a[k][0].rearrange("(j q) p c -> (q p) j c", q=2)).then_inc(ld, 16)
            for i, k in enumerate(("ssm_c_re_2", "ssm_c_im_2")):
                pool.dma_start(craw[:, i], a[k][0].rearrange("(u g) c p -> (g c) u p", u=2)).then_inc(ld, 16)
            pool.dma_start(relb[0:32, :], a["rel_bias_2"]).then_inc(ld, 16)
            pool.dma_start(memx[:, :, :], a["mem_2"][0].rearrange("(j p) d -> p j d", p=P)).then_inc(ld, 16)
            pool.wait_ge(sem("dt_loaded"), 16)
            nc.gpsimd.tensor_copy(prow2[R2_LDT:R2_LDT + NS, :].rearrange("j (q p) -> j q p", q=2), bc(log_dt[0:NS, :], 2, HD)).then_inc(sem("dt_spread"), 1)
            cn, sn, t0, t1 = q26[0], q26[1], q26[2], q26[3]
            pool.wait_ge(sem("angles_ready"), 1)
            st.do(nc.gpsimd.memset(Ct[:, :, 0:1], 1.0))
            st.do(nc.gpsimd.memset(St[:, :, 0:1], 0.0))
            n = 1
            while n < T:
                c_, s_ = bc(cn, 2, n), bc(sn, 2, n)
                st.settle()
                for dst, x0, x1, op in ((Ct, Ct, St, ALU.subtract), (St, St, Ct, ALU.add)):
                    y0, y1 = (t_[:, 0:NS * n].rearrange("p (j n) -> p j n", j=NS) for t_ in pw)
                    st.do(nc.gpsimd.tensor_tensor(y0, x0[:, :, 0:n], c_, ALU.mult))
                    st.do(nc.gpsimd.tensor_tensor(y1, x1[:, :, 0:n], s_, ALU.mult))
                    st.settle()
                    st.do(nc.gpsimd.tensor_tensor(dst[:, :, n:2 * n], y0, y1, op))
                    st.settle()
                st.do(nc.gpsimd.tensor_tensor(t0, cn, sn, ALU.mult))
                st.do(nc.gpsimd.tensor_tensor(t1, sn, sn, ALU.mult))
                st.do(nc.gpsimd.tensor_tensor(q26[4], cn, cn, ALU.mult))
                st.settle()
                st.do(nc.gpsimd.tensor_tensor(cn, q26[4], t1, ALU.subtract))
                st.do(nc.gpsimd.tensor_tensor(sn, t0, t0, ALU.add))
                n *= 2
            st.settle()
            nc.gpsimd.memset(q26[2][:, :], 0.0).then_inc(sem("powers_ready"), 1)
            for h in range(AH):
                pool.wait_ge(sem("toep_act"), h + 1)
                pool.dma_start(toep[h], tstage[:, h, :]).then_inc(sem("toep_stored"), 16)
            pool.wait_ge(sem("toep_stored"), 16 * AH)
            flat = toep.rearrange("h p c -> (h p c)")
            for j, (o, w) in enumerate(((0, P), (P, T))):
                first = 255 - P * j
                src = bass.AP(tensor=toep.tensor, offset=first, ap=[[511, P], [P * 512, AH], [1, w]])
                pool.dma_start(bias[:, :, o:o + w], src).then_inc(sem("bias_loaded"), 16)
            pool.wait_ge(sem("bias_loaded"), 32)
            pool.wait_ge(sem("keys_chosen"), 1)
            for h in range(AH):
                nc.gpsimd.tensor_tensor(bias[:, h, :], bias[:, h, :], score, ALU.add).then_inc(sem("bias_ready"), 1)
            pool.wait_ge(sem("merged_ready"), 1)
            pool.dma_start(gates[:, 1, 2 * D:], a["final_norm_2"][0].partition_broadcast(P)).then_inc(sem("final_gain"), 16)

        @block.tensor
        def _(pe):
            mm = nc.tensor.matmul

            def transpose_x(u, src, ready, banks=(0, 1, 2, 3)):
                pe.wait_ge(*ready)
                for b in range(4):
                    for d in range(2):
                        for j in range(TT):
                            i = nc.tensor.transpose(bk(banks[b], 2, T)[:, d, P * j:P * j + P], src[:, j, P * (2 * b + d):P * (2 * b + d + 1)], ident)
                    i.then_inc(sem("xT_psum"), 1)

            def actT_arrived(u):
                pe.wait_ge(sem("xT_act"), 2 * (u + 1))
                pe.wait_ge(sem("xT_dve"), 2 * (u + 1))

            def mixer(l):
                n0 = (MIX_LOADS + FFN_LOADS) * l
                if l == 0:
                    pe.wait_ge(sem("consts_loaded"), 16)
                    transpose_x(0, x, (sem("x_loaded"), 16))
                    pe.wait_ge(sem("params_loaded"), 16 * (10 * DEPTH + 1))
                    for k in range(DEPTH):
                        i = nc.tensor.transpose(bank[4][:, P * k:P * k + ROWS1], prow[0:ROWS1, k, :], ident[0:ROWS1, 0:ROWS1])
                    i.then_inc(sem("pcol_psum"), 1)
                actT_arrived(3 * l)
                if l == 0:
                    pe.wait_ge(sem("pcol_ready"), 1)
                for m, (c, w, kind) in enumerate(PROJ):
                    ring.arrived(pe, n0 + m)
                    if m >= 4:
                        if m - 4 == GLUA_LOAD:
                            pe.wait_ge(sem("glu_ready"), l + 1)
                        else:
                            pe.wait_ge(sem("proj_act"), act_proj(l, m - 4))
                    wt = ring.slot(n0 + m)[:, 0:8 * w].rearrange("p (k c) -> p k c", k=DT)
                    b = m % 4
                    if kind in ("tokA", "tokC"):
                        for j in range(TT):
                            for k in range(DT):
                                i = mm(bk(b, TT, w)[:, j], actT[:, k, P * j:P * j + P], wt[:, k, :], start=k == 0, stop=k == DT - 1)
                    else:
                        for t in range(w // P):
                            for k in range(DT):
                                i = mm(bk(b, 2, T)[:, t], wt[:, k, P * t:P * t + P], actT[:, k, :], start=k == 0, stop=k == DT - 1)
                    i.then_inc(ring.used, 1)

                pe.wait_ge(sem("logs_ready"), l + 1)
                for j in range(TT):
                    g = gs[:, j, 0:H]
                    for q, lhs in enumerate((const("le64"), const("gt64"), const("inhalf", 0, P), const("inhalf", 1, P))):
                        i = mm(bk(4, TT, 24)[:, j, 6 * q:6 * q + 6], lhs, g, start=True, stop=True)
                i.then_inc(sem("gdn_psum"), 1)
                pe.wait_ge(sem("masked_logs"), 4 * (l + 1))
                for m in range(8):
                    j, hb, tr = m % 4 // 2, m % 2, m // 4
                    if m >= 3:
                        pe.wait_ge(sem("gdn_act"), 12 * l + m - 2)
                    src = (GU if tr else GM)[:, j, 3 * hb:3 * hb + 3, :].rearrange("p a b -> p (a b)")
                    mm(bk(4 + (m + 1) % 4, 384), const("gt64") if tr else const("le64"), src, start=True, stop=True).then_inc(sem("gdn_psum"), 1)
                for m in range(3):
                    pe.wait_ge(sem("gdn_act"), 12 * l + 6 + m)
                    pe.wait_ge(sem("qk_squares"), 3 * l + m + 1)
                    mm(bk(4 + (m + 9) % 4, 512), half, sq.rearrange("p a b c -> p (a b c)")[:, 512 * m:512 * m + 512], start=True, stop=True).then_inc(sem("gdn_psum"), 1)
                pe.wait_ge(sem("qk_normed"), l + 1)
                pe.wait_ge(sem("glu_ready"), l + 1)
                pe.wait_ge(sem("proj_act"), act_proj(l, len(PROJ) - 1))
                for m, (t0, j) in enumerate([(3, 0), (3, 1), (6, 0), (6, 1)]):
                    for t in range(3):
                        i = nc.tensor.transpose(bk(m, 3, P)[:, t], qkv[:, t0 + t, P * j:P * j + P], ident)
                    i.then_inc(sem("kv_tok"), 1)
                pe.wait_ge(sem("gdn_act"), 12 * (l + 1))
                for m in range(8):
                    j, hb, tr = m % 4 // 2, m % 2, m // 4
                    if tr:
                        pe.wait_ge(sem("kv_scaled"), 6 * l + (2, 4, 5, 6)[m % 4])
                    for t in range(3):
                        h = 2 * t + hb
                        i = mm(bk(m % 4 + (0 if tr else 4), 3, P)[:, t], qkv[pick(h), 3 + h // 2, P * j:P * j + P],
                               qkv[pick(h), (0 if tr else 3) + h // 2, P * j:P * j + P], start=True, stop=True)
                    i.then_inc(sem("kk_psum"), 1)
                for n in range(LEVELS):
                    for g in range(4):
                        j, hb = g // 2, g % 2
                        pe.wait_ge(sem("coupling"), 12 * l + 2 * n + j + 1)
                        if n == 0:
                            pe.wait_ge(sem("intra_ready"), 4 * l + 4)
                        else:
                            pe.wait_ge(sem("inv_upd"), 4 * (6 * l + n - 1) + g + 1)
                        for t in range(3):
                            h = 3 * hb + t
                            i = mm(bk(g, 3, P)[:, t], Cl[n % 2][:, j, h], ident if n == 0 else Y[:, j, h], start=True, stop=True)
                        i.then_inc(sem("inv_z"), 1)
                    if n == 0:
                        continue
                    for g in range(4):
                        j, hb = g // 2, g % 2
                        pe.wait_ge(sem("inv_zs"), 4 * (5 * l + n - 1) + g + 1)
                        if g >= 2:
                            pe.wait_ge(sem("inv_upd"), 4 * (6 * l + n) + g - 1)
                        for t in range(3):
                            h = 3 * hb + t
                            mm(bk(4 + 2 * (g % 2), 3, P)[:, t], Zs[:, j, h], X[:, j, h], start=True, stop=True)
                        for t in range(3):
                            h = 3 * hb + t
                            i = mm(bk(5 + 2 * (g % 2), 3, P)[:, t], X[:, j, h], Zs[:, j, h], start=True, stop=True)
                        i.then_inc(sem("inv_xy"), 1)
                pe.wait_ge(sem("inv_upd"), 4 * 6 * (l + 1))
                pe.wait_ge(sem("kv_scaled"), 6 * (l + 1))
                for j in range(TT):
                    for h in range(H):
                        i = mm(bk(j, H, HD)[:, h], Y[:, j, slot(h)], vb[:, j, HD * h:HD * h + HD], start=True, stop=True)
                    i.then_inc(sem("uw_psum"), 1)
                    for h in range(H):
                        i = mm(bk(2 + j, HP, P)[pick(h), h // 2], kbe[:, j, HD * h:HD * h + HD], Y[:, j, slot(h)], start=True, stop=True)
                    i.then_inc(sem("uw_psum"), 1)
                pe.wait_ge(sem("uw_act"), 4 * (l + 1))
                for n in range(4):
                    j, r = n // 2, slice(CHUNK * (n % 2), CHUNK * (n % 2) + CHUNK)
                    pe.wait_ge(sem("state_ready"), 5 * l + n + 1)
                    if n:
                        pe.wait_ge(sem("o_ready"), 4 * l + n)
                    for h in range(H):
                        i = mm(bk(4 + h % 2, HP, HD)[r, h // 2], wT[pick(h), j, h // 2, r], S_st[pick(h), h // 2, :], start=True, stop=True)
                    i.then_inc(sem("ws_psum"), 1)
                    for h in range(H):
                        mm(bk(2 + h % 2, HP, HD)[r, h // 2], qkv[pick(h), h // 2, P * j + CHUNK * (n % 2):P * j + CHUNK * (n % 2) + CHUNK], S_st[pick(h), h // 2, :], start=True, stop=True)
                    pe.wait_ge(sem("vnew_ready"), 2 * (4 * l + n + 1))
                    for h in range(H):
                        i = mm(bk(6, HP, HD)[pick(h), h // 2], kend[r, j, HD * h:HD * h + HD], u_sb[r, j, HD * h:HD * h + HD], start=True, stop=True)
                    i.then_inc(sem("supd_psum"), 1)
                    for h in range(H):
                        i = mm(bk(7, H, HD)[r, h], AT[r, j, slot(h), r], u_sb[r, j, HD * h:HD * h + HD], start=True, stop=True)
                    i.then_inc(sem("o_psum"), 1)
                pe.wait_ge(sem("conv_done"), l + 1)
                for j in range(TT):
                    for t in range(2):
                        i = nc.tensor.transpose(bk(j, 2, P)[:, t], uconv[:, t, P * j:P * j + P], ident)
                    i.then_inc(sem("conv_tok"), 1)
                pe.wait_ge(sem("masked_forget"), 2 * (l + 1))
                pe.wait_ge(sem("o_ready"), 4 * (l + 1))

                def scores(h):
                    b = 4 + h % 2
                    if h >= 2:
                        pe.wait_ge(sem("head_biased"), H * l + h - 1)
                    q = [fqk[pick(h), h // 2, P * j:P * j + P] for j in range(TT)]
                    k = fqk[pick(h), 3 + h // 2, :]
                    mm(bank[b][:, 0:P], q[0], k[:, 0:P], start=True, stop=False)
                    mm(bank[b][:, 0:P], const("le"), GF[:, 0, h, 0:P], start=False, stop=True)
                    mm(bank[b][:, P:3 * P], q[1], k, start=True, stop=False)
                    mm(bank[b][:, P:3 * P], ones, GF[:, 0, h, :], start=False, stop=False)
                    mm(bank[b][:, P:3 * P], const("le"), GF[:, 1, h, :], start=False, stop=True).then_inc(sem("head_scores"), 1)

                def weigh(h):
                    pe.wait_ge(sem("head_p"), 2 * (H * l + h + 1))
                    if h >= 2:
                        pe.wait_ge(sem("head_pT"), H * l + h - 1)
                    for t in range(3):
                        i = nc.tensor.transpose(bk(6 + h % 2, 3, P)[:, t], fp[h % 2][:, P * t:P * t + P], ident)
                    i.then_inc(sem("head_pT_psum"), 1)
                    pe.wait_ge(sem("head_pT"), H * l + h + 1)
                    if h == 0:
                        pe.wait_ge(sem("conv_ln"), 2 * (l + 1))
                    v = [tokC[:, j, HD * h:HD * h + HD] for j in range(TT)]
                    pt = fpT[h % 2]
                    mm(bk(2, H, HD)[:, h], pt[:, 0:P], v[0], start=True, stop=True)
                    mm(bk(3, H, HD)[:, h], pt[:, P:2 * P], v[0], start=True, stop=False)
                    mm(bk(3, H, HD)[:, h], pt[:, 2 * P:3 * P], v[1], start=False, stop=True).then_inc(sem("head_o"), 1)

                scores(0)
                for h in range(H):
                    if h + 1 < H:
                        scores(h + 1)
                    weigh(h)
                transpose_x(3 * l + 1, mixed, (sem("mixed_ready"), l + 1))
                actT_arrived(3 * l + 1)
                for m in range(OUT_LOADS):
                    n = n0 + len(PROJ) + m
                    ring.arrived(pe, n)
                    wt = ring.slot(n).rearrange("p (k c) -> p k c", k=DT)
                    for j in range(TT):
                        for k in range(DT):
                            i = mm(bk(4 + m, TT, FC)[:, j], actT[:, k, P * j:P * j + P], wt[:, k, :], start=k == 0, stop=k == DT - 1)
                    i.then_inc(ring.used, 1)
                transpose_x(3 * l + 2, x, (sem("ln_done"), 2 * l + 1))

            def dense(ring, n0, u):
                hs = 22 * u

                def up(n, s, rounds):
                    w = [ring.slot(n + j).rearrange("p (k c) -> p k c", k=DT) for j in range(2)]
                    for j in range(2):
                        ring.arrived(pe, n + j, rounds)
                        for f in range(2):
                            for k in range(DT):
                                i = mm(bk(4 + 2 * s + f, 2, T)[:, j], w[j][:, k, P * f:P * f + P], actT[:, k, :], start=k == 0, stop=k == DT - 1)
                        i.then_inc(ring.used, 1)

                def down(n, s, rounds):
                    ring.arrived(pe, n, rounds)
                    w = ring.slot(n).rearrange("p (f d) -> p f d", f=2)
                    for f in range(2):
                        for j in range(TT):
                            for q in range(2):
                                i = mm(bank[2 * j + q][:, :], hT[:, 2 * s + f, P * j:P * j + P], w[:, f, 512 * q:512 * q + 512],
                                       start=False, stop=False, skip_group_check=True)
                    i.then_inc(ring.used, 1)

                pe.wait_ge(sem("y_zeroed"), u + 1)
                with pe.Fori(0, FFN_BODIES) as i:
                    pe.wait_ge(sem("h_ready"), i * 4 + hs)
                    up(n0, 0, i)
                    up(n0 + 2, 1, i)
                    for s in range(2):
                        pe.wait_ge(sem("h_ready"), i * 4 + hs + 2 * s + 2)
                        down(n0 + 4 + s, s, i)
                n = n0 + 6 * FFN_BODIES
                pe.wait_ge(sem("h_ready"), hs + 4 * FFN_BODIES)
                up(n, 0, 0)
                pe.wait_ge(sem("h_ready"), hs + 4 * FFN_BODIES + 2)
                down(n + 2, 0, 0)

            def moe(n0):
                for j in range(TT):
                    for k in range(DT):
                        i = mm(bank[4][:, E * j:E * j + E], actT[:, k, P * j:P * j + P], router_sb[:, k, :], start=k == 0, stop=k == DT - 1)
                i.then_inc(sem("router_psum"), 1)
                pe.wait_ge(sem("sel_ready"), 1)
                mm(bank[5][:, 0:E], const("lt"), sel[:, 0], start=True, stop=True)
                mm(bank[5][:, E:2 * E], ones, sel[:, 0], start=True, stop=False)
                mm(bank[5][:, E:2 * E], const("lt"), sel[:, 1], start=False, stop=True)
                mm(bank[5][:, 2 * E:3 * E], ones, sel[:, 0], start=True, stop=False)
                mm(bank[5][:, 2 * E:3 * E], ones, sel[:, 1], start=False, stop=True).then_inc(sem("place_psum"), 1)
                pe.wait_ge(sem("npass_ready"), 1)
                npass = pe.value_load(npass_i[0:1, 0:1], min_val=1, max_val=2)
                with pe.Fori(0, npass) as p, pe.Fori(0, E) as e:
                    it = p * E + e
                    pe.wait_ge(sem("perm_ready"), it * 2 + 2)
                    pe.wait_ge(sem("y_added"), it * 4)
                    for b in range(2):
                        for d in range(4):
                            for j in range(TT):
                                i = mm(bk(b, 4, CAP)[:, d], x[:, j, P * (4 * b + d):P * (4 * b + d + 1)], Pm[:, j, :], start=j == 0, stop=j == TT - 1)
                        i.then_inc(sem("gather_psum"), 1)
                    for j in range(TT):
                        i = nc.tensor.transpose(bk(2, TT, P)[:, j], PG[:, j, :], ident)
                    i.then_inc(sem("gather_psum"), 1)
                    with pe.Fori(0, MOE_BODIES) as k:
                        rounds = it * MOE_BODIES + k
                        hs = rounds * 2
                        pe.wait_ge(sem("gather_act"), it * 2 + 2)
                        pe.wait_ge(sem("gather_dve"), it + 1)
                        pe.wait_ge(sem("moe_zeroed"), it + 1)
                        pe.wait_ge(sem("moe_h"), hs)
                        for s in range(2):
                            for j in range(2):
                                n = n0 + 2 * s + j
                                ring.arrived(pe, n, rounds)
                                w = ring.slot(n).rearrange("p (k c) -> p k c", k=DT)
                                for f in range(2):
                                    for kk in range(DT):
                                        i = mm(bk(4 + s, 2, 2, CAP)[:, j, f], w[:, kk, P * f:P * f + P], xgT[:, kk, :], start=kk == 0, stop=kk == DT - 1)
                                i.then_inc(ring.used, 1)
                        for s in range(2):
                            n = n0 + 4 + s
                            pe.wait_ge(sem("moe_h"), hs + s + 1)
                            ring.arrived(pe, n, rounds)
                            w = ring.slot(n).rearrange("p (f d) -> p f d", f=2)
                            for f in range(2):
                                for q in range(2):
                                    i = mm(bank[6 + q][:, :], hT[:, 2 * s + f, 0:CAP], w[:, f, 512 * q:512 * q + 512],
                                           start=False, stop=False, skip_group_check=True)
                            i.then_inc(ring.used, 1)
                    pe.wait_ge(sem("ysb_ready"), it * 2 + 2)
                    for j in range(TT):
                        for q in range(2):
                            mm(bank[2 * j + q][:, :], PGT[:, j, :], Ysb[:, 512 * q:512 * q + 512], start=True, stop=True).then_inc(sem("scatter_psum"), 1)

            def prepare():
                pe.wait_ge(sem("params2_loaded"), 16 * 17)
                pe.wait_ge(sem("dt_spread"), 1)
                nc.tensor.transpose(bank[4][:, 0:ROWS2], prow2[0:ROWS2, :], ident[0:ROWS2, 0:ROWS2]).then_inc(sem("pcol_psum"), 1)
                pe.wait_ge(sem("relb_ready"), 1)
                for h in range(AH):
                    if h >= 2:
                        pe.wait_ge(sem("toep_act"), h - 1)
                    mm(bank[5 + h % 2][:, :], relb_bc[0:32, h, :], const("hot")[0:32, :], start=True, stop=True).then_inc(sem("toep_psum"), 1)
                transpose_x(6, memx, (sem("rms_done"), 1))
                actT_arrived(6)
                pe.wait_ge(sem("pcol_ready"), 2)
                for m in range(2):
                    ring2.arrived(pe, N_MEM + m)
                    wt = ring2.slot(N_MEM + m).rearrange("p (k c) -> p k c", k=DT)
                    for j in range(TT):
                        for k in range(DT):
                            i = mm(bk((4, 7)[m], TT, FC)[:, j], memT[:, k, P * j:P * j + P], wt[:, k, :], start=k == 0, stop=k == DT - 1)
                    i.then_inc(ring2.used, 1)
                pe.wait_ge(sem("toep_act"), AH)
                pe.wait_ge(sem("blocks_ready"), 1)
                for g in range(2):
                    for r in range(2):
                        nc.tensor.transpose(bk(5, 2, 2, P)[:, g, r], blk[:, r, 4 * g:4 * g + 4, :].rearrange("p j c -> p (j c)"), ident)
                        i = nc.tensor.transpose(bk(6, 2, 2, P)[:, g, r], cd[:, r, g].rearrange("p q c -> p (q c)"), ident)
                i.then_inc(sem("bc_psum"), 1)
                pe.wait_ge(sem("mk_normed"), 1)
                for t in range(2):
                    for j in range(TT):
                        i = nc.tensor.transpose(bk(4, 2, T)[:, t, P * j:P * j + P], mkv[:, j, P * t:P * t + P], ident)
                i.then_inc(sem("mkT_psum"), 1)

            def branches():
                def project(m):
                    c, w, kind = PROJ2[m]
                    n = N_PROJ2 + m
                    b = m % 4
                    ring2.arrived(pe, n)
                    if m >= 4:
                        pe.wait_ge(sem("proj2_act"), m - 3)
                    wt = ring2.slot(n)[:, 0:8 * w].rearrange("p (k c) -> p k c", k=DT)
                    if kind in ("qi", "us"):
                        for t in range(2):
                            for k in range(DT):
                                i = mm(bk(b, 2, T)[:, t], wt[:, k, P * t:P * t + P], actT[:, k, :], start=k == 0, stop=k == DT - 1)
                    elif kind == "kiw":
                        for q in range(2):
                            for k in range(DT):
                                mm(bank[b][HD * q:HD * q + HD, 0:T], wt[:, k, 0:HD], actT[:, k, :], start=k == 0, stop=k == DT - 1)
                        for j in range(TT):
                            for k in range(DT):
                                i = mm(bank[b][:, T + IH * j:T + IH * j + IH], actT[:, k, P * j:P * j + P], wt[:, k, HD:], start=k == 0, stop=k == DT - 1)
                    else:
                        for j in range(TT):
                            for k in range(DT):
                                i = mm(bk(b, TT, w)[:, j], actT[:, k, P * j:P * j + P], wt[:, k, :], start=k == 0, stop=k == DT - 1)
                    i.then_inc(ring2.used, 1)

                for m in range(7):
                    project(m)
                pe.wait_ge(sem("proj2_act"), 2)
                for h in range(IH):
                    q = [qiT[pick(h), h // 2, P * j:P * j + P] for j in range(TT)]
                    mm(bank[4 + h][:, 0:P], q[0], kiT[pick(h), 0:P], start=True, stop=True)
                    mm(bank[4 + h][:, P:3 * P], q[1], kiT[pick(h), :], start=True, stop=True).then_inc(sem("idx_psum"), 1)
                pe.wait_ge(sem("proj2_act"), 6)
                for j in range(NS):
                    if j < 4:
                        pe.wait_ge(sem("idx_rel"), j + 1)
                    else:
                        pe.wait_ge(sem("bu_act"), j - 3)
                    r = slice(32 * (j % 4), 32 * (j % 4) + 32)
                    for q in range(2):
                        i = mm(bk(4 + j % 4, 2, T)[:, q], bT[r, j // 4, q, :], uT[r, j // 4, :], start=True, stop=True)
                    i.then_inc(sem("bu_psum"), 1)
                for m in range(7, 13):
                    project(m)
                pe.wait_ge(sem("bu_act"), NS)
                pe.wait_ge(sem("heads_normed"), 1)
                for b, (src, t) in enumerate(((qa, 0), (qa, 2), (qm, 0))):
                    for d in range(2):
                        for j in range(TT):
                            i = nc.tensor.transpose(bk(4 + b, 2, T)[:, d, P * j:P * j + P], src[:, j, P * (t + d):P * (t + d) + P], ident)
                    i.then_inc(sem("qT_psum"), 1)
                for j in range(TT):
                    i = nc.tensor.transpose(bank[7][:, P * j:P * j + P], kd[:, j, :], ident)
                i.then_inc(sem("qT_psum"), 1)
                for m in range(13, len(PROJ2)):
                    project(m)
                pe.wait_ge(sem("states_ready"), 1)
                pe.wait_ge(sem("proj2_act"), len(PROJ2))
                for j in range(NS):
                    r = slice(32 * (j % 4), 32 * (j % 4) + 32)
                    for q in range(2):
                        i = mm(bank[j // 4][r, 0:T], cT[:, j // 4, q, r], bu[:, j, q, :], start=q == 0, stop=q == 1)
                i.then_inc(sem("y_psum"), 1)
                pe.wait_ge(sem("qT_act"), 4)

                def scores(h):
                    b = 4 + h % 2
                    if h >= 2:
                        pe.wait_ge(sem("head_biased"), HEADS1 + h - 1)
                    if h < AH:
                        mm(bank[b][:, 0:P], qaT[pick(h), h // 2, 0:P], kaT[pick(h), 0:P], start=True, stop=True)
                        i = mm(bank[b][:, P:3 * P], qaT[pick(h), h // 2, P:T], kaT[pick(h), :], start=True, stop=True)
                    else:
                        g = h - AH
                        for j in range(TT):
                            i = mm(bk(b, 2, T)[:, j], qmT[pick(g), g // 2, P * j:P * j + P], mkT[pick(g), g // 2, :], start=True, stop=True)
                    i.then_inc(sem("head_scores"), 1)

                def weigh(h):
                    pe.wait_ge(sem("head_p"), 2 * (HEADS1 + h + 1))
                    if h >= 2:
                        pe.wait_ge(sem("head_pT"), HEADS1 + h - 1)
                    for t in range(3 if h < AH else 4):
                        i = nc.tensor.transpose(bk(6 + h % 2, 4, P)[:, t], ap_[h % 2][:, P * t:P * t + P], ident)
                    i.then_inc(sem("head_pT_psum"), 1)
                    pe.wait_ge(sem("head_pT"), HEADS1 + h + 1)
                    pt = apT[h % 2]
                    if h < AH:
                        vv = [kva[:, j, HD:] for j in range(TT)]
                        mm(bk(2, AH, HD)[:, h], pt[:, 0:P], vv[0], start=True, stop=True)
                        mm(bk(3, AH, HD)[:, h], pt[:, P:2 * P], vv[0], start=True, stop=False)
                        i = mm(bk(3, AH, HD)[:, h], pt[:, 2 * P:3 * P], vv[1], start=False, stop=True)
                    else:
                        g = h - AH
                        if g == 0:
                            pe.wait_ge(sem("y_read"), 2)
                        for j in range(TT):
                            for k in range(TT):
                                i = mm(bk(j, MH, HD)[:, g], pt[:, P * (2 * j + k):P * (2 * j + k + 1)], mkv[:, k, T + HD * g:T + HD * g + HD], start=k == 0, stop=k == 1)
                    i.then_inc(sem("head_o"), 1)

                scores(0)
                for h in range(AH + MH):
                    if h + 1 < AH + MH:
                        scores(h + 1)
                    weigh(h)
                pe.wait_ge(sem("branch_ready"), 1)
                pe.wait_ge(sem("head_pT"), HEADS1 + AH + MH)
                for b in range(3):
                    if b == 2:
                        pe.wait_ge(sem("branch_ready"), 2)
                    for d in range(2):
                        for j in range(TT):
                            src = oa[:, j, P * (2 * b + d):P * (2 * b + d + 1)] if b < 2 else om[:, j, P * d:P * d + P]
                            i = nc.tensor.transpose(bk(4 + b, 2, T)[:, d, P * j:P * j + P], src, ident)
                    i.then_inc(sem("oT_psum"), 1)
                pe.wait_ge(sem("oT_act"), 3)
                for m in range(2):
                    ring2.arrived(pe, N_OA + m)
                    wt = ring2.slot(N_OA + m).rearrange("p (k c) -> p k c", k=4)
                    for j in range(TT):
                        for k in range(4):
                            i = mm(bank[2 * m + j][:, :], actT[:, k, P * j:P * j + P], wt[:, k, :], start=k == 0, stop=k == 3)
                    i.then_inc(ring2.used, 1)

                def wide(n, lhs, b0):
                    ring2.arrived(pe, n)
                    wt = ring2.slot(n).rearrange("p (k c) -> p k c", k=2)
                    for j in range(TT):
                        for q in range(2):
                            for k in range(2):
                                i = mm(bank[b0 + 2 * j + q][:, :], lhs[:, k, P * j:P * j + P], wt[:, k, 512 * q:512 * q + 512], start=k == 0, stop=k == 1)
                    i.then_inc(ring2.used, 1)

                wide(N_OM, actT[:, 4:6, :], 4)
                pe.wait_ge(sem("ys_ready"), 1)
                pe.wait_ge(sem("oa_merged"), 4)
                wide(N_GLU, uT, 0)
                pe.wait_ge(sem("om_gated"), 4)
                wide(N_GLU + 1, uT, 4)
                transpose_x(9, hbuf, (sem("merged_ready"), 1))
                actT_arrived(9)
                for m in range(4):
                    n = N_OUT2 + m
                    ring2.arrived(pe, n)
                    wt = ring2.slot(n).rearrange("p (k c) -> p k c", k=DT)
                    for j in range(TT):
                        for k in range(DT):
                            i = mm(bk(4 + m, TT, FC)[:, j], actT[:, k, P * j:P * j + P], wt[:, k, :], start=k == 0, stop=k == DT - 1)
                    i.then_inc(ring2.used, 1)

            mixer(0)
            actT_arrived(2)
            dense(ring, MIX_LOADS, 0)
            transpose_x(3, x, (sem("ln_done"), 2))
            mixer(1)
            actT_arrived(5)
            moe(2 * MIX_LOADS + FFN_LOADS)
            prepare()
            transpose_x(7, hbuf, (sem("rms_done"), 2))
            actT_arrived(7)
            pe.wait_ge(sem("mkT_act"), 1)
            dense(ring2, N_FFN1, 1)
            transpose_x(8, hbuf, (sem("rms_done"), 3))
            actT_arrived(8)
            branches()
            transpose_x(10, hbuf, (sem("rms_done"), 4))
            actT_arrived(10)
            dense(ring2, N_FFN2, 2)

        @block.scalar
        def _(act):
            def a_(o, i, f, inc, **kw):
                nc.scalar.activation(o, i, f, **kw).then_inc(sem(inc), 1)

            def xT_out(u, scale=None, actT=actT):
                for b in (0, 2):
                    act.wait_ge(sem("xT_psum"), 4 * u + b + 1)
                    if scale is None:
                        a_(actT[:, 2 * b:2 * b + 2, :], bk(b, 2, T), ACT.Copy, "xT_act")
                    else:
                        a_(actT[:, 2 * b, :], bk(b, 2, T)[:, 0], ACT.Copy, "act_steps", scale=scale(2 * b))
                        a_(actT[:, 2 * b + 1, :], bk(b, 2, T)[:, 1], ACT.Copy, "xT_act", scale=scale(2 * b + 1))

            def norm_std(u):
                act.wait_ge(sem("ln_var"), u + 1)
                a_(std[:, 0:TT], mv[:, :, 1], ACT.Sqrt, "ln_std", bias=LN_EPS)

            def mixer(l):
                n0 = (MIX_LOADS + FFN_LOADS) * l
                if l == 0:
                    xT_out(0)
                    act.wait_ge(sem("params_loaded"), 16 * (10 * DEPTH + 1))
                    a_(hpar[:, :, 18:24], hpar[:, :, 12:18], ACT.Exp, "exp_a")

                def project(m):
                    c, w, kind = PROJ[m]
                    act.wait_ge(ring.used, n0 + m + 1)
                    b = m % 4
                    if kind == "tokA":
                        o = 0 if c == C_DECAY else 198
                        a_(tokA[:, :, o:o + w], bk(b, TT, w), ACT.Copy, "proj_act")
                    elif kind == "tokC":
                        a_(tokC[:, :, c - C_FV:c - C_FV + w], bk(b, TT, w), ACT.Copy, "proj_act")
                    elif kind == "qkv":
                        t = c // P
                        a_(qkv_raw[:, t:t + w // P, 3:3 + T], bk(b, 2, T)[:, 0:w // P], ACT.Copy, "proj_act")
                    elif kind == "glub":
                        a_(sigb[:, :, :], bk(b, 2, T), ACT.Sigmoid, "proj_act")
                    elif kind == "fqk":
                        t = (c - C_FQ) // P
                        nq = min(max(3 - t, 0), 2)
                        if nq:
                            a_(fqk[:, t:t + nq, :], bk(b, 2, T)[:, 0:nq], ACT.Copy, "proj_act" if nq == 2 else "act_steps", scale=HD ** -0.5)
                        if nq < 2:
                            a_(fqk[:, t + nq:t + 2, :], bk(b, 2, T)[:, nq:2], ACT.Copy, "proj_act")

                for m in range(3):
                    project(m)
                act.wait_ge(sem("gates_abs"), l + 1)
                a_(lg1[:, :, :], az[:, :, :], ACT.Exp, "act_gate", scale=-1.0)
                act.wait_ge(sem("act_gate"), 3 * l + 1)
                a_(lg1[:, :, :], lg1[:, :, :], ACT.Ln, "act_gate", bias=1.0)
                a_(beta[:, :, :], tokA[:, :, 6:12], ACT.Sigmoid, "act_gate")
                for m in range(3, len(PROJ) - 1):
                    if m == GLUA_LOAD:
                        continue
                    project(m)
                project(len(PROJ) - 1)
                for t in range(9):
                    act.wait_ge(sem("short_conv"), 9 * l + t + 1)
                    a_(qkv[:, t, :], qkv[:, t, :], ACT.Silu, "short_silu")
                for m in range(3):
                    act.wait_ge(sem("short_silu"), 9 * l + 2 * m + 2)
                    a_(sq.rearrange("p a b c -> p (a b c)")[:, 512 * m:512 * m + 512].rearrange("p (a b) -> p a b", a=2),
                       qkv[:, 2 * m:2 * m + 2, :], ACT.Square, "qk_squares")
                act.wait_ge(sem("gdn_psum"), 12 * l + 1)
                a_(eg[:, :, :], bk(4, TT, 24), ACT.Exp, "gdn_act")
                for m in range(8):
                    j, hb, tr = m % 4 // 2, m % 2, m // 4
                    act.wait_ge(sem("gdn_psum"), 12 * l + m + 2)
                    a_((DTm if tr else Dm)[:, j, 3 * hb:3 * hb + 3, :], bk(4 + (m + 1) % 4, 3, P), ACT.Exp, "gdn_act")
                for m in range(3):
                    act.wait_ge(sem("gdn_psum"), 12 * l + m + 10)
                    a_(rn[:, 2 * m:2 * m + 2, :], bk(4 + (m + 9) % 4, 2, T), ACT.Sqrt, "gdn_act", bias=NORM_EPS)
                a_(tokA[:, :, 12:396], tokA[:, :, 12:396], ACT.Silu, "gate_silu")
                for n in range(1, LEVELS):
                    for g in range(4):
                        j, hb = g // 2, g % 2
                        act.wait_ge(sem("inv_z"), 24 * l + 4 * n + g + 1)
                        a_(Zs[:, j, 3 * hb:3 * hb + 3, :], bk(g, 3, P), ACT.Copy, "inv_zs")
                for j in range(TT):
                    act.wait_ge(sem("uw_psum"), 4 * l + 2 * j + 1)
                    a_(u_sb[:, j, :], bk(j, GW), ACT.Copy, "uw_act")
                    act.wait_ge(sem("uw_psum"), 4 * l + 2 * j + 2)
                    a_(wT[:, j], bk(2 + j, HP, P), ACT.Copy, "uw_act")
                act.wait_ge(sem("o_sumsq"), l + 1)
                a_(rr12[:, :], ss12[:, :], ACT.Sqrt, "o_std", scale=1.0 / HD, bias=NORM_EPS)
                act.wait_ge(sem("conv_var"), l + 1)
                a_(std[:, 0:TT], mv[:, :, 1], ACT.Sqrt, "conv_std", bias=LN_EPS)
                act.wait_ge(sem("conv_normed"), l + 1)
                a_(mixed[:, :, GW:GW + CW], mixed[:, :, GW:GW + CW], ACT.Silu, "conv_out")
                for h in range(H):
                    act.wait_ge(sem("head_max"), H * l + h + 1)
                    if h >= 2:
                        act.wait_ge(sem("head_pT_psum"), H * l + h - 1)
                    act.wait_ge(sem("head_max"), H * l + h + 1)
                    a_(fp[h % 2][:, 0:P], fs[h % 2][:, 0:P], ACT.Exp, "head_p", bias=fneg[:, h, 0:1], accum_out=fsum[:, h, 0:1])
                    a_(fp[h % 2][:, P:3 * P], fs[h % 2][:, P:3 * P], ACT.Exp, "head_p", bias=fneg[:, h, 1:2], accum_out=fsum[:, h, 1:2])
                    act.wait_ge(sem("head_pT_psum"), H * l + h + 1)
                    if h >= 2:
                        act.wait_ge(sem("head_o"), H * l + h - 1)
                    a_(fpT[h % 2], bk(6 + h % 2, 384), ACT.Copy, "head_pT")
                xT_out(3 * l + 1, lambda t: pcol[:, l, R_MIX + t:R_MIX + t + 1])
                norm_std(2 * l)
                xT_out(3 * l + 2)

            def dense(ring, n0, u):
                hs = 22 * u

                def silus(qs, counts, i):
                    for q in qs:
                        act.wait_ge(ring.used, counts[q // 2])
                        a_(sil[:, q, :], bk(4 + q, 2, T)[:, 0], ACT.Silu, "sil_ready")

                with act.Fori(0, FFN_BODIES) as i:
                    act.wait_ge(sem("h_ready"), i * 4 + hs)
                    silus(range(4), [i * 6 + n0 + 2, i * 6 + n0 + 4], i)
                act.wait_ge(sem("h_ready"), hs + 4 * FFN_BODIES)
                silus(range(2), [n0 + 6 * FFN_BODIES + 2], 0)

            def moe(n0):
                act.wait_ge(sem("router_max"), 1)
                for j in range(TT):
                    a_(ex[:, j], lgt[:, j], ACT.Exp, "router_exp", bias=m1[:, j:j + 1])
                act.wait_ge(sem("npass_ready"), 1)
                npass = act.value_load(npass_i[0:1, 0:1], min_val=1, max_val=2)
                with act.Fori(0, npass) as p, act.Fori(0, E) as e:
                    it = p * E + e
                    act.wait_ge(sem("gather_psum"), it * 3 + 1)
                    a_(xgT[:, 0:4, :], bk(0, 4, CAP), ACT.Copy, "gather_act")
                    act.wait_ge(sem("gather_psum"), it * 3 + 3)
                    a_(PGT[:, :, :], bk(2, TT, P), ACT.Copy, "gather_act")
                    with act.Fori(0, MOE_BODIES) as k:
                        rounds = it * MOE_BODIES + k
                        act.wait_ge(sem("moe_h"), rounds * 2)
                        for s in range(2):
                            act.wait_ge(ring.used, rounds * 6 + n0 + 2 * s + 2)
                            a_(sil[:, s, :], bk(4 + s, 2, T)[:, 0], ACT.Silu, "moe_sil")
                    act.wait_ge(ring.used, it * MOE_LOADS + n0 + MOE_LOADS)
                    a_(Ysb[:, 0:512], bank[6][:, :], ACT.Copy, "ysb_ready")

            def gain(r):
                return lambda t: pcol2[:, r + t:r + t + 1]

            def rms(u, src, ready):
                act.wait_ge(*ready)
                for j in range(TT):
                    a_(hbuf[:, j, :], src[:, j, :], ACT.Square, "rms_sq", accum_out=ss2[:, j:j + 1])
                act.wait_ge(sem("rms_sq"), TT * (u + 1))
                a_(r2[:, :], ss2[:, :], ACT.Sqrt, "rms_std", scale=1.0 / D, bias=NORM_EPS)

            def prepare():
                act.wait_ge(sem("pcol_ready"), 2)
                a_(q26[5][:, :], pcol2[:, R2_LDT:R2_LDT + NS], ACT.Exp, "dt_ready")
                for h in range(AH):
                    act.wait_ge(sem("toep_psum"), h + 1)
                    a_(tstage[:, h, :], bank[5 + h % 2][:, :], ACT.Copy, "toep_act")
                act.wait_ge(sem("angle_reduced"), 1)
                a_(q26[8][:, :], q26[6][:, :], ACT.Exp, "unit_act")
                a_(q26[1][:, :], q26[10][:, :], ACT.Sin, "unit_act")
                a_(q26[11][:, :], q26[10][:, :], ACT.Sin, "unit_act", scale=0.5)
                act.wait_ge(sem("params2_loaded"), 16 * 17)
                rms(0, memx, (sem("ln_done"), 4))
                xT_out(6, gain(R2_MEM), memT)
                for m in range(2):
                    act.wait_ge(ring2.used, N_MEM + m + 1)
                    a_(mkv[:, :, T * m:T * m + T], bk((4, 7)[m], TT, FC), ACT.Copy, "mkv_ready")
                act.wait_ge(sem("mk_sumsq"), 1)
                a_(rq[:, 0:TT * MH], ssq[:, 0:TT * MH], ACT.Sqrt, "mk_std", scale=1.0 / HD, bias=NORM_EPS)
                act.wait_ge(sem("mkT_psum"), 1)
                a_(mkT[:, :, :], bk(4, 2, T), ACT.Copy, "mkT_act")

            def branches():
                def project(m):
                    c, w, kind = PROJ2[m]
                    act.wait_ge(ring2.used, N_PROJ2 + m + 1)
                    b = m % 4
                    o = bk(b, TT, w)
                    if m == 0:
                        act.wait_ge(sem("powers_ready"), 1)
                    if kind == "qi":
                        a_(qiT[:, :, :], o, ACT.Copy, "proj2_act")
                    elif kind == "kiw":
                        a_(kiT, bank[b][:, 0:T], ACT.Copy, "act_steps")
                        a_(wi[:, :, :], bank[b][:, T:T + TT * IH].rearrange("p (j h) -> p j h", j=TT), ACT.Copy, "proj2_act", scale=IH ** -0.5)
                    elif kind == "qa":
                        a_(qa[:, :, c - C_QA:c - C_QA + w], o, ACT.Copy, "proj2_act")
                    elif kind == "kv":
                        a_(kva[:, :, :], o, ACT.Copy, "proj2_act")
                    elif kind == "us":
                        a_(uT[:, :, :], o, ACT.Copy, "proj2_act")
                    elif kind == "qm":
                        a_(qm[:, :, :], o, ACT.Copy, "proj2_act")
                    else:
                        a_(gates[:, :, c - C_G:c - C_G + w], o, ACT.Sigmoid, "proj2_act")

                for m in range(7):
                    project(m)
                for h in range(IH):
                    act.wait_ge(sem("idx_psum"), h + 1)
                    a_(rel[:, h, :], bk(4 + h, 3 * P), ACT.Relu, "idx_rel", scale=HD ** -0.5)
                for j in range(NS):
                    act.wait_ge(sem("bu_psum"), j + 1)
                    if j == 0:
                        act.wait_ge(sem("toep_stored"), 16 * AH)
                    a_(bu[:, j], bk(4 + j % 4, 2, T), ACT.Copy, "bu_act")
                act.wait_ge(sem("heads_sumsq"), 1)
                a_(rq[:, :], ssq[:, :], ACT.Sqrt, "heads_std", scale=1.0 / HD, bias=NORM_EPS)
                for m in range(7, 13):
                    project(m)
                for b in range(4):
                    act.wait_ge(sem("qT_psum"), b + 1)
                    dst = (qaT[:, 0:2, :], qaT[:, 2:4, :], qmT[:, :, :])[b] if b < 3 else kaT
                    a_(dst, bk(4 + b, 2, T) if b < 3 else bank[7][:, 0:T], ACT.Copy, "qT_act")
                for m in range(13, len(PROJ2)):
                    project(m)
                act.wait_ge(sem("y_read"), 2)
                a_(uT[:, :, :], uT[:, :, :], ACT.Gelu_apprx_tanh, "ys_ready")
                for h in range(AH + MH):
                    act.wait_ge(sem("head_max"), HEADS1 + h + 1)
                    if h >= 2:
                        act.wait_ge(sem("head_pT_psum"), HEADS1 + h - 1)
                    for j in range(TT):
                        if h < AH:
                            c = (slice(0, P), slice(P, 3 * P))[j]
                            src = al[h % 2][:, c]
                        else:
                            c = slice(T * j, T * j + T)
                            src = bank[4 + h % 2][:, c]
                        a_(ap_[h % 2][:, c], src, ACT.Exp, "head_p", bias=aneg[:, h, j:j + 1], accum_out=asum[:, h, j:j + 1])
                    act.wait_ge(sem("head_pT_psum"), HEADS1 + h + 1)
                    if h >= 2:
                        act.wait_ge(sem("head_o"), HEADS1 + h - 1)
                    w = 3 * P if h < AH else 4 * P
                    a_(apT[h % 2][:, 0:w], bk(6 + h % 2, w), ACT.Copy, "head_pT")
                for b in range(3):
                    act.wait_ge(sem("oT_psum"), b + 1)
                    a_(actT[:, 2 * b:2 * b + 2, :], bk(4 + b, 2, T), ACT.Copy, "oT_act")
                act.wait_ge(ring2.used, N_GLU + 1)
                for j in range(TT):
                    for q in range(2):
                        a_(gl[:, j, 512 * q:512 * q + 512], bank[2 * j + q][:, :], ACT.Sigmoid, "glu_sig")
                xT_out(9)

            mixer(0)
            dense(ring, MIX_LOADS, 0)
            norm_std(1)
            xT_out(3)
            mixer(1)
            moe(2 * MIX_LOADS + FFN_LOADS)
            norm_std(3)
            prepare()
            rms(1, x, (sem("mk_normed"), 1))
            xT_out(7, gain(R2_FFN1))
            dense(ring2, N_FFN1, 1)
            rms(2, x, (sem("x_fed"), 1))
            xT_out(8, gain(R2_MIX))
            branches()
            rms(3, x, (sem("x_mixed"), 1))
            xT_out(10, gain(R2_FFN2))
            dense(ring2, N_FFN2, 2)
            rms(4, x, (sem("x_fed"), 2))

        @block.vector
        def _(dve):
            v = nc.vector
            st = Steps(dve, sem("dve_steps"))

            def xT_out(u, scale=None, actT=actT):
                for b in (1, 3):
                    dve.wait_ge(sem("xT_psum"), 4 * u + b + 1)
                    if scale is None:
                        v.tensor_copy(actT[:, 2 * b:2 * b + 2, :], bk(b, 2, T)).then_inc(sem("xT_dve"), 1)
                    else:
                        st.do(v.tensor_scalar(actT[:, 2 * b, :], bk(b, 2, T)[:, 0], scale(2 * b), None, ALU.mult))
                        v.tensor_scalar(actT[:, 2 * b + 1, :], bk(b, 2, T)[:, 1], scale(2 * b + 1), None, ALU.mult).then_inc(sem("xT_dve"), 1)

            def layer_norm(u):
                for j in range(TT):
                    for q in range(2):
                        st.do(v.bn_stats(bst[:, j, q, :], x[:, j, 512 * q:512 * q + 512]))
                st.settle()
                for j in range(TT):
                    i = v.bn_aggr(mv[:, j, :], bst[:, j].rearrange("p a b -> p (a b)"))
                    if j == 0:
                        st.do(i)
                i.then_inc(sem("ln_var"), 1)
                dve.wait_ge(sem("ln_std"), u + 1)
                st.do(v.reciprocal(rstd[:, 0:TT], std[:, 0:TT]))
                st.settle()
                for j in range(TT):
                    st.do(v.tensor_scalar(x[:, j, :], x[:, j, :], mv[:, j, 0:1], rstd[:, j:j + 1], ALU.subtract, ALU.mult))
                dve.wait_ge(sem("lnp_loaded"), 32 * (u + 1))
                st.settle()
                for j in range(TT):
                    st.do(v.tensor_tensor(x[:, j, :], x[:, j, :], lnp[:, 0, :], ALU.mult))
                st.settle()
                for j in range(TT):
                    i = v.tensor_tensor(x[:, j, :], x[:, j, :], lnp[:, 1, :], ALU.add)
                    if j == 0:
                        st.do(i)
                i.then_inc(sem("ln_done"), 1)
                dve.wait_ge(sem("ln_done"), u + 1)

            def mixer(l):
                n0 = (MIX_LOADS + FFN_LOADS) * l
                if l == 0:
                    st.do(v.memset(qkv_raw[:, :, 0:3], 0.0))
                    st.do(v.memset(uraw[:, :, 0:TAPS - 1], 0.0))
                    xT_out(0)
                    dve.wait_ge(sem("pcol_psum"), 1)
                    v.tensor_copy(pcol[:, :, 0:ROWS1], bk(4, 2, P)[:, :, 0:ROWS1]).then_inc(sem("pcol_ready"), 1)
                    dve.wait_ge(sem("exp_a"), 1)
                    st.do(v.tensor_scalar(hpar[:, :, 12:18], hpar[:, :, 18:24], -1.0, None, ALU.mult))
                    st.settle()
                    st.do(v.memset(hpar[:, :, 18:24], -1.0))
                    dve.wait_ge(sem("pcol_ready"), 1)
                    st.settle()
                else:
                    st.do(v.memset(qkv_raw[:, :, 0:3], 0.0))
                    st.do(v.memset(uraw[:, :, 0:TAPS - 1], 0.0))
                st.do(v.memset(S_st[:, :, :], 0.0))
                dve.wait_ge(sem("proj_act"), act_proj(l, 2))
                st.do(v.tensor_tensor(s1[:, :, 0:6], tokA[:, :, 0:6], bc(hpar[:, l, 0:6], 1, TT), ALU.add))
                for j in range(TT):
                    st.do(v.scalar_tensor_tensor(s1[:, j, 6:12], tokC[:, j, 384:390], -1.0, hpar[:, l, 6:12], ALU.mult, ALU.subtract))
                st.settle()
                v.scalar_tensor_tensor(az[:, :, :], s1[:, :, :], -1.0, s1[:, :, :], ALU.mult, ALU.max).then_inc(sem("gates_abs"), 1)
                dve.wait_ge(sem("act_gate"), 3 * l + 2)
                st.do(v.scalar_tensor_tensor(s1[:, :, :], s1[:, :, :], 0.0, lg1[:, :, :], ALU.max, ALU.add))
                st.settle()
                v.tensor_tensor(gs[:, :, :], s1[:, :, :], bc(hpar[:, l, 12:24], 1, TT), ALU.mult).then_inc(sem("logs_ready"), 1)
                for t in range(9):
                    ld = 3 + t // 2
                    dve.wait_ge(sem("proj_act"), act_proj(l, ld))
                    wv = [pcol[:, l, R_GCONV + 9 * k + t:R_GCONV + 9 * k + t + 1] for k in range(4)]
                    st.do(v.tensor_scalar(qkv[:, t, :], qkv_raw[:, t, 0:T], wv[0], None, ALU.mult))
                    for k in range(1, 4):
                        st.settle()
                        i = v.scalar_tensor_tensor(qkv[:, t, :], qkv_raw[:, t, k:k + T], wv[k], qkv[:, t, :], ALU.mult, ALU.add)
                        if k < 3:
                            st.do(i)
                    i.then_inc(sem("short_conv"), 1)
                dve.wait_ge(ring.used, n0 + GLUA_LOAD + 1)
                dve.wait_ge(sem("proj_act"), act_proj(l, GLUA_LOAD - 1))
                v.tensor_tensor(uraw[:, :, TAPS - 1:], bk(GLUA_LOAD % 4, 2, T), sigb[:, :, :], ALU.mult).then_inc(sem("glu_ready"), 1)
                for m in range(3):
                    dve.wait_ge(sem("gdn_act"), 12 * l + 10 + m)
                    st.do(v.reciprocal(rn[:, 2 * m:2 * m + 2, :], rn[:, 2 * m:2 * m + 2, :]))
                st.settle()
                st.do(v.scalar_tensor_tensor(qkv[:, 0:3, :], qkv[:, 0:3, :], HD ** -0.5, rn[:, 0:3, :], ALU.mult, ALU.mult))
                v.tensor_tensor(qkv[:, 3:6, :], qkv[:, 3:6, :], rn[:, 3:6, :], ALU.mult).then_inc(sem("qk_normed"), 1)
                dve.wait_ge(sem("qk_normed"), l + 1)
                dve.wait_ge(sem("act_gate"), 3 * l + 3)
                st.do(v.tensor_tensor(cb[:, :, :], beta[:, :, :], eg[:, :, 0:6], ALU.mult))
                st.settle()
                for p in range(2):
                    for q in range(2):
                        st.do(v.tensor_copy(eglp[HD * q:HD * q + HD, :, p, :], eg[HD * q:HD * q + HD, :, 12 + 6 * p + q:18 + 6 * p:2]))
                for j in range(TT):
                    dve.wait_ge(sem("kv_tok"), 4 * l + j + 1)
                    kt = bk(j, H, HD)
                    v.tensor_tensor(kbe[:, j].rearrange("p (h d) -> p h d", h=H), kt, bc(cb[:, j], 2, HD), ALU.mult).then_inc(sem("kv_scaled"), 1)
                    v.tensor_tensor(kend[:, j].rearrange("p (h d) -> p h d", h=H), kt, bc(eg[:, j, 6:12], 2, HD), ALU.mult).then_inc(sem("kv_scaled"), 1)
                for j in range(TT):
                    dve.wait_ge(sem("kv_tok"), 4 * l + 2 + j + 1)
                    v.tensor_tensor(vb[:, j].rearrange("p (h d) -> p h d", h=H), bk(2 + j, H, HD), bc(beta[:, j], 2, HD), ALU.mult).then_inc(sem("kv_scaled"), 1)
                for m in range(4):
                    j, hb = m // 2, m % 2
                    dve.wait_ge(sem("kk_psum"), 8 * l + m + 1)
                    dve.wait_ge(sem("decay_beta"), 2 * l + j + 1)
                    v.tensor_tensor(Lm[:, j, 3 * hb:3 * hb + 3, :], bk(4 + m, 3, P), Dm[:, j, 3 * hb:3 * hb + 3, :], ALU.mult).then_inc(sem("lower_ready"), 1)
                for m in range(4):
                    j, hb = m // 2, m % 2
                    dve.wait_ge(sem("kk_psum"), 8 * l + 4 + m + 1)
                    dve.wait_ge(sem("decay_causal"), 2 * l + j + 1)
                    v.tensor_tensor(AT[:, j, 3 * hb:3 * hb + 3, :], bk(m, 3, P), DTm[:, j, 3 * hb:3 * hb + 3, :], ALU.mult).then_inc(sem("intra_ready"), 1)

                def conv_taps(k):
                    st.settle()
                    for t in range(2):
                        if k == 0:
                            st.do(v.tensor_scalar(uconv[:, t, :], uraw[:, t, 0:T], taps(l, 0, t), pcol[:, l, R_DWB + t:R_DWB + t + 1], ALU.mult, ALU.add))
                        elif k < TAPS:
                            i = v.scalar_tensor_tensor(uconv[:, t, :], uraw[:, t, k:k + T], taps(l, k, t), uconv[:, t, :], ALU.mult, ALU.add)
                            if k == TAPS - 1 and t == 1:
                                i.then_inc(sem("conv_done"), 1)
                            else:
                                st.do(i)

                dve.wait_ge(sem("glu_ready"), l + 1)
                k = 0
                for n in range(LEVELS):
                    for g in range(4):
                        j, hb = g // 2, g % 2
                        hs = slice(3 * hb, 3 * hb + 3)
                        if n == 0:
                            dve.wait_ge(sem("inv_z"), 24 * l + g + 1)
                            st.do(v.tensor_tensor(X[:, j, hs, :], bc(ident, 1, 3), Cl[0][:, j, hs, :], ALU.subtract))
                            v.tensor_tensor(Y[:, j, hs, :], bc(ident, 1, 3), bk(g, 3, P), ALU.subtract).then_inc(sem("inv_upd"), 1)
                            continue
                        for _ in range(2):
                            conv_taps(k)
                            k += 1
                        dve.wait_ge(sem("inv_xy"), 4 * (5 * l + n - 1) + g + 1)
                        dve.wait_ge(sem("inv_upd"), 4 * (6 * l + n - 1) + g + 1)
                        st.do(v.tensor_tensor(X[:, j, hs, :], X[:, j, hs, :], bk(4 + 2 * (g % 2), 3, P), ALU.subtract))
                        v.tensor_tensor(Y[:, j, hs, :], Y[:, j, hs, :], bk(5 + 2 * (g % 2), 3, P), ALU.subtract).then_inc(sem("inv_upd"), 1)
                v.tensor_copy(S_st[:, :, :], S_st[:, :, :]).then_inc(sem("state_ready"), 1)
                dve.wait_ge(sem("uw_act"), 4 * (l + 1))
                for n in range(4):
                    j, p = n // 2, n % 2
                    r = slice(CHUNK * p, CHUNK * p + CHUNK)
                    dve.wait_ge(sem("ws_psum"), 4 * l + n + 1)
                    dve.wait_ge(sem("state_ready"), 5 * l + n + 1)
                    for q in range(2):
                        uq = u_sb[r, j, :].rearrange("p (t q d) -> p q t d", q=2, d=HD)[:, q]
                        v.tensor_tensor(uq, uq, bk(4 + q, HP, HD)[r], ALU.subtract).then_inc(sem("vnew_ready"), 1)
                    dve.wait_ge(sem("supd_psum"), 4 * l + n + 1)
                    st.do(v.tensor_tensor(S_st[:, :, :], S_st[:, :, :], bc(eglp[:, j, p, :], 2, HD), ALU.mult))
                    for q in range(2):
                        st.do(v.tensor_tensor(oq[r].rearrange("p (t q d) -> p q t d", q=2, d=HD)[:, q], bk(2 + q, HP, HD)[r], bc(eg[r, j, q:6:2], 2, HD), ALU.mult))
                    st.settle()
                    v.tensor_tensor(S_st[:, :, :], S_st[:, :, :], bk(6, HP, HD), ALU.add).then_inc(sem("state_ready"), 1)
                    dve.wait_ge(sem("o_psum"), 4 * l + n + 1)
                    v.tensor_tensor(mixed[r, j, 0:GW], oq[r], bk(7, GW)[r], ALU.add).then_inc(sem("o_ready"), 1)
                dve.wait_ge(sem("o_ready"), 4 * (l + 1))
                dve.wait_ge(sem("gate_silu"), l + 1)
                for j in range(TT):
                    st.do(v.tensor_tensor(kbe[:, j, :], mixed[:, j, 0:GW], mixed[:, j, 0:GW], ALU.mult))
                st.settle()
                v.tensor_reduce(ss12[:, :], kbe.rearrange("p j (h d) -> p (j h) d", h=H), AX_X, ALU.add).then_inc(sem("o_sumsq"), 1)
                for j in range(TT):
                    m3 = mixed[:, j, 0:GW].rearrange("p (h d) -> p h d", h=H)
                    st.do(v.tensor_tensor(m3, m3, bc(nrmw[:, l, :], 1, H), ALU.mult))
                dve.wait_ge(sem("o_std"), l + 1)
                st.do(v.reciprocal(rr12[:, :], rr12[:, :]))
                st.settle()
                for j in range(TT):
                    m3 = mixed[:, j, 0:GW].rearrange("p (h d) -> p h d", h=H)
                    st.do(v.tensor_tensor(m3, m3, bc(rr12[:, H * j:H * j + H], 2, HD), ALU.mult))
                st.settle()
                for j in range(TT):
                    st.do(v.tensor_tensor(mixed[:, j, 0:GW], mixed[:, j, 0:GW], tokA[:, j, 12:396], ALU.mult))
                dve.wait_ge(sem("conv_tok"), 2 * (l + 1))
                for j in range(TT):
                    st.do(v.bn_stats(bst[:, j, 0, :], bk(j, CW)))
                st.settle()
                st.do(v.bn_aggr(mv[:, 0, :], bst[:, 0, 0, :]))
                v.bn_aggr(mv[:, 1, :], bst[:, 1, 0, :]).then_inc(sem("conv_var"), 1)
                dve.wait_ge(sem("conv_std"), l + 1)
                st.do(v.reciprocal(rstd[:, 0:TT], std[:, 0:TT]))
                st.settle()
                for j in range(TT):
                    v.tensor_scalar(mixed[:, j, GW:GW + CW], bk(j, CW), mv[:, j, 0:1], rstd[:, j:j + 1], ALU.subtract, ALU.mult).then_inc(sem("conv_ln"), 1)
                dve.wait_ge(sem("conv_ln"), 2 * (l + 1))
                st.do(v.tensor_tensor(mixed[:, :, GW:GW + CW], mixed[:, :, GW:GW + CW], bc(cln[:, l, 0, :], 1, TT), ALU.mult))
                st.settle()
                v.tensor_tensor(mixed[:, :, GW:GW + CW], mixed[:, :, GW:GW + CW], bc(cln[:, l, 1, :], 1, TT), ALU.add).then_inc(sem("conv_normed"), 1)
                for h in range(H):
                    dve.wait_ge(sem("head_scores"), H * l + h + 1)
                    if h >= 2:
                        dve.wait_ge(sem("head_p"), 2 * (H * l + h - 1))
                    v.tensor_tensor(fs[h % 2], bk(4 + h % 2, 384), const("foxmask"), ALU.add).then_inc(sem("head_biased"), 1)
                    dve.wait_ge(sem("head_biased"), H * l + h + 1)
                    st.do(v.tensor_reduce(fneg[:, h, 0:1], fs[h % 2][:, 0:P], AX_X, ALU.max, negate=True))
                    v.tensor_reduce(fneg[:, h, 1:2], fs[h % 2][:, P:3 * P], AX_X, ALU.max, negate=True).then_inc(sem("head_max"), 1)
                dve.wait_ge(sem("head_p"), 2 * H * (l + 1))
                st.do(v.reciprocal(frec[:, :, :], fsum[:, :, :]))
                st.settle()
                dve.wait_ge(sem("head_o"), H * (l + 1))
                dve.wait_ge(sem("conv_out"), l + 1)
                for j in range(TT):
                    i = v.tensor_tensor(mixed[:, j, GW + CW:].rearrange("p (h d) -> p h d", h=H), bk(2 + j, H, HD), bc(frec[:, :, j], 2, HD), ALU.mult)
                    if j == 0:
                        st.do(i)
                i.then_inc(sem("mixed_ready"), 1)
                xT_out(3 * l + 1, lambda t: pcol[:, l, R_MIX + t:R_MIX + t + 1])
                for m in range(OUT_LOADS):
                    dve.wait_ge(ring.used, n0 + len(PROJ) + m + 1)
                    xs = x[:, :, FC * m:FC * m + FC]
                    st.do(v.scalar_tensor_tensor(xs, xs, ALPHA, bk(4 + m, TT, FC), ALU.mult, ALU.add))
                st.settle()
                layer_norm(2 * l)
                xT_out(3 * l + 2)

            def dense(ring, n0, u, tx):
                hs = 22 * u
                dve.wait_ge(sem("xT_act"), 2 * (tx + 1))
                dve.wait_ge(sem("xT_dve"), 2 * (tx + 1))
                for b in range(4):
                    i = v.memset(bank[b][:, :], 0.0)
                    if b < 3:
                        st.do(i)
                i.then_inc(sem("y_zeroed"), 1)

                def products(qs, ready):
                    for q in qs:
                        dve.wait_ge(sem("sil_ready"), ready + q + 1)
                        v.tensor_tensor(hT[:, q, :], sil[:, q, :], bk(4 + q, 2, T)[:, 1], ALU.mult).then_inc(sem("h_ready"), 1)

                with dve.Fori(0, FFN_BODIES) as i:
                    dve.wait_ge(ring.used, i * 6 + n0)
                    products(range(4), i * 4 + hs)
                dve.wait_ge(ring.used, n0 + 6 * FFN_BODIES)
                products(range(2), hs + 4 * FFN_BODIES)
                dve.wait_ge(ring.used, n0 + FFN_LOADS)

            def moe(n0):
                dve.wait_ge(sem("router_psum"), 1)
                st.do(v.tensor_copy(lgt[:, :, :], bk(4, TT, E)))
                st.settle()
                v.tensor_reduce(m1[:, :], lgt[:, :, :], AX_X, ALU.max, negate=True).then_inc(sem("router_max"), 1)
                for j in range(TT):
                    row, col = bc(lgt[:, j], 1, E), bc(lgt[:, j], 2, E)
                    st.do(v.tensor_tensor(gtm[:, j].rearrange("p (a b) -> p a b", a=E), row, col, ALU.is_gt))
                    st.do(v.tensor_tensor(eqm[:, j].rearrange("p (a b) -> p a b", a=E), row, col, ALU.is_equal))
                st.settle()
                st.do(v.tensor_tensor(eqm[:, :, :], eqm[:, :, :], bc(const("lower8"), 1, TT), ALU.mult))
                st.settle()
                st.do(v.tensor_tensor(gtm[:, :, :], gtm[:, :, :], eqm[:, :, :], ALU.add))
                st.settle()
                st.do(v.tensor_reduce(rank.rearrange("p j e -> p (j e)"), gtm.rearrange("p j (a b) -> p (j a) b", a=E), AX_X, ALU.add))
                st.settle()
                v.tensor_scalar(sel[:, :, :], rank[:, :, :], 1.5, None, ALU.is_lt).then_inc(sem("sel_ready"), 1)
                dve.wait_ge(sem("sel_ready"), 1)
                dve.wait_ge(sem("router_exp"), 2)
                st.do(v.tensor_tensor(ex[:, :, :], ex[:, :, :], sel[:, :, :], ALU.mult))
                st.settle()
                st.do(v.tensor_reduce(esum[:, :], ex[:, :, :], AX_X, ALU.add))
                st.settle()
                st.do(v.reciprocal(esum[:, :], esum[:, :]))
                st.settle()
                st.do(v.tensor_tensor(gate[:, :, :], ex[:, :, :], bc(esum[:, :], 2, E), ALU.mult))
                dve.wait_ge(sem("place_psum"), 1)
                st.do(v.tensor_copy(posx[:, :, 0, :], bk(5, TT, E)))
                st.do(v.tensor_reduce(cnt[:, 0:1], bank[5][:, 2 * E:3 * E], AX_X, ALU.max))
                st.settle()
                st.do(v.scalar_tensor_tensor(posx[:, :, 0, :], posx[:, :, 0, :], 1.0, sel[:, :, :], ALU.add, ALU.mult))
                st.do(v.tensor_scalar(cnt[:, 1:2], cnt[:, 0:1], CAP + 0.5, 1.0, ALU.is_gt, ALU.add))
                st.settle()
                st.do(v.tensor_scalar(posx[:, :, 1, :], posx[:, :, 0, :], -1.0 - CAP, None, ALU.add))
                v.tensor_copy(npass_i[:, :], cnt[:, 1:2]).then_inc(sem("npass_ready"), 1)
                st.settle()
                st.do(v.tensor_scalar(posx[:, :, 0, :], posx[:, :, 0, :], -1.0, None, ALU.add))
                st.do(v.tensor_scalar(yacc[:, :, :], x[:, :, :], ALPHA, None, ALU.mult))
                dve.wait_ge(sem("npass_ready"), 1)
                st.settle()
                npass = dve.value_load(npass_i[0:1, 0:1], min_val=1, max_val=2)
                with dve.Fori(0, npass) as p, dve.Fori(0, E) as e:
                    it = p * E + e
                    dve.wait_ge(sem("gather_psum"), it * 3)
                    v.tensor_copy(poscol[:, :], posx.rearrange("p j a e -> p j (a e)")[:, :, bass.ds(it, 1)].rearrange("p j o -> p (j o)")).then_inc(sem("sel_steps"), 1)
                    v.tensor_copy(gcol[:, :], gate[:, :, bass.ds(e, 1)].rearrange("p j o -> p (j o)")).then_inc(sem("sel_steps"), 1)
                    dve.wait_ge(sem("sel_steps"), it * 4 + 2)
                    for j in range(TT):
                        v.tensor_scalar(Pm[:, j, :], const("iota"), poscol[:, j:j + 1], None, ALU.is_equal).then_inc(sem("sel_steps"), 1)
                    dve.wait_ge(sem("sel_steps"), it * 4 + 4)
                    for j in range(TT):
                        v.tensor_scalar(PG[:, j, :], Pm[:, j, :], gcol[:, j:j + 1], None, ALU.mult).then_inc(sem("perm_ready"), 1)
                    dve.wait_ge(sem("gather_psum"), it * 3 + 2)
                    v.tensor_copy(xgT[:, 4:8, :], bk(1, 4, CAP)).then_inc(sem("gather_dve"), 1)
                    dve.wait_ge(sem("ysb_ready"), it * 2)
                    v.memset(bank[6][:, :], 0.0)
                    v.memset(bank[7][:, :], 0.0).then_inc(sem("moe_zeroed"), 1)
                    with dve.Fori(0, MOE_BODIES) as k:
                        rounds = it * MOE_BODIES + k
                        dve.wait_ge(ring.used, rounds * 6 + n0)
                        for s in range(2):
                            dve.wait_ge(sem("moe_sil"), rounds * 2 + s + 1)
                            v.tensor_tensor(hT[:, 2 * s:2 * s + 2, 0:CAP], sil[:, s, :].rearrange("p (f c) -> p f c", f=2), bk(4 + s, 2, 2, CAP)[:, 1], ALU.mult).then_inc(sem("moe_h"), 1)
                    dve.wait_ge(ring.used, it * MOE_LOADS + n0 + MOE_LOADS)
                    v.tensor_copy(Ysb[:, 512:1024], bank[7][:, :]).then_inc(sem("ysb_ready"), 1)
                    for j in range(TT):
                        for q in range(2):
                            dve.wait_ge(sem("scatter_psum"), it * 4 + 2 * j + q + 1)
                            ys = yacc[:, j, 512 * q:512 * q + 512]
                            v.tensor_tensor(ys, ys, bank[2 * j + q][:, :], ALU.add).then_inc(sem("y_added"), 1)
                dve.wait_ge(sem("y_added"), npass * (4 * E))

            mixer(0)
            dense(ring, MIX_LOADS, 0, 2)
            for j in range(TT):
                for q in range(2):
                    xs = x[:, j, 512 * q:512 * q + 512]
                    st.do(v.scalar_tensor_tensor(xs, xs, ALPHA, bank[2 * j + q][:, :], ALU.mult, ALU.add))
            st.settle()
            layer_norm(1)
            xT_out(3)
            mixer(1)
            moe(2 * MIX_LOADS + FFN_LOADS)
            st.do(v.tensor_copy(x[:, :, :], yacc[:, :, :]))
            st.settle()
            layer_norm(3)

            def gain(r):
                return lambda t: pcol2[:, r + t:r + t + 1]

            def rms(u, src, dst):
                dve.wait_ge(sem("rms_std"), u + 1)
                st.do(v.reciprocal(r2[:, :], r2[:, :]))
                st.settle()
                for j in range(TT):
                    i = v.tensor_scalar(dst[:, j, :], src[:, j, :], r2[:, j:j + 1], None, ALU.mult)
                    if j == 0:
                        st.do(i)
                i.then_inc(sem("rms_done"), 1)

            def op(ins):
                st.do(ins)
                st.settle()

            def prepare():
                tt = v.tensor_tensor
                dve.wait_ge(sem("pcol_psum"), 2)
                v.tensor_copy(pcol2[:, 0:ROWS2], bank[4][:, 0:ROWS2]).then_inc(sem("pcol_ready"), 1)
                v.tensor_copy(relb_bc[0:32], bc(relb[0:32, :], 2, P)).then_inc(sem("relb_ready"), 1)
                dve.wait_ge(sem("relb_ready"), 1)
                lr, li = pcol2[:, R2_LRE:R2_LRE + NS], pcol2[:, R2_LIM:R2_LIM + NS]
                cn, sn = q26[0], q26[1]
                dve.wait_ge(sem("dt_ready"), 1)
                op(tt(q26[6], lr, q26[5], ALU.mult))
                op(tt(q26[7], li, q26[5], ALU.mult))
                op(v.tensor_scalar(q26[9], q26[7], float(1 / (2 * np.pi)), ROUND, ALU.mult, ALU.add))
                op(v.tensor_scalar(q26[9], q26[9], ROUND, None, ALU.subtract))
                op(v.scalar_tensor_tensor(q26[10], q26[9], -TWO_PI[0], q26[7], ALU.mult, ALU.add))
                op(v.scalar_tensor_tensor(q26[10], q26[9], -TWO_PI[1], q26[10], ALU.mult, ALU.add))
                op(v.scalar_tensor_tensor(q26[10], q26[9], -TWO_PI[2], q26[10], ALU.mult, ALU.add))
                v.tensor_scalar(q26[10], q26[10], PI_F, -PI_F, ALU.min, ALU.max).then_inc(sem("angle_reduced"), 1)
                op(v.tensor_scalar(headg[:, 0:3:2, :], headg[:, 0:3:2, :], HD ** -0.5, None, ALU.mult))
                dve.wait_ge(sem("unit_act"), 3)
                op(tt(q26[12], q26[11], q26[11], ALU.mult))
                op(v.tensor_scalar(cn, q26[12], -2.0, 1.0, ALU.mult, ALU.add))
                op(tt(q26[13], q26[8], cn, ALU.mult))
                v.tensor_tensor(q26[14], q26[8], sn, ALU.mult).then_inc(sem("angles_ready"), 1)
                dve.wait_ge(sem("angles_ready"), 1)
                op(tt(q26[15], lr, lr, ALU.mult))
                op(tt(q26[5], li, li, ALU.mult))
                op(tt(q26[15], q26[15], q26[5], ALU.add))
                op(v.reciprocal(q26[15], q26[15]))
                op(v.tensor_scalar(q26[13], q26[13], 1.0, None, ALU.subtract))
                op(tt(q26[5], q26[13], lr, ALU.mult))
                op(tt(q26[6], q26[14], li, ALU.mult))
                op(tt(q26[5], q26[5], q26[6], ALU.add))
                op(tt(q26[5], q26[5], q26[15], ALU.mult))
                op(tt(q26[7], q26[14], lr, ALU.mult))
                op(tt(q26[9], q26[13], li, ALU.mult))
                op(tt(q26[7], q26[7], q26[9], ALU.subtract))
                op(tt(q26[7], q26[7], q26[15], ALU.mult))
                fr, fi = bc(q26[5], 2, 16), bc(q26[7], 2, 16)
                op(v.memset(blk[:, :, :, :], 0.0))
                for r, (b0, b1, o) in enumerate(((0, 1, ALU.subtract), (1, 0, ALU.add))):
                    op(tt(btmp[:, 0], fr, braw[:, b0], ALU.mult))
                    op(tt(btmp[:, 1], fi, braw[:, b1], ALU.mult))
                    for q in range(2):
                        hs = slice(HD * q, HD * q + HD)
                        op(tt(blk[hs, r, :, 16 * q:16 * q + 16], btmp[hs, 0], btmp[hs, 1], o))
                for r in range(2):
                    for q in range(2):
                        i = v.tensor_scalar(cd[:, r, :, q, :], craw[:, r], const("parity")[:, q:q + 1], (1.0, -1.0)[r], ALU.mult, ALU.mult)
                        if (r, q) != (1, 1):
                            st.do(i)
                i.then_inc(sem("blocks_ready"), 1)
                rms(0, memx, memx)
                xT_out(6, gain(R2_MEM), memT)
                dve.wait_ge(sem("bc_psum"), 1)
                op(v.tensor_copy(bT[:, :, :, :], bk(5, 2, 2, P)))
                op(v.tensor_copy(cT[:, :, :, :], bk(6, 2, 2, P)))
                dve.wait_ge(sem("mkv_ready"), 1)
                mk = mkv[:, :, 0:T]
                op(tt(hbuf[:, :, 0:T], mk, mk, ALU.mult))
                v.tensor_reduce(ssq[:, 0:TT * MH].rearrange("p (j h) -> p j h", j=TT), hbuf[:, :, 0:T].rearrange("p j (h d) -> p j h d", d=HD), AX_X, ALU.add).then_inc(sem("mk_sumsq"), 1)
                dve.wait_ge(sem("mk_std"), 1)
                op(v.reciprocal(rq[:, 0:TT * MH], rq[:, 0:TT * MH]))
                for j in range(TT):
                    m3 = mkv[:, j, 0:T].rearrange("p (h d) -> p h d", d=HD)
                    op(tt(m3, m3, bc(rq[:, MH * j:MH * j + MH], 2, HD), ALU.mult))
                    i = tt(m3, m3, bc(headg[:, 3, :], 1, MH), ALU.mult)
                    if j == 0:
                        op(i)
                i.then_inc(sem("mk_normed"), 1)

            def branches():
                tt = v.tensor_tensor
                dve.wait_ge(sem("proj2_act"), 7)
                st.do(tt(hbuf[:, :, 0:512], qa[:, :, :], qa[:, :, :], ALU.mult))
                st.do(tt(hbuf[:, :, 512:576], kva[:, :, 0:HD], kva[:, :, 0:HD], ALU.mult))
                st.do(tt(hbuf[:, :, 576:832], qm[:, :, :], qm[:, :, :], ALU.mult))
                st.settle()
                v.tensor_reduce(ssq.rearrange("p (j h) -> p j h", j=TT), hbuf[:, :, 0:832].rearrange("p j (h d) -> p j h d", d=HD), AX_X, ALU.add).then_inc(sem("heads_sumsq"), 1)
                dve.wait_ge(sem("heads_std"), 1)
                op(v.reciprocal(rq[:, :], rq[:, :]))
                for j in range(TT):
                    r = rq[:, 13 * j:13 * j + 13]
                    q3, m3 = (t[:, j, :].rearrange("p (h d) -> p h d", d=HD) for t in (qa, qm))
                    st.do(tt(q3, q3, bc(r[:, 0:8], 2, HD), ALU.mult))
                    st.do(tt(m3, m3, bc(r[:, 9:13], 2, HD), ALU.mult))
                    st.do(v.scalar_tensor_tensor(kd[:, j, 0:HD], kva[:, j, 0:HD], r[:, 8:9], headg[:, 1, :], ALU.mult, ALU.mult))
                    st.settle()
                    st.do(tt(q3, q3, bc(headg[:, 0, :], 1, AH), ALU.mult))
                    st.do(tt(m3, m3, bc(headg[:, 2, :], 1, MH), ALU.mult))
                    i = v.tensor_copy(kd[:, j, HD:], kd[:, j, 0:HD])
                    if j == 0:
                        st.do(i)
                i.then_inc(sem("heads_normed"), 1)
                dve.wait_ge(sem("heads_normed"), 1)
                dve.wait_ge(sem("idx_rel"), IH)
                parts = (slice(0, P), slice(P, 3 * P))
                for h in range(IH):
                    for j, c in enumerate(parts):
                        w = wi[:, j, h:h + 1]
                        if h == 0:
                            st.do(v.tensor_scalar(score[:, c], rel[:, h, c], w, None, ALU.mult))
                        else:
                            st.do(v.scalar_tensor_tensor(score[:, c], rel[:, h, c], w, score[:, c], ALU.mult, ALU.add))
                    st.settle()
                cap = const("cap")
                st.do(tt(work[:, parts[0]], score[:, parts[0]], cap[:, 0:P], ALU.min))
                st.do(tt(work[:, parts[1]], score[:, parts[1]], cap[:, T:2 * T], ALU.min))
                st.settle()
                for _ in range(TOPK // 8):
                    for j, c in enumerate(parts):
                        st.do(v.max(max8[:, j, :], work[:, c]))
                    st.settle()
                    for j, c in enumerate(parts):
                        st.do(v.match_replace(out=work[:, c], in_to_replace=max8[:, j, :], in_values=work[:, c], imm_value=-3.0e38))
                    st.settle()
                v.tensor_scalar(score, work, -2.5e38, NEG, ALU.is_gt, ALU.mult).then_inc(sem("keys_chosen"), 1)
                dve.wait_ge(sem("bu_act"), NS)
                dve.wait_ge(sem("powers_ready"), 1)
                for sign in (-1, 1):
                    for j in range(NS):
                        c, s, br, bi = Ct[:, j, :], St[:, j, :], bu[:, j, 0, :], bu[:, j, 1, :]
                        t0, t1, t2 = hbuf[:, 0, 0:T], hbuf[:, 0, T:2 * T], hbuf[:, 0, 2 * T:3 * T]
                        st.do(tt(t0, br, s, ALU.mult))
                        st.do(tt(t1, bi, s, ALU.mult))
                        st.do(tt(t2, bi, c, ALU.mult))
                        st.do(tt(br, br, c, ALU.mult))
                        st.settle()
                        st.do(tt(br, br, t1, ALU.add if sign < 0 else ALU.subtract))
                        st.do(tt(bi, t2, t0, ALU.subtract if sign < 0 else ALU.add))
                        st.settle()
                        if sign < 0:
                            m = q26[8][:, j:j + 1].broadcast_to([P, T])
                            st.do(v.tensor_tensor_scan(br, m, br, 0.0, ALU.mult, ALU.add))
                            st.do(v.tensor_tensor_scan(bi, m, bi, 0.0, ALU.mult, ALU.add))
                            st.settle()
                st.do(v.tensor_copy(ss2[:, :], ss2[:, :]))
                st.settle()
                v.tensor_copy(r2[:, :], r2[:, :]).then_inc(sem("states_ready"), 1)
                dve.wait_ge(sem("y_psum"), 1)
                for t in range(2):
                    v.scalar_tensor_tensor(uT[:, t, :], uT[:, t, :], pcol2[:, R2_D + t:R2_D + t + 1], bank[t][:, 0:T], ALU.mult, ALU.add).then_inc(sem("y_read"), 1)
                for h in range(AH + MH):
                    dve.wait_ge(sem("head_scores"), HEADS1 + h + 1)
                    if h >= 2:
                        dve.wait_ge(sem("head_p"), 2 * (HEADS1 + h - 1))
                    if h < AH:
                        dve.wait_ge(sem("bias_ready"), h + 1)
                        v.tensor_tensor(al[h % 2], bk(4 + h % 2, 3 * P), bias[:, h, :], ALU.add).then_inc(sem("head_biased"), 1)
                        dve.wait_ge(sem("head_biased"), HEADS1 + h + 1)
                        st.do(v.tensor_reduce(aneg[:, h, 0:1], al[h % 2][:, 0:P], AX_X, ALU.max, negate=True))
                        v.tensor_reduce(aneg[:, h, 1:2], al[h % 2][:, P:3 * P], AX_X, ALU.max, negate=True).then_inc(sem("head_max"), 1)
                    else:
                        v.tensor_reduce(aneg[:, h, :], bk(4 + h % 2, TT, T), AX_X, ALU.max, negate=True).then_inc(sem("head_max"), 1)
                        dve.wait_ge(sem("head_p"), 2 * (HEADS1 + h + 1))
                        v.tensor_copy(q26[2][:, 0:1], q26[2][:, 0:1]).then_inc(sem("head_biased"), 1)
                        dve.wait_ge(sem("head_biased"), HEADS1 + h + 1)
                    if h == AH:
                        op(v.reciprocal(arec[:, 0:AH], asum[:, 0:AH]))
                        dve.wait_ge(sem("head_o"), HEADS1 + AH)
                        for j in range(TT):
                            i = tt(oa[:, j].rearrange("p (h d) -> p h d", d=HD), bk(2 + j, AH, HD), bc(arec[:, 0:AH, j], 2, HD), ALU.mult)
                            if j == 0:
                                st.do(i)
                        i.then_inc(sem("branch_ready"), 1)
                op(v.reciprocal(arec[:, AH:], asum[:, AH:]))
                dve.wait_ge(sem("head_o"), HEADS1 + AH + MH)
                for j in range(TT):
                    i = tt(om[:, j].rearrange("p (h d) -> p h d", d=HD), bk(j, MH, HD), bc(arec[:, AH:, j], 2, HD), ALU.mult)
                    if j == 0:
                        st.do(i)
                i.then_inc(sem("branch_ready"), 1)
                for m in range(2):
                    dve.wait_ge(ring2.used, N_OA + m + 1)
                    c = slice(512 * m, 512 * m + 512)
                    for j in range(TT):
                        tt(hbuf[:, j, c], bank[2 * m + j][:, :], gates[:, j, c], ALU.mult).then_inc(sem("oa_merged"), 1)
                dve.wait_ge(ring2.used, N_OM + 1)
                for j in range(TT):
                    for q in range(2):
                        g = gates[:, j, 2 * D + 512 * q:2 * D + 512 * q + 512]
                        tt(g, bank[4 + 2 * j + q][:, :], g, ALU.mult).then_inc(sem("om_gated"), 1)
                dve.wait_ge(sem("om_gated"), 4)
                op(tt(hbuf[:, :, :], hbuf[:, :, :], gates[:, :, 2 * D:], ALU.add))
                dve.wait_ge(sem("glu_sig"), 4)
                op(tt(gl[:, :, :], gl[:, :, :], gates[:, :, D:2 * D], ALU.mult))
                dve.wait_ge(ring2.used, N_GLU + 2)
                for j in range(TT):
                    for q in range(2):
                        c = slice(512 * q, 512 * q + 512)
                        st.do(tt(gl2[:, j, c], bank[4 + 2 * j + q][:, :], gl[:, j, c], ALU.mult))
                st.settle()
                tt(hbuf[:, :, :], hbuf[:, :, :], gl2[:, :, :], ALU.add).then_inc(sem("merged_ready"), 1)
                xT_out(9)
                for m in range(4):
                    dve.wait_ge(ring2.used, N_OUT2 + m + 1)
                    xs = x[:, :, FC * m:FC * m + FC]
                    i = tt(xs, xs, bk(4 + m, TT, FC), ALU.add)
                    if m < 3:
                        st.do(i)
                i.then_inc(sem("x_mixed"), 1)

            def fed(n0, u, tx):
                dense(ring2, n0, u, tx)
                for j in range(TT):
                    for q in range(2):
                        xs = x[:, j, 512 * q:512 * q + 512]
                        i = v.scalar_tensor_tensor(xs, bank[2 * j + q][:, :], 0.5, xs, ALU.mult, ALU.add)
                        if 2 * j + q < 3:
                            st.do(i)
                i.then_inc(sem("x_fed"), 1)

            prepare()
            rms(1, x, hbuf)
            xT_out(7, gain(R2_FFN1))
            fed(N_FFN1, 1, 7)
            rms(2, x, hbuf)
            xT_out(8, gain(R2_MIX))
            branches()
            rms(3, x, hbuf)
            xT_out(10, gain(R2_FFN2))
            fed(N_FFN2, 2, 10)
            rms(4, x, hbuf)
            dve.wait_ge(sem("rms_done"), 5)
            dve.wait_ge(sem("final_gain"), 16)
            v.tensor_tensor(x[:, :, :], hbuf[:, :, :], bc(gates[:, 1, 2 * D:], 1, TT), ALU.mult).then_inc(sem("x_done"), 1)


NAMES = """x w_in mix_scale w_out gdn_conv_w gdn_a_log gdn_dt_bias gdn_norm_w cnv_dw_w cnv_dw_b cnv_ln_g cnv_ln_b
fox_f_bias ln_mix_g ln_mix_b ln_ffn_g ln_ffn_b ffn_w1 ffn_w3 ffn_w2 moe_router moe_w1 moe_w3 moe_w2 mem_2 ffn1_norm_2
ffn1_w_in_2 ffn1_w_out_2 mix_norm_2 w_in_2 a_q_gain_2 a_k_gain_2 rel_bias_2 w_o_a_2 ssm_lambda_re_2 ssm_lambda_im_2
ssm_log_dt_2 ssm_b_re_2 ssm_b_im_2 ssm_c_re_2 ssm_c_im_2 ssm_d_2 w_glu_2 mem_norm_2 w_mem_kv_2 m_q_gain_2 m_k_gain_2
w_o_m_2 w_out_2 ffn2_norm_2 ffn2_w_in_2 ffn2_w_out_2 final_norm_2""".split()


def kernel(**inputs):
    import concourse.bacc as bacc
    from concourse.bass_utils import run_bass_kernel_spmd

    nc = bacc.Bacc("TRN2", target_bir_lowering=False, num_devices=1)
    arrays, args = {}, {}
    laid = {k: np.ascontiguousarray(inputs[k]) for k in NAMES}
    laid["consts"] = np.concatenate(list(shape_constants().values()), 1)
    for name, v in laid.items():
        arrays[f"in_{name}"] = v
        args[name] = nc.dram_tensor(f"in_{name}", v.shape, mybir.dt.from_np(v.dtype), kind="ExternalInput").ap()
    out = nc.dram_tensor("out", (1, T, D), F32, kind="ExternalOutput").ap()
    two_block_kernel(nc, args, out)
    r = run_bass_kernel_spmd(nc, [arrays], core_ids=[0])
    return r.results[0]["out"]
```

```python
from contextlib import ExitStack

import numpy as np

import concourse.bass as bass
from concourse import mybir

F32 = mybir.dt.float32
F32R = mybir.dt.float32r
I32 = mybir.dt.int32
ALU = mybir.AluOpType
ACT = mybir.ActivationFunctionType
AX_X = mybir.AxisListType.X

P = 128
D = 1024
T = 256
TT = T // P
DT = D // P
DEPTH = 2
ALPHA = float((2 * DEPTH) ** 0.25)
LN_EPS, NORM_EPS = 1e-5, 1e-6
HD = 64
GW, CW, XW = 384, 256, 384
H = GW // HD
HP = H // 2
TAPS = 31
CHUNK = 64
FFN = 2816
E, FE = 8, 3584
CAP = P
FC = 256
RING = 6

C_QKV, C_DECAY, C_GATE = 0, 1152, 1164
C_GLUA, C_GLUB, C_FQ, C_FV, IN_COLS = 1548, 1804, 2060, 2828, 3218
PROJ = [(C_DECAY, 198, "tokA"), (C_FV, 195, "tokC"), (C_FV + 195, 195, "tokC")]
PROJ += [(C_QKV + 256 * i, 256 if i < 4 else 128, "qkv") for i in range(5)]
PROJ += [(C_GLUB, 256, "glub"), (C_GLUA, 256, "glua")]
PROJ += [(C_FQ + 256 * i, 256, "fqk") for i in range(3)]
PROJ += [(C_DECAY + 198, 198, "tokA")]
GLUA_LOAD = [k for _, _, k in PROJ].index("glua")
OUT_LOADS = 4
MIX_LOADS = len(PROJ) + OUT_LOADS
FFN_CHUNKS, MOE_CHUNKS = FFN // FC, FE // FC
FFN_LOADS, MOE_LOADS = 3 * FFN_CHUNKS, 3 * MOE_CHUNKS
LEVELS = 6
NEG = -1.0e30

HEADS1 = DEPTH * H
AH, IH, MH = 8, 4, 4
TOPK = 64
NS = 8
C_QA, C_KV, C_QI, C_KI, C_US, C_QM, C_G = 0, 512, 640, 896, 964, 1220, 1476
PROJ2 = [(C_QI, 256, "qi"), (C_KI, 68, "kiw"), (C_QA, 256, "qa"), (C_QA + 256, 256, "qa"), (C_KV, 128, "kv"),
         (C_US, 256, "us"), (C_QM, 256, "qm")] + [(C_G + 256 * i, 256, "gate") for i in range(12)]
N_FFN1 = 0
N_MEM = N_FFN1 + FFN_LOADS
N_PROJ2 = N_MEM + 2
N_OA = N_PROJ2 + len(PROJ2)
N_OM = N_OA + 2
N_GLU = N_OM + 1
N_OUT2 = N_GLU + 2
N_FFN2 = N_OUT2 + 4
N_END = N_FFN2 + FFN_LOADS
R2_LDT, R2_FFN1, R2_MIX, R2_MEM, R2_FFN2, R2_LRE, R2_LIM, R2_D, ROWS2 = 0, 8, 16, 24, 32, 40, 48, 56, 58
TWO_PI = (6.28125, 0.0019350051879882812, 3.0199157663446e-07)
ROUND = 12582912.0
PI_F = 3.1415925
ARENA = 27672

R_GCONV, R_DW, R_DWB, R_MIX, ROWS1 = 0, 36, 98, 100, 108


def bucket_of(rel):
    half, exact = 16, 8
    n = abs(rel)
    large = exact + int(np.float32(np.log(np.float32(max(n, 1)) / np.float32(exact))) / np.float32(np.log(128 / exact)) * np.float32(half - exact))
    return (half if rel > 0 else 0) + (n if n < exact else min(large, half - 1))


def shape_constants():
    i, j = np.arange(P)[:, None], np.arange(P)[None, :]
    same = (i // CHUNK) == (j // CHUNK)
    t = {}
    t["ident"] = i == j
    t["le"] = i <= j
    t["lt"] = i < j
    t["ones"] = np.ones((P, P))
    t["half"] = same
    t["le64"] = (i <= j) & same
    t["gt64"] = (i > j) & same
    t["inhalf"] = np.concatenate([(i // CHUNK == p) & (j >= 0) for p in range(2)], 1)
    t["gt256"] = np.concatenate([np.arange(P)[:, None] + P * a > np.arange(T)[None, :] for a in range(TT)], 1)
    b = [1 << n for n in range(LEVELS)]
    t["lvl"] = np.concatenate([(i // (2 * n) == j // (2 * n)) & (i % (2 * n) >= n) & (j % (2 * n) < n) for n in b], 1)
    diag = np.where(j > i, NEG, 0.0)
    t["foxmask"] = np.concatenate([diag, diag * 0, diag], 1)
    key = np.arange(T)[None, :]
    t["cap"] = np.concatenate([np.where(key < ((np.arange(P)[:, None] + P * a) // CHUNK + 1) * CHUNK, 3e38, -2e38) for a in range(TT)], 1)
    t["iota"] = np.broadcast_to(j, (P, P))
    t["lower8"] = np.broadcast_to((np.arange(8)[:, None] > np.arange(8)[None, :]).reshape(1, 64), (P, 64))
    t["parity"] = np.concatenate([(i // 16) % 2 == p for p in range(2)], 1)
    hot = np.zeros((P, 512))
    for c in range(511):
        hot[bucket_of(c - 255), c] = 1
    t["hot"] = hot
    return {k: np.ascontiguousarray(v, dtype=np.float32) for k, v in t.items()}


def constant_offsets():
    at, out = 0, {}
    for k, v in shape_constants().items():
        out[k] = (at, v.shape[1])
        at += v.shape[1]
    return out, at


ONCE = (
    ("lambda_inverse", "mk_sumsq", "mk_normed", "heads_sumsq", "heads_normed", "keys_chosen", "states_ready"),
    ("relb_ready", "angle_reduced", "blocks_ready", "powers_ready"),
    ("dt_ready", "unit_act", "mk_std", "mkT_act", "heads_std", "ys_ready"),
    ("router_psum", "place_psum", "bc_psum", "mkT_psum", "y_psum"),
)


def stage(name):
    return [names.index(name) for names in ONCE if name in names][0] + 1


class Steps:

    def __init__(self, eng, sem):
        self.eng, self.sem, self.n = eng, sem, 0

    def do(self, ins):
        self.n += 1
        ins.then_inc(self.sem, 1)

    def settle(self):
        self.eng.wait_ge(self.sem, self.n)


class Ring:

    def __init__(self, data, loaded, used, hi_done, lo_done, shift=0):
        self.data, self.loaded, self.used, self.shift = data, loaded, used, shift
        self.hi_done, self.lo_done = hi_done, lo_done
        self.before = None

    def slot(self, n):
        return self.data[:, (n + self.shift) % RING, :]

    def load(self, sp, n, dst, src, more=0):
        if n + 1 > RING or not isinstance(more, int):
            sp.wait_ge(self.used, n + 1 - RING + more)
        elif self.before:
            self.before(n)
        half = dst.shape[1] // 2
        if isinstance(src, tuple):
            parts = [(dst[:, :, FC * i:FC * i + FC], src[i]) for i in range(2)]
        else:
            parts = [(dst[:, half * i:half * i + half, :], src[:, half * i:half * i + half, :]) for i in range(2)]
        for d, r in parts:
            sp.dma_start(d, r).then_inc(self.loaded[n % RING], 16)

    def halves(self, n):
        return 32 * (n // RING + 1)

    def arrived(self, eng, n, rounds=0):
        eng.wait_ge(self.loaded[n % RING], self.halves(n) + 32 * rounds)


class Gated:

    def __init__(self, sem, kind, ring, hi, lo, first, split_before, chunks, chunks_before, up_banks, y_banks, x, bufs):
        self.ring, self.hi, self.lo, self.n0, self.m0 = ring, hi, lo, first, split_before
        self.chunks, self.c0, self.up_banks, self.y_banks = chunks, chunks_before, up_banks, y_banks
        self.tiles = len(y_banks)
        self.x_hi, self.x_lo = x
        self.sil, self.h, self.hT_hi, self.hT_lo = bufs
        self.sil_done, self.h_done, self.hT_psum, self.hT_hi_done, self.hT_done = (
            sem(f"{kind}_{k}") for k in ("silu", "h", "hT_psum", "hT_hi", "hT"))
        self.bodies = (chunks - 2) // 2

    def up_at(self, c):
        return max(3 * c - 1, 0)

    def down_at(self, c):
        return 3 * c + 4 if c < self.chunks - 1 else 3 * self.chunks - 1

    def hi_slot(self, n):
        return self.hi[(n + self.ring.shift) % RING]

    def lo_slot(self, n):
        return self.lo[:, (n + self.ring.shift) % RING, :]


def cols(ap, c, w):
    return ap[:, c:c + w].rearrange("(k p) c -> p k c", p=P)


def two_block_kernel(nc, a, out):
    CO, CONST_W = constant_offsets()
    with ExitStack() as ctx:
        place = {}

        def sb(name, shape, dt=F32):
            t = ctx.enter_context(nc.sbuf_tensor(name, shape, dt))
            place[name] = nc.sbuf_base - 4 * int(np.prod(shape[1:]))
            return t

        def split_parts(name, base, at, *dims):
            t = nc.alloc_sbuf_tensor_at(name, [P, int(np.prod(dims))], F32R, offset=place[base] + 4 * at)
            return shaped(t[:, :], *dims)

        def shaped(v, *dims):
            if len(dims) == 1:
                return v
            names = "abcd"[:len(dims)]
            return v.rearrange("p (" + " ".join(names) + ") -> p " + " ".join(names), **{k: d for k, d in zip(names[:-1], dims[:-1])})

        S = {}

        def sem(name):
            if name not in S:
                S[name] = ctx.enter_context(nc.semaphore(name))
            return S[name]

        bank = [ctx.enter_context(nc.psum_tensor(f"bank{i}", [P, 512], F32)) for i in range(8)]

        def bk(i, *dims):
            n = int(np.prod(dims))
            v = bank[i][:, 0:n]
            if len(dims) == 2:
                v = v.rearrange("p (a b) -> p a b", a=dims[0])
            if len(dims) == 3:
                v = v.rearrange("p (a b c) -> p a b c", a=dims[0], b=dims[1])
            return v

        consts = sb("consts_sb", [P, CONST_W])

        def const(name, k=0, w=None):
            o, width = CO[name]
            w = w or width
            return consts[:, o + k * w:o + (k + 1) * w]

        ident, ones, half = const("ident"), const("ones"), const("half")

        ring_data = sb("ring_data", [P, RING, 8 * FC])
        ring = Ring(ring_data, [sem(f"loaded{i}") for i in range(RING)], sem("weights_used"), sem("weights_hi"), sem("weights_lo"))
        x = sb("x", [P, TT, D])
        actT = sb("actT", [P, DT, T])
        lnp = sb("lnp", [P, 2, D])
        prow = sb("prow", [P, DEPTH, P])
        pcol = sb("pcol", [P, DEPTH, P])
        hpar = sb("hpar", [P, DEPTH, 24])
        nrmw = sb("nrmw", [P, DEPTH, HD])
        cln = sb("cln", [P, DEPTH, 2, CW])
        router_sb = sb("router_sb", [P, DT, E])
        headg = sb("headg", [P, 4, HD])
        toep = nc.dram_tensor("toep", (AH, P, 512), F32, kind="Internal").ap()
        small = sb("small", [P, 1024])
        npass_i = sb("npass_i", [P, 2], I32)
        arena = sb("arena", [P, ARENA])

        class Area:

            def __init__(self, at=0):
                self.at = at

            def __call__(self, *dims):
                n = int(np.prod(dims))
                v = arena[:, self.at:self.at + n]
                self.at += n
                if self.at > ARENA:
                    raise ValueError(self.at)
                names = "abcd"[:len(dims)]
                if len(dims) > 1:
                    v = v.rearrange("p (" + " ".join(names) + ") -> p " + " ".join(names),
                                    **{k: d for k, d in zip(names[:-1], dims[:-1])})
                return v

        class Small(Area):
            def __call__(self, *dims):
                n = int(np.prod(dims))
                v = small[:, self.at:self.at + n]
                self.at += n
                if self.at > 1024:
                    raise ValueError(self.at)
                names = "abcd"[:len(dims)]
                if len(dims) > 1:
                    v = v.rearrange("p (" + " ".join(names) + ") -> p " + " ".join(names),
                                    **{k: d for k, d in zip(names[:-1], dims[:-1])})
                return v

        ar = Area()
        mixed = ar(TT, D)
        tokA, tokC = ar(TT, 396), ar(TT, 390)
        at_qkv_raw = ar.at
        qkv_raw = ar(9, 3 + T)
        qkv = ar(9, T)
        fqk = ar(6, T)
        uraw = ar(2, TAPS - 1 + T)
        sigb = ar(2, T)
        uconv = sigb
        at_gm = ar.at
        GM, GU = ar(TT, H, P), ar(TT, H, P)
        X, Y = GM, GU
        Dm, DTm = ar(TT, H, P), ar(TT, H, P)
        Lm, AT = Dm, DTm
        Cl = [ar(TT, H, P) for _ in range(2)]
        at_cl = ar.at - TT * H * P
        Zs = ar(TT, H, P)
        kend, vb = ar(TT, GW), ar(TT, GW)
        GF = ar(TT, H, T)
        over = Area(at_qkv_raw)
        kbe, u_sb, wT = over(TT, GW), over(TT, GW), over(TT, HP, P)
        over = Area(at_cl)
        fs, fp, fpT = ([over(3 * P) for _ in range(2)] for _ in range(3))
        S_st = ar(HP, HD)
        oq = ar(GW)
        sq = Zs
        rn = Cl[0].rearrange("p a b c -> p (a b c)").rearrange("p (a b) -> p a b", a=6)
        def ffn_buffers(which, at, silu):
            ar = Area(at)
            return (silu, ar(2, TT, FC), split_parts(f"hT_hi{which}", "arena", ar.at, 2, 2, T),
                    split_parts(f"hT_lo{which}", "arena", ar.at + 4 * T, 2, 2, T))

        ar = Area()
        yacc = ar(TT, D)
        hi_slots = split_parts("weights_hi1", "arena", ar.at, RING, 8 * FC)
        hi1 = [hi_slots[:, i, :] for i in range(RING)]
        ar.at += RING * 8 * FC
        silu1 = ar(2, TT, FC)
        bufs1 = ffn_buffers(1, ar.at, silu1)
        ar.at += 3 * 4 * T
        Ysb = ar(D)
        Pm, PG, PGT = ar(TT, CAP), ar(TT, CAP), ar(TT, P)
        lo_slots = split_parts("weights_lo", "ring_data", 0, RING, 8 * FC)
        xT_hi, xT1_lo = split_parts("xT_hi", "actT", 0, DT, T), split_parts("xT_lo1", "arena", ar.at, DT, T)
        xg_hi, xg_lo = (split_parts(f"xg_{k}", "actT", D * i, DT, CAP) for i, k in enumerate(("hi", "lo")))
        sm = Small()
        s1, az, lg1, gs = sm(TT, 12), sm(TT, 12), sm(TT, 12), sm(TT, 12)
        beta, eg, cb, eglp = sm(TT, H), sm(TT, 24), sm(TT, H), sm(TT, 2, HP)
        ss12, rr12 = sm(TT * H), sm(TT * H)
        bst, mv, std, rstd = sm(TT, D // FC, 6), sm(TT, 2), sm(TT), sm(TT)
        fneg, fsum, frec = sm(H, TT), sm(H, TT), sm(H, TT)
        lgt, gtm, eqm = sm(TT, E), sm(TT, 64), sm(TT, 64)
        rank, sel, m1, ex, esum, gate = sm(TT, E), sm(TT, E), sm(TT), sm(TT, E), sm(TT), sm(TT, 2, E)
        posx, cnt, poscol, gcol = sm(TT, 2, E), sm(3), sm(TT), sm(TT)

        ring2 = Ring(ring_data, [sem(f"loaded2_{i}") for i in range(RING)], sem("weights2_used"), sem("weights2_hi"), sem("weights2_lo"), (2 * MIX_LOADS + FFN_LOADS) % RING)
        prow2, pcol2 = prow[:, 0, :], pcol.rearrange("p a b -> p (a b)")
        hbuf = lnp
        ar = Area()
        gates = ar(TT, 3 * D)
        score, work = ar(3 * P), ar(3 * P)
        Ct, St = ar(NS, T), ar(NS, T)
        bu = ar(NS, 2, T)
        tstage = bu.rearrange("p a b c -> p (a b c)").rearrange("p (h c) -> p h c", h=AH)
        gl = bu.rearrange("p a b c -> p (a b c)")[:, 0:TT * D].rearrange("p (j d) -> p j d", j=TT)
        gl2 = bu.rearrange("p a b c -> p (a b c)")[:, TT * D:2 * TT * D].rearrange("p (j d) -> p j d", j=TT)
        bias = ar(AH, 3 * P)
        at_att = ar.at
        al = [ar(3 * P) for _ in range(2)]
        ap_ = [ar(512) for _ in range(2)]
        apT = [ar(512) for _ in range(2)]
        rel = arena[:, at_att:at_att + IH * 3 * P].rearrange("p (h c) -> p h c", h=IH)
        at_q = ar.at
        qa, qaT = ar(TT, 512), ar(4, T)
        qm, qmT = ar(TT, 256), ar(2, T)
        qiT, kiT, kaT = ar(2, T), ar(T), ar(T)
        kva, kd = ar(TT, P), ar(TT, P)
        uT = ar(2, T)
        mkT = ar(2, T)
        at_bT = ar.at
        bT, cT = ar(2, 2, P), ar(2, 2, P)
        mkv = cln.rearrange("p a b c -> p (a b c)").rearrange("p (j c) -> p j c", j=TT)
        over = Area(at_q)
        relb, relb_bc = over(AH), over(AH, P)
        braw, blk = over(2, NS, 16), over(2, NS, 32)
        craw, cd = over(2, 2, HD), over(2, 2, 2, HD)
        btmp = over(2, NS, 16)
        at_pw = over.at
        pw = [over(NS * P) for _ in range(2)]
        memx = arena[:, at_pw:at_pw + TT * D].rearrange("p (j d) -> p j d", j=TT)
        squares = arena[:, at_bT:at_bT + D]
        mk_sq = arena[:, 3 * D * TT:3 * D * TT + TT * T].rearrange("p (j c) -> p j c", j=TT)
        memT = arena[:, 4096:6144].rearrange("p (k t) -> p k t", k=DT)
        oa, om = qa, qm
        at_bu = 3 * D * TT + 6 * P + 2 * NS * T
        hi_gates, hi_bu = (split_parts(f"weights_hi2_{i}", "arena", o, 3, 8 * FC) for i, o in enumerate((0, at_bu)))
        hi2 = [h[:, i, :] for h in (hi_gates, hi_bu) for i in range(3)]
        bufs2 = ffn_buffers(2, at_bu + 3 * 8 * FC, cln.rearrange("p a b c -> p (a b c)").rearrange("p (s j c) -> p s j c", s=2, j=TT))
        final_g = qa.rearrange("p j c -> p (j c)")
        xT2_lo = split_parts("xT_lo2", "lnp", 0, DT, T)
        sm = Small(sm.at)
        ss2, r2 = sm(TT), sm(TT)
        ssq, rq = sm(TT * 13), sm(TT * 13)
        q26 = [sm(NS) for _ in range(16)]
        wi, log_dt, lam2 = sm(TT, IH), sm(2), sm(2, NS)
        max8 = sm(2, 8)
        aneg, asum, arec = sm(AH + MH, TT), sm(AH + MH, TT), sm(AH + MH, TT)

        def bc(ap, axis, n):
            v = ap.unsqueeze(axis)
            shape = list(v.shape)
            shape[axis] = n
            return v.broadcast_to(shape)

        def slots(ap):
            return ap.rearrange("p (t q) -> p q t", q=2)

        def slot(h):
            return HP * (h % 2) + h // 2

        def four(ap):
            return ap.rearrange("p (q t) c -> p q t c", q=2)

        def bc4(ap, n):
            v = slots(ap).unsqueeze(3)
            return v.broadcast_to([P, 2, HP, n])

        def taps(l, k, tile):
            return pcol[:, l, R_DW + 2 * k + tile:R_DW + 2 * k + tile + 1]

        def pick(h):
            return slice(HD * (h % 2), HD * (h % 2) + HD)

        proj_on_act = [m for m in range(len(PROJ)) if m != GLUA_LOAD]

        def act_proj(l, m):
            return l * len(proj_on_act) + proj_on_act.index(m) + 1

        n_moe = 2 * MIX_LOADS + FFN_LOADS
        dense_banks = [[4, 5], [6, 7]], [[0, 1], [2, 3]]
        ffn = Gated(sem, "ffn", ring, hi1, lo_slots, MIX_LOADS, 0, FFN_CHUNKS, 0, *dense_banks, (xT_hi, xT1_lo), bufs1)
        ffn1 = Gated(sem, "ffn", ring2, hi2, lo_slots, N_FFN1, 0, FFN_CHUNKS, FFN_CHUNKS, *dense_banks, (xT_hi, xT2_lo), bufs2)
        ffn2 = Gated(sem, "ffn", ring2, hi2, lo_slots, N_FFN2, FFN_LOADS, FFN_CHUNKS, 2 * FFN_CHUNKS, *dense_banks, (xT_hi, xT2_lo), bufs2)
        experts = Gated(sem, "moe", ring, hi1, lo_slots, n_moe, FFN_LOADS, MOE_CHUNKS, 0, [[4], [5]], [[6, 7]], (xg_hi, xg_lo), bufs1)
        T_FFN, T_FFN1, T_MEM, T_MIX, T_MERGED, T_FFN2 = 2, 6, 7, 8, 9, 10
        SPLIT = (T_FFN, T_FFN1, T_FFN2)

        def plain(u):
            return len([i for i in range(u + 1) if i not in SPLIT])

        block = ctx.enter_context(nc.Block())

        @block.sync
        def _(sp):
            sp.dma_start(x[:, :, :], a["x"][0].rearrange("(j p) d -> p j d", p=P)).then_inc(sem("x_loaded"), 16)

            def mixer(l):
                n0 = (MIX_LOADS + FFN_LOADS) * l
                for m, (c, w, _) in enumerate(PROJ):
                    if l == 0 and m == 2:
                        ring.arrived(sp, 0)
                    ring.load(sp, n0 + m, ring.slot(n0 + m)[:, 0:8 * w].rearrange("p (k c) -> p k c", k=DT), cols(a["w_in"][l], c, w))
                for m in range(OUT_LOADS):
                    n = n0 + len(PROJ) + m
                    ring.load(sp, n, ring.slot(n).rearrange("p (k c) -> p k c", k=DT), cols(a["w_out"][l], FC * m, FC))

            def up(f, w1, w3, c, at, r):
                for half in range(2):
                    n = f.n0 + at + half
                    f.ring.load(sp, n, f.ring.slot(n).rearrange("p (k c) -> p k c", k=4),
                                tuple(w(c, half).rearrange("(k p) c -> p k c", p=P) for w in (w1, w3)), r * 6)

            def down(f, w2, c, at, r):
                n = f.n0 + at
                f.ring.load(sp, n, f.ring.slot(n).rearrange("p (f d) -> p f d", f=2), w2(c).rearrange("(f p) d -> p f d", p=P), r * 6)

            def first(f, w1, w3, w2, r=0):
                up(f, w1, w3, 0, 0, r)

            def rest(f, w1, w3, w2, r=0):
                def chunk(c, i, r):
                    up(f, w1, w3, i * 2 + c, f.up_at(c), r)
                    down(f, w2, i * 2 + (c - 1), f.down_at(c - 1), r)

                peel = f.n0 < RING
                if peel:
                    chunk(1, 0, r)
                    chunk(2, 0, r)
                with sp.Fori(int(peel), f.bodies) as i:
                    chunk(1, i, r + i)
                    chunk(2, i, r + i)
                for c in range(2 * f.bodies + 1, f.chunks):
                    chunk(c, 0, r)
                down(f, w2, f.chunks - 1, f.down_at(f.chunks - 1), r)

            def dense(f, w1, w3, w2):
                w = (lambda c, half: w1[512 * half:512 * half + 512, bass.ds(c * FC, FC)],
                     lambda c, half: w3[512 * half:512 * half + 512, bass.ds(c * FC, FC)],
                     lambda c: w2[bass.ds(c * FC, FC), :])
                first(f, *w)
                rest(f, *w)

            mixer(0)
            dense(ffn, a["ffn_w1"][0], a["ffn_w3"][0], a["ffn_w2"][0])
            mixer(1)
            w1, w3, w2 = (a[k].rearrange("o e d f -> (o e d) f") for k in ("moe_w1", "moe_w3", "moe_w2"))

            def expert(part, e, it):
                part(experts, lambda c, half: w1[bass.ds(e * D + 512 * half, 512), bass.ds(c * FC, FC)],
                     lambda c, half: w3[bass.ds(e * D + 512 * half, 512), bass.ds(c * FC, FC)],
                     lambda c: w2[bass.ds(e * FE + c * FC, FC), :], it * (MOE_LOADS // RING))

            expert(first, 0, 0)
            sp.wait_ge(sem("npass_ready"), 1)
            npass = sp.value_load(npass_i[0:1, 0:1], min_val=1, max_val=2)
            last = sp.value_load(npass_i[0:1, 1:2], min_val=E - 1, max_val=2 * E - 1)
            with sp.Fori(0, last) as it:
                expert(rest, it % E, it)
                expert(first, (it + 1) % E, it + 1)
            expert(rest, E - 1, last)
            ring2.before = lambda n: sp.wait_ge(ring.used, npass * (E * MOE_LOADS) + (n_moe + n + 1 - RING))

            def slots_of(n, k):
                return ring2.slot(n).rearrange("p (k c) -> p k c", k=k)

            w = a["ffn1_w_in_2"][0]
            dense(ffn1, w[:, 0:FFN], w[:, FFN:2 * FFN], a["ffn1_w_out_2"][0])
            for m in range(2):
                ring2.load(sp, N_MEM + m, slots_of(N_MEM + m, DT), cols(a["w_mem_kv_2"][0], FC * m, FC))
            for m, (c, w, _) in enumerate(PROJ2):
                n = N_PROJ2 + m
                ring2.load(sp, n, ring2.slot(n)[:, 0:8 * w].rearrange("p (k c) -> p k c", k=DT), cols(a["w_in_2"][0], c, w))
            for m in range(2):
                ring2.load(sp, N_OA + m, slots_of(N_OA + m, 4), a["w_o_a_2"][0][:, 512 * m:512 * m + 512].rearrange("(k p) c -> p k c", p=P))
            ring2.load(sp, N_OM, slots_of(N_OM, 2), a["w_o_m_2"][0].rearrange("(k p) c -> p k c", p=P))
            for m in range(2):
                ring2.load(sp, N_GLU + m, slots_of(N_GLU + m, 2), a["w_glu_2"][0][:, D * (1 - m):D * (2 - m)].rearrange("(k p) c -> p k c", p=P))
            for m in range(4):
                ring2.load(sp, N_OUT2 + m, slots_of(N_OUT2 + m, DT), cols(a["w_out_2"][0], FC * m, FC))
            w = a["ffn2_w_in_2"][0]
            dense(ffn2, w[:, 0:FFN], w[:, FFN:2 * FFN], a["ffn2_w_out_2"][0])
            for j in range(TT):
                sp.wait_ge(sem("x_done"), j + 1)
                sp.dma_start(out[0, P * j:P * j + P, :], x[:, j, :]).then_inc(sem("out_stored"), 16)
            sp.wait_ge(sem("out_stored"), 16 * TT)

        @block.gpsimd
        def _(pool):
            st = Steps(pool, sem("pool_steps"))
            pool.wait_ge(sem("consts_loaded"), 16)

            def layer_norm_params(u):
                g, b = [("ln_mix_g", "ln_mix_b"), ("ln_ffn_g", "ln_ffn_b")][u % 2]
                if u:
                    pool.wait_ge(sem("ln_done"), TT * u)
                pool.dma_start(lnp[:, 0, :], a[g][u // 2].partition_broadcast(P)).then_inc(sem("lnp_loaded"), 16)
                pool.dma_start(lnp[:, 1, :], a[b][u // 2].partition_broadcast(P)).then_inc(sem("lnp_loaded"), 16)

            def mixer(l):
                pool.wait_ge(sem("logs_ready"), l + 1)
                for j in range(TT):
                    nc.gpsimd.tensor_tensor(four(GM[:, j]), bc(bc(const("gt64"), 1, HP), 1, 2), bc4(gs[:, j, 0:H], P), ALU.mult).then_inc(sem("masked_logs"), 1)
                    nc.gpsimd.tensor_tensor(four(GU[:, j]), bc(bc(const("le64"), 1, HP), 1, 2), bc4(gs[:, j, 0:H], P), ALU.mult).then_inc(sem("masked_logs"), 1)
                for j in range(TT):
                    nc.gpsimd.tensor_tensor(GF[:, j], bc(const("gt256", j, T), 1, H), bc(gs[:, j, H:2 * H], 2, T), ALU.mult).then_inc(sem("masked_forget"), 1)
                for j in range(TT):
                    pool.wait_ge(sem("gdn_act"), 12 * l + 1 + 2 * (j + 1))
                    nc.gpsimd.tensor_tensor(four(Dm[:, j]), four(Dm[:, j]), bc4(beta[:, j], P), ALU.mult).then_inc(sem("decay_beta"), 1)
                for j in range(TT):
                    pool.wait_ge(sem("gdn_act"), 12 * l + 5 + 2 * (j + 1))
                    nc.gpsimd.tensor_tensor(DTm[:, j], DTm[:, j], bc(const("le64"), 1, H), ALU.mult).then_inc(sem("decay_causal"), 1)
                for n in range(LEVELS):
                    for j in range(TT):
                        if n == 0:
                            pool.wait_ge(sem("lower_ready"), l * 4 + 2 * (j + 1))
                        if n >= 2:
                            pool.wait_ge(sem("inv_z"), l * 24 + (n - 2) * 4 + 4)
                        if n == 2:
                            pool.wait_ge(sem("inv_upd"), l * 24 + 4)
                        nc.gpsimd.tensor_tensor(Cl[n % 2][:, j], Lm[:, j], bc(const("lvl", n, P), 1, H), ALU.mult).then_inc(sem("coupling"), 1)

            for l in range(DEPTH):
                layer_norm_params(2 * l)
                mixer(l)
                layer_norm_params(2 * l + 1)

            def op(ins):
                st.do(ins)
                st.settle()

            def states_parameters():
                g, tt = nc.gpsimd, nc.gpsimd.tensor_tensor
                pool.wait_ge(sem("params2_loaded"), 16 * 16)
                g.tensor_copy(relb_bc[0:32], bc(relb[0:32, :], 2, P)).then_inc(sem("pool_stage"), 1)
                st.do(g.tensor_scalar(headg[:, 0:3:2, :], headg[:, 0:3:2, :], HD ** -0.5, None, ALU.mult))
                st.do(g.memset(blk[:, :, :, :], 0.0))
                lr, li = pcol2[:, R2_LRE:R2_LRE + NS], pcol2[:, R2_LIM:R2_LIM + NS]
                cn, sn = q26[0], q26[1]
                pool.wait_ge(sem("pcol_ready"), 2)
                pool.wait_ge(sem("act_stage"), stage("dt_ready"))
                st.do(tt(q26[6], lr, q26[5], ALU.mult))
                op(tt(q26[7], li, q26[5], ALU.mult))
                op(g.tensor_scalar(q26[9], q26[7], float(1 / (2 * np.pi)), ROUND, ALU.mult, ALU.add))
                op(g.tensor_scalar(q26[9], q26[9], ROUND, None, ALU.subtract))
                for part in TWO_PI:
                    op(g.tensor_scalar(q26[10], q26[9], -part, None, ALU.mult))
                    op(tt(q26[7], q26[7], q26[10], ALU.add))
                g.tensor_scalar(q26[10], q26[7], PI_F, -PI_F, ALU.min, ALU.max).then_inc(sem("pool_stage"), 1)
                pool.wait_ge(sem("act_stage"), stage("unit_act"))
                op(tt(q26[12], q26[11], q26[11], ALU.mult))
                op(g.tensor_scalar(cn, q26[12], -2.0, 1.0, ALU.mult, ALU.add))
                st.do(tt(q26[13], q26[8], cn, ALU.mult))
                op(tt(q26[14], q26[8], sn, ALU.mult))
                op(g.tensor_scalar(q26[13], q26[13], 1.0, None, ALU.subtract))
                st.do(tt(q26[5], q26[13], lr, ALU.mult))
                st.do(tt(q26[6], q26[14], li, ALU.mult))
                st.do(tt(q26[7], q26[14], lr, ALU.mult))
                op(tt(q26[9], q26[13], li, ALU.mult))
                st.do(tt(q26[5], q26[5], q26[6], ALU.add))
                op(tt(q26[7], q26[7], q26[9], ALU.subtract))
                pool.wait_ge(sem("dve_stage"), stage("lambda_inverse"))
                st.do(tt(q26[5], q26[5], q26[15], ALU.mult))
                op(tt(q26[7], q26[7], q26[15], ALU.mult))
                fr, fi = bc(q26[5], 2, 16), bc(q26[7], 2, 16)
                for r, (b0, b1, o) in enumerate(((0, 1, ALU.subtract), (1, 0, ALU.add))):
                    st.do(tt(btmp[:, 0], fr, braw[:, b0], ALU.mult))
                    op(tt(btmp[:, 1], fi, braw[:, b1], ALU.mult))
                    for q in range(2):
                        hs = slice(HD * q, HD * q + HD)
                        op(tt(blk[hs, r, :, 16 * q:16 * q + 16], btmp[hs, 0], btmp[hs, 1], o))
                for r in range(2):
                    for q in range(2):
                        i = g.tensor_scalar(cd[:, r, :, q, :], craw[:, r], const("parity")[:, q:q + 1], (1.0, -1.0)[r], ALU.mult, ALU.mult)
                        if (r, q) != (1, 1):
                            st.do(i)
                i.then_inc(sem("pool_stage"), 1)

            pool.wait_ge(sem("ln_done"), TT * 3)
            ld = sem("params2_loaded")
            for r, k, n in ((R2_FFN1, "ffn1_norm_2", 8), (R2_MIX, "mix_norm_2", 8), (R2_MEM, "mem_norm_2", 8), (R2_FFN2, "ffn2_norm_2", 8), (R2_D, "ssm_d_2", 2)):
                pool.dma_start(prow2[r:r + n, :], a[k][0].rearrange("(t p) -> t p", p=P)).then_inc(ld, 16)
            for r, k in ((R2_LRE, "ssm_lambda_re_2"), (R2_LIM, "ssm_lambda_im_2")):
                pool.dma_start(prow2[r:r + NS, :], a[k][0].rearrange("(j q) p -> j (q p)", q=2)).then_inc(ld, 16)
            pool.dma_start(log_dt[0:NS, :], a["ssm_log_dt_2"][0].rearrange("(j q) -> j q", q=2)).then_inc(sem("dt_loaded"), 16)
            for i, k in enumerate(("a_q_gain_2", "a_k_gain_2", "m_q_gain_2", "m_k_gain_2")):
                pool.dma_start(headg[:, i, :], a[k][0].partition_broadcast(P)).then_inc(ld, 16)
            for i, k in enumerate(("ssm_b_re_2", "ssm_b_im_2")):
                pool.dma_start(braw[:, i], a[k][0].rearrange("(j q) p c -> (q p) j c", q=2)).then_inc(ld, 16)
            for i, k in enumerate(("ssm_c_re_2", "ssm_c_im_2")):
                pool.dma_start(craw[:, i], a[k][0].rearrange("(u g) c p -> (g c) u p", u=2)).then_inc(ld, 16)
            pool.dma_start(relb[0:32, :], a["rel_bias_2"]).then_inc(ld, 16)
            pool.wait_ge(sem("dt_loaded"), 16)
            nc.gpsimd.tensor_copy(prow2[R2_LDT:R2_LDT + NS, :].rearrange("j (q p) -> j q p", q=2), bc(log_dt[0:NS, :], 2, HD)).then_inc(sem("dt_spread"), 1)
            states_parameters()
            cn, sn, t0, t1 = q26[0], q26[1], q26[2], q26[3]
            pool.wait_ge(sem("ln_done"), TT * 4)
            st.do(nc.gpsimd.memset(Ct[:, :, 0:1], 1.0))
            st.do(nc.gpsimd.memset(St[:, :, 0:1], 0.0))
            n = 1
            while n < T:
                c_, s_ = bc(cn, 2, n), bc(sn, 2, n)
                st.settle()
                for dst, x0, x1, op in ((Ct, Ct, St, ALU.subtract), (St, St, Ct, ALU.add)):
                    y0, y1 = (t_[:, 0:NS * n].rearrange("p (j n) -> p j n", j=NS) for t_ in pw)
                    st.do(nc.gpsimd.tensor_tensor(y0, x0[:, :, 0:n], c_, ALU.mult))
                    st.do(nc.gpsimd.tensor_tensor(y1, x1[:, :, 0:n], s_, ALU.mult))
                    st.settle()
                    st.do(nc.gpsimd.tensor_tensor(dst[:, :, n:2 * n], y0, y1, op))
                    st.settle()
                st.do(nc.gpsimd.tensor_tensor(t0, cn, sn, ALU.mult))
                st.do(nc.gpsimd.tensor_tensor(t1, sn, sn, ALU.mult))
                st.do(nc.gpsimd.tensor_tensor(q26[4], cn, cn, ALU.mult))
                st.settle()
                st.do(nc.gpsimd.tensor_tensor(cn, q26[4], t1, ALU.subtract))
                st.do(nc.gpsimd.tensor_tensor(sn, t0, t0, ALU.add))
                n *= 2
            st.settle()
            nc.gpsimd.memset(q26[2][:, :], 0.0).then_inc(sem("pool_stage"), 1)
            pool.wait_ge(sem("pool_stage"), stage("powers_ready"))
            pool.dma_start(memx[:, :, :], a["mem_2"][0].rearrange("(j p) d -> p j d", p=P)).then_inc(sem("mem_loaded"), 16)
            for h in range(AH):
                pool.wait_ge(sem("toep_act"), h + 1)
                pool.dma_start(toep[h], tstage[:, h, :]).then_inc(sem("toep_stored"), 16)
            pool.wait_ge(sem("toep_stored"), 16 * AH)
            flat = toep.rearrange("h p c -> (h p c)")
            for j, (o, w) in enumerate(((0, P), (P, T))):
                first = 255 - P * j
                src = bass.AP(tensor=toep.tensor, offset=first, ap=[[511, P], [P * 512, AH], [1, w]])
                pool.dma_start(bias[:, :, o:o + w], src).then_inc(sem("bias_loaded"), 16)
            pool.wait_ge(sem("bias_loaded"), 32)
            pool.wait_ge(sem("dve_stage"), stage("keys_chosen"))
            for h in range(AH):
                nc.gpsimd.tensor_tensor(bias[:, h, :], bias[:, h, :], score, ALU.add).then_inc(sem("bias_ready"), 1)
            pool.wait_ge(sem("merged_ready"), 1)
            pool.dma_start(final_g, a["final_norm_2"][0].partition_broadcast(P)).then_inc(sem("final_gain"), 16)

        @block.tensor
        def _(pe):
            mm = nc.tensor.matmul

            def transpose_x(u, src, ready, banks=(0, 1, 2, 3)):
                pe.wait_ge(*ready)
                for b in range(4):
                    turn_bank(b, src, banks[b])

            def transpose_tiles(u, src, done, n, banks=(0, 1, 2, 3)):
                for j in range(TT):
                    pe.wait_ge(done, TT * n + j + 1)
                    for b in range(4):
                        for d in range(2):
                            i = nc.tensor.transpose(bk(banks[b], 2, T)[:, d, P * j:P * j + P], src[:, j, P * (2 * b + d):P * (2 * b + d + 1)], ident)
                        if j == TT - 1:
                            i.then_inc(sem("xT_psum"), 1)

            def turn_bank(b, src, to):
                for d in range(2):
                    for j in range(TT):
                        i = nc.tensor.transpose(bk(to, 2, T)[:, d, P * j:P * j + P], src[:, j, P * (2 * b + d):P * (2 * b + d + 1)], ident)
                i.then_inc(sem("xT_psum"), 1)

            def actT_arrived(u):
                if u in SPLIT:
                    pe.wait_ge(sem("xT_lo"), 4 * (SPLIT.index(u) + 1))
                else:
                    pe.wait_ge(sem("xT_act"), 2 * plain(u))
                    pe.wait_ge(sem("xT_dve"), 2 * plain(u))

            def mixer(l):
                n0 = (MIX_LOADS + FFN_LOADS) * l
                if l == 0:
                    pe.wait_ge(sem("ident_loaded"), 16)
                    transpose_x(0, x, (sem("x_loaded"), 16))
                actT_arrived(3 * l)
                for m, (c, w, kind) in enumerate(PROJ):
                    ring.arrived(pe, n0 + m)
                    if m >= 4:
                        if m - 4 == GLUA_LOAD:
                            pe.wait_ge(sem("glu_ready"), l + 1)
                        else:
                            pe.wait_ge(sem("proj_act"), act_proj(l, m - 4))
                    wt = ring.slot(n0 + m)[:, 0:8 * w].rearrange("p (k c) -> p k c", k=DT)
                    b = m % 4
                    if kind in ("tokA", "tokC"):
                        for j in range(TT):
                            for k in range(DT):
                                i = mm(bk(b, TT, w)[:, j], actT[:, k, P * j:P * j + P], wt[:, k, :], start=k == 0, stop=k == DT - 1)
                    else:
                        for t in range(w // P):
                            for k in range(DT):
                                i = mm(bk(b, 2, T)[:, t], wt[:, k, P * t:P * t + P], actT[:, k, :], start=k == 0, stop=k == DT - 1)
                    i.then_inc(ring.used, 1)
                    if l == 0 and m == 1:
                        pe.wait_ge(sem("consts_loaded"), 16)
                        pe.wait_ge(sem("params_loaded"), 16 * (10 * DEPTH + 1))
                        for k in range(DEPTH):
                            i = nc.tensor.transpose(bank[4][:, P * k:P * k + ROWS1], prow[0:ROWS1, k, :], ident[0:ROWS1, 0:ROWS1])
                        i.then_inc(sem("pcol_psum"), 1)

                pe.wait_ge(sem("logs_ready"), l + 1)
                for j in range(TT):
                    g = gs[:, j, 0:H]
                    for q, lhs in enumerate((const("le64"), const("gt64"), const("inhalf", 0, P), const("inhalf", 1, P))):
                        i = mm(bk(4, TT, 24)[:, j, 6 * q:6 * q + 6], lhs, g, start=True, stop=True)
                i.then_inc(sem("gdn_psum"), 1)
                pe.wait_ge(sem("masked_logs"), 4 * (l + 1))
                for m in range(8):
                    j, hb, tr = m % 4 // 2, m % 2, m // 4
                    if m >= 3:
                        pe.wait_ge(sem("gdn_act"), 12 * l + m - 2)
                    src = (GU if tr else GM)[:, j, 3 * hb:3 * hb + 3, :].rearrange("p a b -> p (a b)")
                    mm(bk(4 + (m + 1) % 4, 384), const("gt64") if tr else const("le64"), src, start=True, stop=True).then_inc(sem("gdn_psum"), 1)
                for m in range(3):
                    pe.wait_ge(sem("gdn_act"), 12 * l + 6 + m)
                    pe.wait_ge(sem("qk_squares"), 3 * l + m + 1)
                    mm(bk(4 + (m + 9) % 4, 512), half, sq.rearrange("p a b c -> p (a b c)")[:, 512 * m:512 * m + 512], start=True, stop=True).then_inc(sem("gdn_psum"), 1)
                pe.wait_ge(sem("masked_forget"), 2 * (l + 1))
                pe.wait_ge(sem("gdn_act"), 12 * (l + 1))
                pe.wait_ge(sem("proj_act"), act_proj(l, len(PROJ) - 1))

                def scores(h):
                    b = 4 + h % 2
                    if h >= 2:
                        pe.wait_ge(sem("head_biased"), H * l + h - 1)
                    q = [fqk[pick(h), h // 2, P * j:P * j + P] for j in range(TT)]
                    k = fqk[pick(h), 3 + h // 2, :]
                    mm(bank[b][:, 0:P], q[0], k[:, 0:P], start=True, stop=False)
                    mm(bank[b][:, 0:P], const("le"), GF[:, 0, h, 0:P], start=False, stop=True)
                    mm(bank[b][:, P:3 * P], q[1], k, start=True, stop=False)
                    mm(bank[b][:, P:3 * P], ones, GF[:, 0, h, :], start=False, stop=False)
                    mm(bank[b][:, P:3 * P], const("le"), GF[:, 1, h, :], start=False, stop=True).then_inc(sem("head_scores"), 1)

                def turn_p(h):
                    pe.wait_ge(sem("head_p"), 2 * (H * l + h + 1))
                    if h >= 2:
                        pe.wait_ge(sem("head_pT"), H * l + h - 1)
                    for t in range(3):
                        i = nc.tensor.transpose(bk(6 + h % 2, 3, P)[:, t], fp[h % 2][:, P * t:P * t + P], ident)
                    i.then_inc(sem("head_pT_psum"), 1)

                def weigh(h):
                    pe.wait_ge(sem("head_pT"), H * l + h + 1)
                    v = [tokC[:, j, HD * h:HD * h + HD] for j in range(TT)]
                    pt = fpT[h % 2]
                    mm(bk(2, H, HD)[:, h], pt[:, 0:P], v[0], start=True, stop=True)
                    mm(bk(3, H, HD)[:, h], pt[:, P:2 * P], v[0], start=True, stop=False)
                    mm(bk(3, H, HD)[:, h], pt[:, 2 * P:3 * P], v[1], start=False, stop=True).then_inc(sem("head_o"), 1)

                scores(0)
                for h in range(H):
                    if h + 1 < H:
                        scores(h + 1)
                    turn_p(h)
                    if h:
                        weigh(h - 1)
                weigh(H - 1)
                pe.wait_ge(sem("fox_done"), l + 1)
                pe.wait_ge(sem("qk_normed"), l + 1)
                pe.wait_ge(sem("glu_ready"), l + 1)
                pe.wait_ge(sem("proj_act"), act_proj(l, len(PROJ) - 1))
                for m, (t0, j) in enumerate([(3, 0), (3, 1), (6, 0), (6, 1)]):
                    for t in range(3):
                        i = nc.tensor.transpose(bk(m, 3, P)[:, t], qkv[:, t0 + t, P * j:P * j + P], ident)
                    i.then_inc(sem("kv_tok"), 1)
                for m in range(8):
                    j, hb, tr = m % 4 // 2, m % 2, m // 4
                    if tr:
                        pe.wait_ge(sem("kv_scaled"), 6 * l + (2, 4, 5, 6)[m % 4])
                    for t in range(3):
                        h = 2 * t + hb
                        i = mm(bk(m % 4 + (0 if tr else 4), 3, P)[:, t], qkv[pick(h), 3 + h // 2, P * j:P * j + P],
                               qkv[pick(h), (0 if tr else 3) + h // 2, P * j:P * j + P], start=True, stop=True)
                    i.then_inc(sem("kk_psum"), 1)
                for n in range(LEVELS):
                    for g in range(4):
                        j, hb = g // 2, g % 2
                        pe.wait_ge(sem("coupling"), 12 * l + 2 * n + j + 1)
                        if n == 0:
                            pe.wait_ge(sem("intra_ready"), 4 * l + 4)
                        else:
                            pe.wait_ge(sem("inv_upd"), 4 * (6 * l + n - 1) + g + 1)
                        for t in range(3):
                            h = 3 * hb + t
                            i = mm(bk(g, 3, P)[:, t], Cl[n % 2][:, j, h], ident if n == 0 else Y[:, j, h], start=True, stop=True)
                        i.then_inc(sem("inv_z"), 1)
                    if n == 0:
                        continue
                    for g in range(4):
                        j, hb = g // 2, g % 2
                        pe.wait_ge(sem("inv_zs"), 4 * (5 * l + n - 1) + g + 1)
                        if g >= 2:
                            pe.wait_ge(sem("inv_upd"), 4 * (6 * l + n) + g - 1)
                        for t in range(3):
                            h = 3 * hb + t
                            mm(bk(4 + 2 * (g % 2), 3, P)[:, t], Zs[:, j, h], X[:, j, h], start=True, stop=True)
                        for t in range(3):
                            h = 3 * hb + t
                            i = mm(bk(5 + 2 * (g % 2), 3, P)[:, t], X[:, j, h], Zs[:, j, h], start=True, stop=True)
                        i.then_inc(sem("inv_xy"), 1)
                pe.wait_ge(sem("inv_upd"), 4 * 6 * (l + 1))
                pe.wait_ge(sem("kv_scaled"), 6 * (l + 1))
                for j in range(TT):
                    for h in range(H):
                        i = mm(bk(j, H, HD)[:, h], Y[:, j, slot(h)], vb[:, j, HD * h:HD * h + HD], start=True, stop=True)
                    i.then_inc(sem("uw_psum"), 1)
                    for h in range(H):
                        i = mm(bk(2 + j, HP, P)[pick(h), h // 2], kbe[:, j, HD * h:HD * h + HD], Y[:, j, slot(h)], start=True, stop=True)
                    i.then_inc(sem("uw_psum"), 1)
                pe.wait_ge(sem("uw_act"), 4 * (l + 1))
                pe.wait_ge(sem("conv_done"), l + 1)
                for j in range(TT):
                    for t in range(2):
                        i = nc.tensor.transpose(bk(j, 2, P)[:, t], uconv[:, t, P * j:P * j + P], ident)
                    i.then_inc(sem("conv_tok"), 1)
                for n in range(4):
                    j, r = n // 2, slice(CHUNK * (n % 2), CHUNK * (n % 2) + CHUNK)
                    pe.wait_ge(sem("state_ready"), 5 * l + n + 1)
                    if n:
                        pe.wait_ge(sem("o_ready"), 4 * l + n)
                    for h in range(H):
                        i = mm(bk(4 + h % 2, HP, HD)[r, h // 2], wT[pick(h), j, h // 2, r], S_st[pick(h), h // 2, :], start=True, stop=True)
                    i.then_inc(sem("ws_psum"), 1)
                    for h in range(H):
                        mm(bk(2 + h % 2, HP, HD)[r, h // 2], qkv[pick(h), h // 2, P * j + CHUNK * (n % 2):P * j + CHUNK * (n % 2) + CHUNK], S_st[pick(h), h // 2, :], start=True, stop=True)
                    pe.wait_ge(sem("vnew_ready"), 2 * (4 * l + n + 1))
                    for h in range(H):
                        i = mm(bk(6, HP, HD)[pick(h), h // 2], kend[r, j, HD * h:HD * h + HD], u_sb[r, j, HD * h:HD * h + HD], start=True, stop=True)
                    i.then_inc(sem("supd_psum"), 1)
                    for h in range(H):
                        i = mm(bk(7, H, HD)[r, h], AT[r, j, slot(h), r], u_sb[r, j, HD * h:HD * h + HD], start=True, stop=True)
                    i.then_inc(sem("o_psum"), 1)
                def out(ks, first=False, last=False):
                    for m in range(OUT_LOADS):
                        n = n0 + len(PROJ) + m
                        if first:
                            ring.arrived(pe, n)
                        wt = ring.slot(n).rearrange("p (k c) -> p k c", k=DT)
                        for j in range(TT):
                            for k in ks:
                                i = mm(bk(4 + m, TT, FC)[:, j], actT[:, k, P * j:P * j + P], wt[:, k, :],
                                       start=first and j == 0 and k == ks[0], stop=False, skip_group_check=True)
                        if last:
                            i.then_inc(ring.used, 1)

                pe.wait_ge(sem("fox_done"), l + 1)
                pe.wait_ge(sem("o_ready"), 4 * (l + 1))
                turn_bank(3, mixed, 3)
                pe.wait_ge(sem("xT_act"), 2 * plain(3 * l + 1) - 1)
                out((6, 7), first=True)
                pe.wait_ge(sem("conv_out"), l + 1)
                turn_bank(2, mixed, 2)
                pe.wait_ge(sem("xT_act"), 2 * plain(3 * l + 1))
                out((4, 5))
                pe.wait_ge(sem("mixed_ready"), l + 1)
                turn_bank(1, mixed, 1)
                turn_bank(0, mixed, 0)
                pe.wait_ge(sem("xT_dve"), 2 * plain(3 * l + 1))
                out((2, 3, 0, 1), last=True)
                transpose_tiles(3 * l + 2, x, sem("ln_done"), 2 * l)

            def three(o, x_hi, x_lo, w_hi, w_lo, start, stop, **kw):
                mm(o, x_hi, w_hi, start=start, stop=False, **kw)
                mm(o, x_hi, w_lo, start=False, stop=False, **kw)
                return mm(o, x_lo, w_hi, start=False, stop=stop, **kw)

            def up(f, c, half, r=0):
                at = f.up_at(c) + half
                pe.wait_ge(f.ring.lo_done, f.m0 + at + 1 + r * 6)
                w_hi, w_lo = (w.rearrange("p (k c) -> p k c", k=4) for w in (f.hi_slot(f.n0 + at), f.lo_slot(f.n0 + at)))
                for j in range(f.tiles):
                    t = slice(P * j, P * j + P)
                    for k in range(4 * half, 4 * half + 4):
                        i = three(bank[f.up_banks[c % 2][j]][:, :], f.x_hi[:, k, t], f.x_lo[:, k, t],
                                  w_hi[:, k % 4, :], w_lo[:, k % 4, :], k == 0, k == DT - 1)
                i.then_inc(f.ring.used, 1)

            def turn(f, c, r=0):
                pe.wait_ge(f.h_done, f.c0 + c + 1 + r * 2)
                for j in range(f.tiles):
                    for q in range(2):
                        i = nc.tensor.transpose(bank[f.up_banks[c % 2][j]][:, P * q:P * q + P], f.h[:, c % 2, j, P * q:P * q + P], ident)
                i.then_inc(f.hT_psum, 1)

            def down(f, c, r=0):
                at = f.down_at(c)
                pe.wait_ge(f.ring.lo_done, f.m0 + at + 1 + r * 6)
                pe.wait_ge(f.hT_done, f.c0 + c + 1 + r * 2)
                w_hi, w_lo = (w.rearrange("p (f d) -> p f d", f=2) for w in (f.hi_slot(f.n0 + at), f.lo_slot(f.n0 + at)))
                for q in range(2):
                    for j in range(f.tiles):
                        t = slice(P * j, P * j + P)
                        for d in range(2):
                            cd = slice(512 * d, 512 * d + 512)
                            i = three(bank[f.y_banks[j][d]][:, :], f.hT_hi[:, c % 2, q, t], f.hT_lo[:, c % 2, q, t],
                                      w_hi[:, q, cd], w_lo[:, q, cd], False, False, skip_group_check=True)
                i.then_inc(f.ring.used, 1)

            def step(f, c, r=0):
                up(f, c, 0, r)
                turn(f, c - 1, r)
                up(f, c, 1, r)
                down(f, c - 1, r)

            def steps(f, r=0):
                with pe.Fori(0, f.bodies) as i:
                    step(f, 1, r + i)
                    step(f, 2, r + i)
                for c in range(2 * f.bodies + 1, f.chunks):
                    step(f, c, r)

            def dense(f, u):
                pe.wait_ge(sem("y_zeroed"), u + 1)
                up(f, 0, 0)
                up(f, 0, 1)
                steps(f)
                turn(f, f.chunks - 1)
                down(f, f.chunks - 1)

            def moe():
                f = experts
                for j in range(TT):
                    for k in range(DT):
                        i = mm(bank[4][:, E * j:E * j + E], actT[:, k, P * j:P * j + P], router_sb[:, k, :], start=k == 0, stop=k == DT - 1)
                i.then_inc(sem("pe_stage"), 1)
                pe.wait_ge(sem("sel_ready"), 1)
                mm(bank[5][:, 0:E], const("lt"), sel[:, 0], start=True, stop=True)
                mm(bank[5][:, E:2 * E], ones, sel[:, 0], start=True, stop=False)
                mm(bank[5][:, E:2 * E], const("lt"), sel[:, 1], start=False, stop=True)
                mm(bank[5][:, 2 * E:3 * E], ones, sel[:, 0], start=True, stop=False)
                mm(bank[5][:, 2 * E:3 * E], ones, sel[:, 1], start=False, stop=True).then_inc(sem("pe_stage"), 1)
                pe.wait_ge(sem("npass_ready"), 1)
                last = pe.value_load(npass_i[0:1, 1:2], min_val=E - 1, max_val=2 * E - 1)

                def gather(it):
                    pe.wait_ge(sem("perm_ready"), it + 1)
                    for b in range(2):
                        for d in range(4):
                            for j in range(TT):
                                i = mm(bk(b, 4, CAP)[:, d], x[:, j, P * (4 * b + d):P * (4 * b + d + 1)], Pm[:, j, :], start=j == 0, stop=j == TT - 1)
                        i.then_inc(sem("gather_psum"), 1)

                def scatter(it):
                    pe.wait_ge(sem("ysb_ready"), it * 2 + 2)
                    pe.wait_ge(sem("pgT_ready"), it + 1)
                    pe.wait_ge(sem("moe_zeroed"), it + 1)
                    for j in range(TT):
                        for q in range(2):
                            mm(bank[2 * j + q][:, :], PGT[:, j, :], Ysb[:, 512 * q:512 * q + 512], start=True, stop=True).then_inc(sem("scatter_psum"), 1)

                def expert(it, is_last):
                    r = it * (MOE_LOADS // RING)
                    pe.wait_ge(sem("xg_ready"), it + 1)
                    up(f, 0, 0, r)
                    up(f, 0, 1, r)
                    scatter(it)
                    steps(f, r)
                    pe.wait_ge(sem("y_added"), it * 4 + 4)
                    if not is_last:
                        gather(it + 1)
                    pe.wait_ge(sem("pg_ready"), it + 1)
                    for j in range(TT):
                        i = nc.tensor.transpose(bk(2, TT, P)[:, j], PG[:, j, :], ident)
                    i.then_inc(sem("pgT_psum"), 1)
                    turn(f, f.chunks - 1, r)
                    down(f, f.chunks - 1, r)

                gather(0)
                with pe.Fori(0, last) as it:
                    expert(it, False)
                expert(last, True)
                scatter(last + 1)

            def prepare():
                pe.wait_ge(sem("params2_loaded"), 16 * 16)
                pe.wait_ge(sem("dt_spread"), 1)
                nc.tensor.transpose(bank[4][:, 0:ROWS2], prow2[0:ROWS2, :], ident[0:ROWS2, 0:ROWS2]).then_inc(sem("pcol_psum"), 1)

            def prepare_more():
                transpose_tiles(T_MEM, memx, sem("rms_done"), 1, (4, 5, 6, 7))
                actT_arrived(T_MEM)
                pe.wait_ge(sem("pcol_ready"), 2)
                for m in range(2):
                    ring2.arrived(pe, N_MEM + m)
                    wt = ring2.slot(N_MEM + m).rearrange("p (k c) -> p k c", k=DT)
                    for j in range(TT):
                        for k in range(DT):
                            i = mm(bk((4, 7)[m], TT, FC)[:, j], memT[:, k, P * j:P * j + P], wt[:, k, :], start=k == 0, stop=k == DT - 1)
                    i.then_inc(ring2.used, 1)
                pe.wait_ge(sem("pool_stage"), stage("relb_ready"))
                for h in range(AH):
                    if h >= 2:
                        pe.wait_ge(sem("toep_act"), h - 1)
                    mm(bank[5 + h % 2][:, :], relb_bc[0:32, h, :], const("hot")[0:32, :], start=True, stop=True).then_inc(sem("toep_psum"), 1)
                pe.wait_ge(sem("toep_act"), AH)
                pe.wait_ge(sem("pool_stage"), stage("blocks_ready"))
                for g in range(2):
                    for r in range(2):
                        nc.tensor.transpose(bk(5, 2, 2, P)[:, g, r], blk[:, r, 4 * g:4 * g + 4, :].rearrange("p j c -> p (j c)"), ident)
                        i = nc.tensor.transpose(bk(6, 2, 2, P)[:, g, r], cd[:, r, g].rearrange("p q c -> p (q c)"), ident)
                i.then_inc(sem("pe_stage"), 1)

            def branches():
                def project(m):
                    c, w, kind = PROJ2[m]
                    n = N_PROJ2 + m
                    b = m % 4
                    ring2.arrived(pe, n)
                    if m >= 4:
                        pe.wait_ge(sem("proj2_act"), m - 3)
                    wt = ring2.slot(n)[:, 0:8 * w].rearrange("p (k c) -> p k c", k=DT)
                    if kind in ("qi", "us"):
                        for t in range(2):
                            for k in range(DT):
                                i = mm(bk(b, 2, T)[:, t], wt[:, k, P * t:P * t + P], actT[:, k, :], start=k == 0, stop=k == DT - 1)
                    elif kind == "kiw":
                        for q in range(2):
                            for k in range(DT):
                                mm(bank[b][HD * q:HD * q + HD, 0:T], wt[:, k, 0:HD], actT[:, k, :], start=k == 0, stop=k == DT - 1)
                        for j in range(TT):
                            for k in range(DT):
                                i = mm(bank[b][:, T + IH * j:T + IH * j + IH], actT[:, k, P * j:P * j + P], wt[:, k, HD:], start=k == 0, stop=k == DT - 1)
                    else:
                        for j in range(TT):
                            for k in range(DT):
                                i = mm(bk(b, TT, w)[:, j], actT[:, k, P * j:P * j + P], wt[:, k, :], start=k == 0, stop=k == DT - 1)
                    i.then_inc(ring2.used, 1)

                for m in range(3):
                    project(m)
                pe.wait_ge(sem("dve_stage"), stage("mk_normed"))
                for t in range(2):
                    for j in range(TT):
                        i = nc.tensor.transpose(bk(4, 2, T)[:, t, P * j:P * j + P], mkv[:, j, P * t:P * t + P], ident)
                i.then_inc(sem("pe_stage"), 1)
                for m in range(3, 7):
                    project(m)
                pe.wait_ge(sem("act_stage"), stage("mkT_act"))
                pe.wait_ge(sem("proj2_act"), 2)
                for h in range(IH):
                    q = [qiT[pick(h), h // 2, P * j:P * j + P] for j in range(TT)]
                    mm(bank[4 + h][:, 0:P], q[0], kiT[pick(h), 0:P], start=True, stop=True)
                    mm(bank[4 + h][:, P:3 * P], q[1], kiT[pick(h), :], start=True, stop=True).then_inc(sem("idx_psum"), 1)
                pe.wait_ge(sem("proj2_act"), 6)
                for j in range(NS):
                    if j < 4:
                        pe.wait_ge(sem("idx_rel"), j + 1)
                    else:
                        pe.wait_ge(sem("bu_act"), j - 3)
                    r = slice(32 * (j % 4), 32 * (j % 4) + 32)
                    for q in range(2):
                        i = mm(bk(4 + j % 4, 2, T)[:, q], bT[r, j // 4, q, :], uT[r, j // 4, :], start=True, stop=True)
                    i.then_inc(sem("bu_psum"), 1)
                for m in range(7, 13):
                    project(m)
                pe.wait_ge(sem("bu_act"), NS)
                pe.wait_ge(sem("dve_stage"), stage("heads_normed"))
                for b, (src, t) in enumerate(((qa, 0), (qa, 2), (qm, 0))):
                    for d in range(2):
                        for j in range(TT):
                            i = nc.tensor.transpose(bk(4 + b, 2, T)[:, d, P * j:P * j + P], src[:, j, P * (t + d):P * (t + d) + P], ident)
                    i.then_inc(sem("qT_psum"), 1)
                for j in range(TT):
                    i = nc.tensor.transpose(bank[7][:, P * j:P * j + P], kd[:, j, :], ident)
                i.then_inc(sem("qT_psum"), 1)
                for m in range(13, len(PROJ2)):
                    project(m)
                pe.wait_ge(sem("dve_stage"), stage("states_ready"))
                pe.wait_ge(sem("proj2_act"), len(PROJ2))
                for j in range(NS):
                    r = slice(32 * (j % 4), 32 * (j % 4) + 32)
                    for q in range(2):
                        i = mm(bank[j // 4][r, 0:T], cT[:, j // 4, q, r], bu[:, j, q, :], start=q == 0, stop=q == 1)
                i.then_inc(sem("pe_stage"), 1)
                pe.wait_ge(sem("qT_act"), 4)

                def scores(h):
                    b = 4 + h % 2
                    if h >= AH + 2:
                        pe.wait_ge(sem("head_p"), 2 * (HEADS1 + h - 1))
                    elif h >= 2:
                        pe.wait_ge(sem("head_biased"), HEADS1 + h - 1)
                    if h < AH:
                        mm(bank[b][:, 0:P], qaT[pick(h), h // 2, 0:P], kaT[pick(h), 0:P], start=True, stop=True)
                        i = mm(bank[b][:, P:3 * P], qaT[pick(h), h // 2, P:T], kaT[pick(h), :], start=True, stop=True)
                    else:
                        g = h - AH
                        for j in range(TT):
                            i = mm(bk(b, 2, T)[:, j], qmT[pick(g), g // 2, P * j:P * j + P], mkT[pick(g), g // 2, :], start=True, stop=True)
                    i.then_inc(sem("head_scores"), 1)

                def turn_p(h):
                    pe.wait_ge(sem("head_p"), 2 * (HEADS1 + h + 1))
                    if h >= 2:
                        pe.wait_ge(sem("head_pT"), HEADS1 + h - 1)
                    for t in range(3 if h < AH else 4):
                        i = nc.tensor.transpose(bk(6 + h % 2, 4, P)[:, t], ap_[h % 2][:, P * t:P * t + P], ident)
                    i.then_inc(sem("head_pT_psum"), 1)

                def weigh(h):
                    pe.wait_ge(sem("head_pT"), HEADS1 + h + 1)
                    pt = apT[h % 2]
                    if h < AH:
                        vv = [kva[:, j, HD:] for j in range(TT)]
                        mm(bk(2, AH, HD)[:, h], pt[:, 0:P], vv[0], start=True, stop=True)
                        mm(bk(3, AH, HD)[:, h], pt[:, P:2 * P], vv[0], start=True, stop=False)
                        i = mm(bk(3, AH, HD)[:, h], pt[:, 2 * P:3 * P], vv[1], start=False, stop=True)
                    else:
                        g = h - AH
                        if g == 0:
                            pe.wait_ge(sem("y_read"), 2)
                        for j in range(TT):
                            for k in range(TT):
                                i = mm(bk(j, MH, HD)[:, g], pt[:, P * (2 * j + k):P * (2 * j + k + 1)], mkv[:, k, T + HD * g:T + HD * g + HD], start=k == 0, stop=k == 1)
                    i.then_inc(sem("head_o"), 1)

                scores(0)
                for h in range(AH + MH):
                    if h + 1 < AH + MH:
                        scores(h + 1)
                    turn_p(h)
                    if h:
                        weigh(h - 1)
                weigh(AH + MH - 1)
                pe.wait_ge(sem("branch_ready"), 1)
                pe.wait_ge(sem("head_pT"), HEADS1 + AH + MH)
                for b in range(3):
                    if b == 2:
                        pe.wait_ge(sem("branch_ready"), 2)
                    for d in range(2):
                        for j in range(TT):
                            src = oa[:, j, P * (2 * b + d):P * (2 * b + d + 1)] if b < 2 else om[:, j, P * d:P * d + P]
                            i = nc.tensor.transpose(bk(4 + b, 2, T)[:, d, P * j:P * j + P], src, ident)
                    i.then_inc(sem("oT_psum"), 1)
                pe.wait_ge(sem("oT_act"), 3)
                for m in range(2):
                    ring2.arrived(pe, N_OA + m)
                    wt = ring2.slot(N_OA + m).rearrange("p (k c) -> p k c", k=4)
                    for j in range(TT):
                        for k in range(4):
                            i = mm(bank[2 * m + j][:, :], actT[:, k, P * j:P * j + P], wt[:, k, :], start=k == 0, stop=k == 3)
                    i.then_inc(ring2.used, 1)

                def wide(n, lhs, b0):
                    ring2.arrived(pe, n)
                    wt = ring2.slot(n).rearrange("p (k c) -> p k c", k=2)
                    for j in range(TT):
                        for q in range(2):
                            for k in range(2):
                                i = mm(bank[b0 + 2 * j + q][:, :], lhs[:, k, P * j:P * j + P], wt[:, k, 512 * q:512 * q + 512], start=k == 0, stop=k == 1)
                    i.then_inc(ring2.used, 1)

                wide(N_OM, actT[:, 4:6, :], 4)
                pe.wait_ge(sem("act_stage"), stage("ys_ready"))
                pe.wait_ge(sem("oa_merged"), 4)
                wide(N_GLU, uT, 0)
                pe.wait_ge(sem("om_gated"), 4)
                wide(N_GLU + 1, uT, 4)
                transpose_x(T_MERGED, hbuf, (sem("merged_ready"), 1))
                actT_arrived(T_MERGED)
                for m in range(4):
                    n = N_OUT2 + m
                    ring2.arrived(pe, n)
                    wt = ring2.slot(n).rearrange("p (k c) -> p k c", k=DT)
                    for j in range(TT):
                        for k in range(DT):
                            i = mm(bk(4 + m, TT, FC)[:, j], actT[:, k, P * j:P * j + P], wt[:, k, :], start=k == 0, stop=k == DT - 1)
                    i.then_inc(ring2.used, 1)

            mixer(0)
            actT_arrived(T_FFN)
            dense(ffn, 0)
            transpose_tiles(3, x, sem("ln_done"), 1)
            mixer(1)
            actT_arrived(5)
            moe()
            prepare()
            transpose_tiles(T_FFN1, hbuf, sem("rms_done"), 0)
            actT_arrived(T_FFN1)
            dense(ffn1, 1)
            prepare_more()
            transpose_tiles(T_MIX, hbuf, sem("rms_done"), 2)
            actT_arrived(T_MIX)
            branches()
            transpose_tiles(T_FFN2, hbuf, sem("rms_done"), 3)
            actT_arrived(T_FFN2)
            dense(ffn2, 2)

        @block.scalar
        def _(act):
            def a_(o, i, f, inc, **kw):
                nc.scalar.activation(o, i, f, **kw).then_inc(sem(inc), 1)

            def xT_out(u, scale=None, actT=actT, banks=(0, 1, 2, 3)):
                for b in (0, 2):
                    act.wait_ge(sem("xT_psum"), 4 * u + b + 1)
                    if scale is None:
                        a_(actT[:, 2 * b:2 * b + 2, :], bk(banks[b], 2, T), ACT.Copy, "xT_act")
                    else:
                        a_(actT[:, 2 * b, :], bk(banks[b], 2, T)[:, 0], ACT.Copy, "act_steps", scale=scale(2 * b))
                        a_(actT[:, 2 * b + 1, :], bk(banks[b], 2, T)[:, 1], ACT.Copy, "xT_act", scale=scale(2 * b + 1))

            def split_xT(u, scale=None):
                for b in range(4):
                    act.wait_ge(sem("xT_psum"), 4 * u + b + 1)
                    if scale is None:
                        a_(xT_hi[:, 2 * b:2 * b + 2, :], bk(b, 2, T), ACT.Copy, "xT_hi")
                    else:
                        a_(xT_hi[:, 2 * b, :], bk(b, 2, T)[:, 0], ACT.Copy, "act_steps", scale=scale(2 * b))
                        a_(xT_hi[:, 2 * b + 1, :], bk(b, 2, T)[:, 1], ACT.Copy, "xT_hi", scale=scale(2 * b + 1))

            def high(f, at, r=0):
                f.ring.arrived(act, f.n0 + at, r)
                nc.scalar.activation(f.hi_slot(f.n0 + at), f.ring.slot(f.n0 + at), ACT.Copy).then_inc(f.ring.hi_done, 1)

            def silu(f, c, r=0):
                act.wait_ge(f.ring.used, f.n0 + f.up_at(c) + 2 + r * 6)
                for j in range(f.tiles):
                    i = nc.scalar.activation(f.sil[:, c % 2, j, :], bank[f.up_banks[c % 2][j]][:, 0:FC], ACT.Silu)
                i.then_inc(f.sil_done, 1)

            def turned(f, c, r=0):
                act.wait_ge(f.hT_psum, f.c0 + c + 1 + r * 2)
                for j in range(f.tiles):
                    i = nc.scalar.activation(f.hT_hi[:, c % 2, :, P * j:P * j + P], bk(f.up_banks[c % 2][j], 2, P), ACT.Copy)
                i.then_inc(f.hT_hi_done, 1)

            def step(f, c, r=0, further=True):
                silu(f, c - 1, r)
                if further:
                    high(f, f.up_at(c + 1), r)
                turned(f, c - 1, r)
                if further:
                    high(f, f.up_at(c + 1) + 1, r)
                high(f, f.down_at(c), r)

            def steps(f, r=0, late=None):
                for at in (f.up_at(1), f.up_at(1) + 1, f.down_at(0)):
                    high(f, at, r)
                with act.Fori(0, f.bodies) as i:
                    step(f, 1, r + i)
                    step(f, 2, r + i)
                if late:
                    late()
                for c in range(2 * f.bodies + 1, f.chunks):
                    step(f, c, r, c + 1 < f.chunks)

            def dense(f, late=None):
                steps(f, 0, late)
                silu(f, f.chunks - 1)
                turned(f, f.chunks - 1)

            def norm_std(u):
                act.wait_ge(sem("ln_var"), u + 1)
                a_(std[:, 0:TT], mv[:, :, 1], ACT.Sqrt, "ln_std", bias=LN_EPS)

            def mixer(l):
                n0 = (MIX_LOADS + FFN_LOADS) * l
                def project(m):
                    c, w, kind = PROJ[m]
                    act.wait_ge(ring.used, n0 + m + 1)
                    b = m % 4
                    if kind == "tokA":
                        o = 0 if c == C_DECAY else 198
                        a_(tokA[:, :, o:o + w], bk(b, TT, w), ACT.Copy, "proj_act")
                    elif kind == "tokC":
                        a_(tokC[:, :, c - C_FV:c - C_FV + w], bk(b, TT, w), ACT.Copy, "proj_act")
                    elif kind == "qkv":
                        t = c // P
                        a_(qkv_raw[:, t:t + w // P, 3:3 + T], bk(b, 2, T)[:, 0:w // P], ACT.Copy, "proj_act")
                    elif kind == "glub":
                        a_(sigb[:, :, :], bk(b, 2, T), ACT.Sigmoid, "proj_act")
                    elif kind == "fqk":
                        t = (c - C_FQ) // P
                        nq = min(max(3 - t, 0), 2)
                        if nq:
                            a_(fqk[:, t:t + nq, :], bk(b, 2, T)[:, 0:nq], ACT.Copy, "proj_act" if nq == 2 else "act_steps", scale=HD ** -0.5)
                        if nq < 2:
                            a_(fqk[:, t + nq:t + 2, :], bk(b, 2, T)[:, nq:2], ACT.Copy, "proj_act")

                for m in range(3):
                    project(m)
                if l == 0:
                    act.wait_ge(sem("params_loaded"), 16 * (10 * DEPTH + 1))
                    a_(hpar[:, :, 18:24], hpar[:, :, 12:18], ACT.Exp, "exp_a")
                act.wait_ge(sem("gates_abs"), l + 1)
                a_(lg1[:, :, :], az[:, :, :], ACT.Exp, "act_gate", scale=-1.0)
                act.wait_ge(sem("act_gate"), 3 * l + 1)
                a_(lg1[:, :, :], lg1[:, :, :], ACT.Ln, "act_gate", bias=1.0)
                a_(beta[:, :, :], tokA[:, :, 6:12], ACT.Sigmoid, "act_gate")
                for m in range(3, len(PROJ) - 1):
                    if m == GLUA_LOAD:
                        continue
                    project(m)
                project(len(PROJ) - 1)
                for t in range(9):
                    act.wait_ge(sem("short_conv"), 9 * l + t + 1)
                    a_(qkv[:, t, :], qkv[:, t, :], ACT.Silu, "short_silu")
                for m in range(3):
                    act.wait_ge(sem("short_silu"), 9 * l + 2 * m + 2)
                    a_(sq.rearrange("p a b c -> p (a b c)")[:, 512 * m:512 * m + 512].rearrange("p (a b) -> p a b", a=2),
                       qkv[:, 2 * m:2 * m + 2, :], ACT.Square, "qk_squares")
                act.wait_ge(sem("gdn_psum"), 12 * l + 1)
                a_(eg[:, :, :], bk(4, TT, 24), ACT.Exp, "gdn_act")
                for m in range(8):
                    j, hb, tr = m % 4 // 2, m % 2, m // 4
                    act.wait_ge(sem("gdn_psum"), 12 * l + m + 2)
                    a_((DTm if tr else Dm)[:, j, 3 * hb:3 * hb + 3, :], bk(4 + (m + 1) % 4, 3, P), ACT.Exp, "gdn_act")
                for m in range(3):
                    act.wait_ge(sem("gdn_psum"), 12 * l + m + 10)
                    a_(rn[:, 2 * m:2 * m + 2, :], bk(4 + (m + 9) % 4, 2, T), ACT.Sqrt, "gdn_act", bias=NORM_EPS)
                def weights(h):
                    act.wait_ge(sem("head_max"), H * l + h + 1)
                    if h >= 2:
                        act.wait_ge(sem("head_pT_psum"), H * l + h - 1)
                    a_(fp[h % 2][:, 0:P], fs[h % 2][:, 0:P], ACT.Exp, "head_p", bias=fneg[:, h, 0:1], accum_out=fsum[:, h, 0:1])
                    a_(fp[h % 2][:, P:3 * P], fs[h % 2][:, P:3 * P], ACT.Exp, "head_p", bias=fneg[:, h, 1:2], accum_out=fsum[:, h, 1:2])

                weights(0)
                for h in range(H):
                    if h + 1 < H:
                        weights(h + 1)
                    act.wait_ge(sem("head_pT_psum"), H * l + h + 1)
                    if h >= 2:
                        act.wait_ge(sem("head_o"), H * l + h - 1)
                    a_(fpT[h % 2], bk(6 + h % 2, 384), ACT.Copy, "head_pT")
                a_(tokA[:, :, 12:396], tokA[:, :, 12:396], ACT.Silu, "gate_silu")
                for n in range(1, LEVELS):
                    for g in range(4):
                        j, hb = g // 2, g % 2
                        act.wait_ge(sem("inv_z"), 24 * l + 4 * n + g + 1)
                        a_(Zs[:, j, 3 * hb:3 * hb + 3, :], bk(g, 3, P), ACT.Copy, "inv_zs")
                for j in range(TT):
                    act.wait_ge(sem("uw_psum"), 4 * l + 2 * j + 1)
                    a_(u_sb[:, j, :], bk(j, GW), ACT.Copy, "uw_act")
                    act.wait_ge(sem("uw_psum"), 4 * l + 2 * j + 2)
                    a_(wT[:, j], bk(2 + j, HP, P), ACT.Copy, "uw_act")
                def mixed_out(i, b):
                    act.wait_ge(sem("xT_psum"), 4 * (3 * l + 1) + i + 1)
                    for d in range(2):
                        a_(actT[:, 2 * b + d, :], bk(b, 2, T)[:, d], ACT.Copy, ("act_steps", "xT_act")[d], scale=pcol[:, l, R_MIX + 2 * b + d:R_MIX + 2 * b + d + 1])

                act.wait_ge(sem("conv_var"), l + 1)
                a_(std[:, 0:TT], mv[:, :, 1], ACT.Sqrt, "conv_std", bias=LN_EPS)
                mixed_out(0, 3)
                act.wait_ge(sem("o_sumsq"), l + 1)
                a_(rr12[:, :], ss12[:, :], ACT.Sqrt, "o_std", scale=1.0 / HD, bias=NORM_EPS)
                act.wait_ge(sem("conv_normed"), l + 1)
                a_(mixed[:, :, GW:GW + CW], mixed[:, :, GW:GW + CW], ACT.Silu, "conv_out")
                mixed_out(1, 2)
                act.wait_ge(sem("mixed_ready"), l + 1)
                for at in range(2):
                    high((ffn, experts)[l], at)
                norm_std(2 * l)
                (split_xT, xT_out)[l](3 * l + 2)

            def moe():
                f = experts
                act.wait_ge(sem("router_max"), 1)
                for j in range(TT):
                    a_(ex[:, j], lgt[:, j], ACT.Exp, "router_exp", bias=m1[:, j:j + 1])
                act.wait_ge(sem("npass_ready"), 1)
                last = act.value_load(npass_i[0:1, 1:2], min_val=E - 1, max_val=2 * E - 1)

                def gathered(it):
                    for b in range(2):
                        act.wait_ge(sem("gather_psum"), it * 2 + b + 1)
                        a_(xg_hi[:, 4 * b:4 * b + 4, :], bk(b, 4, CAP), ACT.Copy, "xg_hi")

                def expert(it, is_last):
                    r = it * (MOE_LOADS // RING)
                    steps(f, r)
                    if not is_last:
                        high(f, MOE_LOADS, r)
                    silu(f, f.chunks - 1, r)
                    if not is_last:
                        gathered(it + 1)
                    act.wait_ge(sem("pgT_psum"), it + 1)
                    a_(PGT[:, :, :], bk(2, TT, P), ACT.Copy, "pgT_ready")
                    turned(f, f.chunks - 1, r)
                    if not is_last:
                        high(f, MOE_LOADS + 1, r)
                    act.wait_ge(ring.used, r * 6 + n_moe + MOE_LOADS)
                    a_(Ysb[:, 0:512], bank[6][:, :], ACT.Copy, "ysb_ready")

                gathered(0)
                with act.Fori(0, last) as it:
                    expert(it, False)
                expert(last, True)

            def gain(r):
                return lambda t: pcol2[:, r + t:r + t + 1]

            def rms(u, src, ready, tiles=False):
                for j in range(TT):
                    if j == 0 or tiles:
                        act.wait_ge(ready[0], ready[1] + j)
                    a_(hbuf[:, j, :], src[:, j, :], ACT.Square, "rms_sq", accum_out=ss2[:, j:j + 1])
                act.wait_ge(sem("rms_sq"), TT * (u + 1))
                a_(r2[:, :], ss2[:, :], ACT.Sqrt, "rms_std", scale=1.0 / D, bias=NORM_EPS)

            def prepare():
                act.wait_ge(sem("pcol_ready"), 2)
                a_(q26[5][:, :], pcol2[:, R2_LDT:R2_LDT + NS], ACT.Exp, "act_stage")

            def memory_squares():
                act.wait_ge(sem("mem_loaded"), 16)
                for j in range(TT):
                    a_(squares, memx[:, j, :], ACT.Square, "rms_sq", accum_out=ss2[:, j:j + 1])
                    act.wait_ge(sem("rms_sq"), TT + j + 1)
                a_(r2[:, :], ss2[:, :], ACT.Sqrt, "rms_std", scale=1.0 / D, bias=NORM_EPS)

            def prepare_more():
                for m in range(2):
                    act.wait_ge(ring2.used, N_MEM + m + 1)
                    a_(mkv[:, :, T * m:T * m + T], bk((4, 7)[m], TT, FC), ACT.Copy, "mkv_ready")
                for h in range(AH):
                    act.wait_ge(sem("toep_psum"), h + 1)
                    a_(tstage[:, h, :], bank[5 + h % 2][:, :], ACT.Copy, "toep_act")

            def keys_std():
                act.wait_ge(sem("dve_stage"), stage("mk_sumsq"))
                a_(rq[:, 0:TT * MH], ssq[:, 0:TT * MH], ACT.Sqrt, "act_stage", scale=1.0 / HD, bias=NORM_EPS)

            def branches():
                def project(m):
                    c, w, kind = PROJ2[m]
                    act.wait_ge(ring2.used, N_PROJ2 + m + 1)
                    b = m % 4
                    o = bk(b, TT, w)
                    if m == 0:
                        act.wait_ge(sem("pool_stage"), stage("powers_ready"))
                    if kind == "qi":
                        a_(qiT[:, :, :], o, ACT.Copy, "proj2_act")
                    elif kind == "kiw":
                        a_(kiT, bank[b][:, 0:T], ACT.Copy, "act_steps")
                        a_(wi[:, :, :], bank[b][:, T:T + TT * IH].rearrange("p (j h) -> p j h", j=TT), ACT.Copy, "proj2_act", scale=IH ** -0.5)
                    elif kind == "qa":
                        a_(qa[:, :, c - C_QA:c - C_QA + w], o, ACT.Copy, "proj2_act")
                    elif kind == "kv":
                        a_(kva[:, :, :], o, ACT.Copy, "proj2_act")
                    elif kind == "us":
                        a_(uT[:, :, :], o, ACT.Copy, "proj2_act")
                    elif kind == "qm":
                        a_(qm[:, :, :], o, ACT.Copy, "proj2_act")
                    else:
                        a_(gates[:, :, c - C_G:c - C_G + w], o, ACT.Sigmoid, "proj2_act")

                for m in range(3):
                    project(m)
                act.wait_ge(sem("pe_stage"), stage("mkT_psum"))
                a_(mkT[:, :, :], bk(4, 2, T), ACT.Copy, "act_stage")
                for m in range(3, 7):
                    project(m)
                for h in range(IH):
                    act.wait_ge(sem("idx_psum"), h + 1)
                    a_(rel[:, h, :], bk(4 + h, 3 * P), ACT.Relu, "idx_rel", scale=HD ** -0.5)
                for j in range(NS):
                    act.wait_ge(sem("bu_psum"), j + 1)
                    if j == 0:
                        act.wait_ge(sem("toep_stored"), 16 * AH)
                    a_(bu[:, j], bk(4 + j % 4, 2, T), ACT.Copy, "bu_act")
                act.wait_ge(sem("dve_stage"), stage("heads_sumsq"))
                a_(rq[:, :], ssq[:, :], ACT.Sqrt, "act_stage", scale=1.0 / HD, bias=NORM_EPS)
                for m in range(7, 13):
                    project(m)
                for b in range(4):
                    act.wait_ge(sem("qT_psum"), b + 1)
                    dst = (qaT[:, 0:2, :], qaT[:, 2:4, :], qmT[:, :, :])[b] if b < 3 else kaT
                    a_(dst, bk(4 + b, 2, T) if b < 3 else bank[7][:, 0:T], ACT.Copy, "qT_act")
                for m in range(13, len(PROJ2)):
                    project(m)
                act.wait_ge(sem("y_read"), 2)
                a_(uT[:, :, :], uT[:, :, :], ACT.Gelu_apprx_tanh, "act_stage")
                def weights(h):
                    act.wait_ge(sem("head_max"), HEADS1 + h + 1)
                    if h >= 2:
                        act.wait_ge(sem("head_pT_psum"), HEADS1 + h - 1)
                    for j in range(TT):
                        if h < AH:
                            c = (slice(0, P), slice(P, 3 * P))[j]
                            src = al[h % 2][:, c]
                        else:
                            c = slice(T * j, T * j + T)
                            src = bank[4 + h % 2][:, c]
                        a_(ap_[h % 2][:, c], src, ACT.Exp, "head_p", bias=aneg[:, h, j:j + 1], accum_out=asum[:, h, j:j + 1])

                weights(0)
                for h in range(AH + MH):
                    if h + 1 < AH + MH:
                        weights(h + 1)
                    act.wait_ge(sem("head_pT_psum"), HEADS1 + h + 1)
                    if h >= 2:
                        act.wait_ge(sem("head_o"), HEADS1 + h - 1)
                    w = 3 * P if h < AH else 4 * P
                    a_(apT[h % 2][:, 0:w], bk(6 + h % 2, w), ACT.Copy, "head_pT")
                for b in range(3):
                    act.wait_ge(sem("oT_psum"), b + 1)
                    a_(actT[:, 2 * b:2 * b + 2, :], bk(4 + b, 2, T), ACT.Copy, "oT_act")
                act.wait_ge(ring2.used, N_GLU + 1)
                for j in range(TT):
                    for q in range(2):
                        a_(gl[:, j, 512 * q:512 * q + 512], bank[2 * j + q][:, :], ACT.Sigmoid, "glu_sig")
                xT_out(T_MERGED)

            def unit_factors():
                act.wait_ge(sem("pool_stage"), stage("angle_reduced"))
                a_(q26[8][:, :], q26[6][:, :], ACT.Exp, "act_steps")
                a_(q26[1][:, :], q26[10][:, :], ACT.Sin, "act_steps")
                a_(q26[11][:, :], q26[10][:, :], ACT.Sin, "act_stage", scale=0.5)

            def first(f):
                for at in range(2):
                    high(f, at)

            act.dma_start(consts[:, 0:P], a["consts"][:, 0:P]).then_inc(sem("ident_loaded"), 16)
            act.dma_start(consts[:, P:], a["consts"][:, P:]).then_inc(sem("consts_loaded"), 16)
            ld = sem("params_loaded")
            for l in range(DEPTH):
                act.dma_start(prow[R_GCONV:R_GCONV + 36, l, :], a["gdn_conv_w"][l].rearrange("k (t p) -> (k t) p", p=P)).then_inc(ld, 16)
                act.dma_start(prow[R_DW:R_DW + 2 * TAPS, l, :], a["cnv_dw_w"][l].rearrange("k (t p) -> (k t) p", p=P)).then_inc(ld, 16)
                act.dma_start(prow[R_DWB:R_DWB + 2, l, :], a["cnv_dw_b"][l].rearrange("(t p) -> t p", p=P)).then_inc(ld, 16)
                act.dma_start(prow[R_MIX:R_MIX + 8, l, :], a["mix_scale"][l].rearrange("(t p) -> t p", p=P)).then_inc(ld, 16)
                act.dma_start(hpar[:, l, 0:6], a["gdn_dt_bias"][l].partition_broadcast(P)).then_inc(ld, 16)
                act.dma_start(hpar[:, l, 6:12], a["fox_f_bias"][l].partition_broadcast(P)).then_inc(ld, 16)
                act.dma_start(hpar[:, l, 12:18], a["gdn_a_log"][l].partition_broadcast(P)).then_inc(ld, 16)
                act.dma_start(nrmw[:, l, :], a["gdn_norm_w"][l].partition_broadcast(P)).then_inc(ld, 16)
                act.dma_start(cln[:, l, 0, :], a["cnv_ln_g"][l].partition_broadcast(P)).then_inc(ld, 16)
                act.dma_start(cln[:, l, 1, :], a["cnv_ln_b"][l].partition_broadcast(P)).then_inc(ld, 16)
            act.dma_start(router_sb[:, :, :], a["moe_router"][0].rearrange("(k p) e -> p k e", p=P)).then_inc(ld, 16)
            mixer(0)
            dense(ffn)
            norm_std(1)
            xT_out(3)
            mixer(1)
            moe()
            first(ffn1)
            norm_std(3)
            prepare()
            rms(0, x, (sem("ln_done"), TT * 3 + 1), tiles=True)
            split_xT(T_FFN1, gain(R2_FFN1))
            unit_factors()
            dense(ffn1, memory_squares)
            xT_out(T_MEM, gain(R2_MEM), memT, (4, 5, 6, 7))
            rms(2, x, (sem("x_fed"), 1))
            prepare_more()
            xT_out(T_MIX, gain(R2_MIX))
            keys_std()
            branches()
            first(ffn2)
            rms(3, x, (sem("x_mixed"), 1))
            split_xT(T_FFN2, gain(R2_FFN2))
            dense(ffn2)
            rms(4, x, (sem("x_fed"), 2))

        @block.vector
        def _(dve):
            v = nc.vector
            st = Steps(dve, sem("dve_steps"))

            def xT_out(u, scale=None, actT=actT, banks=(0, 1, 2, 3)):
                for b in (1, 3):
                    dve.wait_ge(sem("xT_psum"), 4 * u + b + 1)
                    if scale is None:
                        v.tensor_copy(actT[:, 2 * b:2 * b + 2, :], bk(banks[b], 2, T)).then_inc(sem("xT_dve"), 1)
                    else:
                        st.do(v.tensor_scalar(actT[:, 2 * b, :], bk(banks[b], 2, T)[:, 0], scale(2 * b), None, ALU.mult))
                        v.tensor_scalar(actT[:, 2 * b + 1, :], bk(banks[b], 2, T)[:, 1], scale(2 * b + 1), None, ALU.mult).then_inc(sem("xT_dve"), 1)

            def split_xT(u, lo, scale=None):
                dve.wait_ge(sem("xT_psum"), 4 * u + 4)
                for b in range(4):
                    dve.wait_ge(sem("xT_hi"), 4 * SPLIT.index(u) + b + 1)
                    if scale is None:
                        i = v.tensor_tensor(lo[:, 2 * b:2 * b + 2, :], bk(b, 2, T), xT_hi[:, 2 * b:2 * b + 2, :], ALU.subtract)
                    else:
                        for d in range(2):
                            i = v.scalar_tensor_tensor(lo[:, 2 * b + d, :], bk(b, 2, T)[:, d], scale(2 * b + d), xT_hi[:, 2 * b + d, :], ALU.mult, ALU.subtract)
                    i.then_inc(sem("xT_lo"), 1)

            def low(f, at, r=0):
                dve.wait_ge(f.ring.hi_done, f.m0 + at + 1 + r * 6)
                w = f.ring.slot(f.n0 + at)
                v.tensor_tensor(f.lo_slot(f.n0 + at), w, f.hi_slot(f.n0 + at), ALU.subtract).then_inc(f.ring.lo_done, 1)

            def product(f, c, r=0):
                dve.wait_ge(f.sil_done, f.c0 + c + 1 + r * 2)
                for j in range(f.tiles):
                    i = v.tensor_tensor(f.h[:, c % 2, j, :], f.sil[:, c % 2, j, :], bank[f.up_banks[c % 2][j]][:, FC:2 * FC], ALU.mult)
                i.then_inc(f.h_done, 1)

            def turned(f, c, r=0):
                dve.wait_ge(f.hT_hi_done, f.c0 + c + 1 + r * 2)
                for j in range(f.tiles):
                    t = slice(P * j, P * j + P)
                    i = v.tensor_tensor(f.hT_lo[:, c % 2, :, t], bk(f.up_banks[c % 2][j], 2, P), f.hT_hi[:, c % 2, :, t], ALU.subtract)
                i.then_inc(f.hT_done, 1)

            def step(f, c, r=0, further=True):
                product(f, c - 1, r)
                if further:
                    low(f, f.up_at(c + 1), r)
                turned(f, c - 1, r)
                if further:
                    low(f, f.up_at(c + 1) + 1, r)
                low(f, f.down_at(c), r)

            def steps(f, r=0, between=None, late=None):
                for at in (f.up_at(1), f.up_at(1) + 1, f.down_at(0)):
                    low(f, at, r)
                if between:
                    between()
                with dve.Fori(0, f.bodies) as i:
                    step(f, 1, r + i)
                    step(f, 2, r + i)
                if late:
                    late()
                for c in range(2 * f.bodies + 1, f.chunks):
                    step(f, c, r, c + 1 < f.chunks)

            def dense(f, u, late=None):
                dve.wait_ge(sem("xT_lo"), 4 * (u + 1))
                for b in range(4):
                    i = v.memset(bank[b][:, :], 0.0)
                    if b < 3:
                        st.do(i)
                i.then_inc(sem("y_zeroed"), 1)
                steps(f, 0, None, late)
                product(f, f.chunks - 1)
                turned(f, f.chunks - 1)
                dve.wait_ge(f.ring.used, f.n0 + FFN_LOADS)

            def statistics(src, m):
                for j in range(TT):
                    st.do(v.bn_stats(bst[:, j, m, :], src[:, j, FC * m:FC * m + FC]))

            def layer_norm(u, src):
                st.settle()
                for j in range(TT):
                    i = v.bn_aggr(mv[:, j, :], bst[:, j].rearrange("p a b -> p (a b)"))
                    if j == 0:
                        st.do(i)
                i.then_inc(sem("ln_var"), 1)
                dve.wait_ge(sem("ln_std"), u + 1)
                st.do(v.reciprocal(rstd[:, 0:TT], std[:, 0:TT]))
                st.settle()
                dve.wait_ge(sem("lnp_loaded"), 32 * (u + 1))
                for j in range(TT):
                    st.do(v.scalar_tensor_tensor(x[:, j, :], src[:, j, :], mv[:, j, 0:1], lnp[:, 0, :], ALU.subtract, ALU.mult))
                st.settle()
                for j in range(TT):
                    v.scalar_tensor_tensor(x[:, j, :], x[:, j, :], rstd[:, j:j + 1], lnp[:, 1, :], ALU.mult, ALU.add).then_inc(sem("ln_done"), 1)
                dve.wait_ge(sem("ln_done"), TT * (u + 1))

            def mixer(l):
                n0 = (MIX_LOADS + FFN_LOADS) * l
                if l == 0:
                    st.do(v.memset(qkv_raw[:, :, 0:3], 0.0))
                    st.do(v.memset(uraw[:, :, 0:TAPS - 1], 0.0))
                    for b in range(4):
                        dve.wait_ge(sem("xT_psum"), b + 1)
                        v.tensor_copy(actT[:, 2 * b:2 * b + 2, :], bk(b, 2, T)).then_inc(sem(("xT_act", "xT_dve")[b % 2]), 1)
                    dve.wait_ge(sem("pcol_psum"), 1)
                    v.tensor_copy(pcol[:, :, 0:ROWS1], bk(4, 2, P)[:, :, 0:ROWS1]).then_inc(sem("pcol_ready"), 1)
                    dve.wait_ge(sem("exp_a"), 1)
                    st.do(v.tensor_scalar(hpar[:, :, 12:18], hpar[:, :, 18:24], -1.0, None, ALU.mult))
                    st.settle()
                    st.do(v.memset(hpar[:, :, 18:24], -1.0))
                    dve.wait_ge(sem("pcol_ready"), 1)
                    st.settle()
                else:
                    st.do(v.memset(qkv_raw[:, :, 0:3], 0.0))
                    st.do(v.memset(uraw[:, :, 0:TAPS - 1], 0.0))
                st.do(v.memset(S_st[:, :, :], 0.0))
                dve.wait_ge(sem("proj_act"), act_proj(l, 2))
                st.do(v.tensor_tensor(s1[:, :, 0:6], tokA[:, :, 0:6], bc(hpar[:, l, 0:6], 1, TT), ALU.add))
                for j in range(TT):
                    st.do(v.scalar_tensor_tensor(s1[:, j, 6:12], tokC[:, j, 384:390], -1.0, hpar[:, l, 6:12], ALU.mult, ALU.subtract))
                st.settle()
                v.scalar_tensor_tensor(az[:, :, :], s1[:, :, :], -1.0, s1[:, :, :], ALU.mult, ALU.max).then_inc(sem("gates_abs"), 1)
                dve.wait_ge(sem("act_gate"), 3 * l + 2)
                st.do(v.scalar_tensor_tensor(s1[:, :, :], s1[:, :, :], 0.0, lg1[:, :, :], ALU.max, ALU.add))
                st.settle()
                v.tensor_tensor(gs[:, :, :], s1[:, :, :], bc(hpar[:, l, 12:24], 1, TT), ALU.mult).then_inc(sem("logs_ready"), 1)
                for t in range(9):
                    ld = 3 + t // 2
                    dve.wait_ge(sem("proj_act"), act_proj(l, ld))
                    wv = [pcol[:, l, R_GCONV + 9 * k + t:R_GCONV + 9 * k + t + 1] for k in range(4)]
                    st.do(v.tensor_scalar(qkv[:, t, :], qkv_raw[:, t, 0:T], wv[0], None, ALU.mult))
                    for k in range(1, 4):
                        st.settle()
                        i = v.scalar_tensor_tensor(qkv[:, t, :], qkv_raw[:, t, k:k + T], wv[k], qkv[:, t, :], ALU.mult, ALU.add)
                        if k < 3:
                            st.do(i)
                    i.then_inc(sem("short_conv"), 1)
                dve.wait_ge(ring.used, n0 + GLUA_LOAD + 1)
                dve.wait_ge(sem("proj_act"), act_proj(l, GLUA_LOAD - 1))
                v.tensor_tensor(uraw[:, :, TAPS - 1:], bk(GLUA_LOAD % 4, 2, T), sigb[:, :, :], ALU.mult).then_inc(sem("glu_ready"), 1)
                dve.wait_ge(sem("glu_ready"), l + 1)
                for k in range(TAPS):
                    if k:
                        st.settle()
                    for t in range(2):
                        if k == 0:
                            i = v.tensor_scalar(uconv[:, t, :], uraw[:, t, 0:T], taps(l, 0, t), pcol[:, l, R_DWB + t:R_DWB + t + 1], ALU.mult, ALU.add)
                        else:
                            i = v.scalar_tensor_tensor(uconv[:, t, :], uraw[:, t, k:k + T], taps(l, k, t), uconv[:, t, :], ALU.mult, ALU.add)
                        if (k, t) != (TAPS - 1, 1):
                            st.do(i)
                i.then_inc(sem("conv_done"), 1)
                for h in range(H):
                    dve.wait_ge(sem("head_scores"), H * l + h + 1)
                    if h >= 2:
                        dve.wait_ge(sem("head_p"), 2 * (H * l + h - 1))
                    v.tensor_tensor(fs[h % 2], bk(4 + h % 2, 384), const("foxmask"), ALU.add).then_inc(sem("head_biased"), 1)
                    dve.wait_ge(sem("head_biased"), H * l + h + 1)
                    st.do(v.tensor_reduce(fneg[:, h, 0:1], fs[h % 2][:, 0:P], AX_X, ALU.max, negate=True))
                    v.tensor_reduce(fneg[:, h, 1:2], fs[h % 2][:, P:3 * P], AX_X, ALU.max, negate=True).then_inc(sem("head_max"), 1)
                    if h < 3:
                        dve.wait_ge(sem("gdn_act"), 12 * l + 10 + h)
                        st.do(v.reciprocal(rn[:, 2 * h:2 * h + 2, :], rn[:, 2 * h:2 * h + 2, :]))
                    elif h == 3:
                        st.settle()
                        st.do(v.scalar_tensor_tensor(qkv[:, 0:3, :], qkv[:, 0:3, :], HD ** -0.5, rn[:, 0:3, :], ALU.mult, ALU.mult))
                    elif h == 4:
                        v.tensor_tensor(qkv[:, 3:6, :], qkv[:, 3:6, :], rn[:, 3:6, :], ALU.mult).then_inc(sem("qk_normed"), 1)
                dve.wait_ge(sem("head_p"), 2 * H * (l + 1))
                st.do(v.reciprocal(frec[:, :, :], fsum[:, :, :]))
                st.settle()
                dve.wait_ge(sem("head_o"), H * (l + 1))
                for j in range(TT):
                    i = v.tensor_tensor(mixed[:, j, GW + CW:].rearrange("p (h d) -> p h d", h=H), bk(2 + j, H, HD), bc(frec[:, :, j], 2, HD), ALU.mult)
                    if j == 0:
                        st.do(i)
                i.then_inc(sem("fox_done"), 1)
                dve.wait_ge(sem("qk_normed"), l + 1)
                dve.wait_ge(sem("act_gate"), 3 * l + 3)
                st.do(v.tensor_tensor(cb[:, :, :], beta[:, :, :], eg[:, :, 0:6], ALU.mult))
                st.settle()
                for p in range(2):
                    for q in range(2):
                        st.do(v.tensor_copy(eglp[HD * q:HD * q + HD, :, p, :], eg[HD * q:HD * q + HD, :, 12 + 6 * p + q:18 + 6 * p:2]))
                for j in range(TT):
                    dve.wait_ge(sem("kv_tok"), 4 * l + j + 1)
                    kt = bk(j, H, HD)
                    v.tensor_tensor(kbe[:, j].rearrange("p (h d) -> p h d", h=H), kt, bc(cb[:, j], 2, HD), ALU.mult).then_inc(sem("kv_scaled"), 1)
                    v.tensor_tensor(kend[:, j].rearrange("p (h d) -> p h d", h=H), kt, bc(eg[:, j, 6:12], 2, HD), ALU.mult).then_inc(sem("kv_scaled"), 1)
                for j in range(TT):
                    dve.wait_ge(sem("kv_tok"), 4 * l + 2 + j + 1)
                    v.tensor_tensor(vb[:, j].rearrange("p (h d) -> p h d", h=H), bk(2 + j, H, HD), bc(beta[:, j], 2, HD), ALU.mult).then_inc(sem("kv_scaled"), 1)
                for m in range(4):
                    j, hb = m // 2, m % 2
                    dve.wait_ge(sem("kk_psum"), 8 * l + m + 1)
                    dve.wait_ge(sem("decay_beta"), 2 * l + j + 1)
                    v.tensor_tensor(Lm[:, j, 3 * hb:3 * hb + 3, :], bk(4 + m, 3, P), Dm[:, j, 3 * hb:3 * hb + 3, :], ALU.mult).then_inc(sem("lower_ready"), 1)
                for m in range(4):
                    j, hb = m // 2, m % 2
                    dve.wait_ge(sem("kk_psum"), 8 * l + 4 + m + 1)
                    dve.wait_ge(sem("decay_causal"), 2 * l + j + 1)
                    v.tensor_tensor(AT[:, j, 3 * hb:3 * hb + 3, :], bk(m, 3, P), DTm[:, j, 3 * hb:3 * hb + 3, :], ALU.mult).then_inc(sem("intra_ready"), 1)

                for n in range(LEVELS):
                    for g in range(4):
                        j, hb = g // 2, g % 2
                        hs = slice(3 * hb, 3 * hb + 3)
                        if n == 0:
                            dve.wait_ge(sem("inv_z"), 24 * l + g + 1)
                            st.do(v.tensor_tensor(X[:, j, hs, :], bc(ident, 1, 3), Cl[0][:, j, hs, :], ALU.subtract))
                            v.tensor_tensor(Y[:, j, hs, :], bc(ident, 1, 3), bk(g, 3, P), ALU.subtract).then_inc(sem("inv_upd"), 1)
                            continue
                        dve.wait_ge(sem("inv_xy"), 4 * (5 * l + n - 1) + g + 1)
                        dve.wait_ge(sem("inv_upd"), 4 * (6 * l + n - 1) + g + 1)
                        st.do(v.tensor_tensor(X[:, j, hs, :], X[:, j, hs, :], bk(4 + 2 * (g % 2), 3, P), ALU.subtract))
                        v.tensor_tensor(Y[:, j, hs, :], Y[:, j, hs, :], bk(5 + 2 * (g % 2), 3, P), ALU.subtract).then_inc(sem("inv_upd"), 1)
                v.tensor_copy(S_st[:, :, :], S_st[:, :, :]).then_inc(sem("state_ready"), 1)
                dve.wait_ge(sem("uw_act"), 4 * (l + 1))
                for n in range(4):
                    j, p = n // 2, n % 2
                    r = slice(CHUNK * p, CHUNK * p + CHUNK)
                    dve.wait_ge(sem("ws_psum"), 4 * l + n + 1)
                    dve.wait_ge(sem("state_ready"), 5 * l + n + 1)
                    for q in range(2):
                        uq = u_sb[r, j, :].rearrange("p (t q d) -> p q t d", q=2, d=HD)[:, q]
                        v.tensor_tensor(uq, uq, bk(4 + q, HP, HD)[r], ALU.subtract).then_inc(sem("vnew_ready"), 1)
                    dve.wait_ge(sem("supd_psum"), 4 * l + n + 1)
                    st.do(v.tensor_tensor(S_st[:, :, :], S_st[:, :, :], bc(eglp[:, j, p, :], 2, HD), ALU.mult))
                    for q in range(2):
                        st.do(v.tensor_tensor(oq[r].rearrange("p (t q d) -> p q t d", q=2, d=HD)[:, q], bk(2 + q, HP, HD)[r], bc(eg[r, j, q:6:2], 2, HD), ALU.mult))
                    st.settle()
                    v.tensor_tensor(S_st[:, :, :], S_st[:, :, :], bk(6, HP, HD), ALU.add).then_inc(sem("state_ready"), 1)
                    if n == 1:
                        dve.wait_ge(sem("conv_tok"), 2 * (l + 1))
                        for jt in range(TT):
                            st.do(v.bn_stats(bst[:, jt, 0, :], bk(jt, CW)))
                        st.settle()
                        st.do(v.bn_aggr(mv[:, 0, :], bst[:, 0, 0, :]))
                        v.bn_aggr(mv[:, 1, :], bst[:, 1, 0, :]).then_inc(sem("conv_var"), 1)
                    dve.wait_ge(sem("o_psum"), 4 * l + n + 1)
                    v.tensor_tensor(mixed[r, j, 0:GW], oq[r], bk(7, GW)[r], ALU.add).then_inc(sem("o_ready"), 1)
                dve.wait_ge(sem("o_ready"), 4 * (l + 1))
                dve.wait_ge(sem("gate_silu"), l + 1)
                for j in range(TT):
                    st.do(v.tensor_tensor(kbe[:, j, :], mixed[:, j, 0:GW], mixed[:, j, 0:GW], ALU.mult))
                st.settle()
                v.tensor_reduce(ss12[:, :], kbe.rearrange("p j (h d) -> p (j h) d", h=H), AX_X, ALU.add).then_inc(sem("o_sumsq"), 1)
                dve.wait_ge(sem("conv_std"), l + 1)
                st.do(v.reciprocal(rstd[:, 0:TT], std[:, 0:TT]))
                st.settle()
                for j in range(TT):
                    v.tensor_scalar(mixed[:, j, GW:GW + CW], bk(j, CW), mv[:, j, 0:1], rstd[:, j:j + 1], ALU.subtract, ALU.mult).then_inc(sem("conv_ln"), 1)
                dve.wait_ge(sem("conv_ln"), 2 * (l + 1))
                st.do(v.tensor_tensor(mixed[:, :, GW:GW + CW], mixed[:, :, GW:GW + CW], bc(cln[:, l, 0, :], 1, TT), ALU.mult))
                st.settle()
                v.tensor_tensor(mixed[:, :, GW:GW + CW], mixed[:, :, GW:GW + CW], bc(cln[:, l, 1, :], 1, TT), ALU.add).then_inc(sem("conv_normed"), 1)
                for j in range(TT):
                    m3 = mixed[:, j, 0:GW].rearrange("p (h d) -> p h d", h=H)
                    st.do(v.tensor_tensor(m3, m3, bc(nrmw[:, l, :], 1, H), ALU.mult))
                dve.wait_ge(sem("o_std"), l + 1)
                st.do(v.reciprocal(rr12[:, :], rr12[:, :]))
                st.settle()
                for j in range(TT):
                    m3 = mixed[:, j, 0:GW].rearrange("p (h d) -> p h d", h=H)
                    st.do(v.tensor_tensor(m3, m3, bc(rr12[:, H * j:H * j + H], 2, HD), ALU.mult))
                st.settle()
                for j in range(TT):
                    i = v.tensor_tensor(mixed[:, j, 0:GW], mixed[:, j, 0:GW], tokA[:, j, 12:396], ALU.mult)
                    if j == 0:
                        st.do(i)
                i.then_inc(sem("mixed_ready"), 1)
                for i, b in ((2, 1), (3, 0)):
                    dve.wait_ge(sem("xT_psum"), 4 * (3 * l + 1) + i + 1)
                    for d in range(2):
                        o = v.tensor_scalar(actT[:, 2 * b + d, :], bk(b, 2, T)[:, d], pcol[:, l, R_MIX + 2 * b + d:R_MIX + 2 * b + d + 1], None, ALU.mult)
                        o.then_inc((st.sem, sem("xT_dve"))[d], 1)
                    st.n += 1
                for at in range(2):
                    low((ffn, experts)[l], at)
                for m in range(OUT_LOADS):
                    dve.wait_ge(ring.used, n0 + len(PROJ) + m + 1)
                    xs = x[:, :, FC * m:FC * m + FC]
                    st.do(v.scalar_tensor_tensor(xs, xs, ALPHA, bk(4 + m, TT, FC), ALU.mult, ALU.add))
                    st.settle()
                    statistics(x, m)
                layer_norm(2 * l, x)
                if l == 0:
                    split_xT(T_FFN, xT1_lo)
                else:
                    xT_out(3 * l + 2)

            def moe():
                f = experts
                dve.wait_ge(sem("pe_stage"), stage("router_psum"))
                st.do(v.tensor_copy(lgt[:, :, :], bk(4, TT, E)))
                st.settle()
                v.tensor_reduce(m1[:, :], lgt[:, :, :], AX_X, ALU.max, negate=True).then_inc(sem("router_max"), 1)
                for j in range(TT):
                    row, col = bc(lgt[:, j], 1, E), bc(lgt[:, j], 2, E)
                    st.do(v.tensor_tensor(gtm[:, j].rearrange("p (a b) -> p a b", a=E), row, col, ALU.is_gt))
                    st.do(v.tensor_tensor(eqm[:, j].rearrange("p (a b) -> p a b", a=E), row, col, ALU.is_equal))
                st.settle()
                st.do(v.tensor_tensor(eqm[:, :, :], eqm[:, :, :], bc(const("lower8"), 1, TT), ALU.mult))
                st.settle()
                st.do(v.tensor_tensor(gtm[:, :, :], gtm[:, :, :], eqm[:, :, :], ALU.add))
                st.settle()
                st.do(v.tensor_reduce(rank.rearrange("p j e -> p (j e)"), gtm.rearrange("p j (a b) -> p (j a) b", a=E), AX_X, ALU.add))
                st.settle()
                v.tensor_scalar(sel[:, :, :], rank[:, :, :], 1.5, None, ALU.is_lt).then_inc(sem("sel_ready"), 1)
                dve.wait_ge(sem("sel_ready"), 1)
                dve.wait_ge(sem("router_exp"), 2)
                st.do(v.tensor_tensor(ex[:, :, :], ex[:, :, :], sel[:, :, :], ALU.mult))
                st.settle()
                st.do(v.tensor_reduce(esum[:, :], ex[:, :, :], AX_X, ALU.add))
                st.settle()
                st.do(v.reciprocal(esum[:, :], esum[:, :]))
                st.settle()
                for p in range(2):
                    st.do(v.tensor_tensor(gate[:, :, p, :], ex[:, :, :], bc(esum[:, :], 2, E), ALU.mult))
                dve.wait_ge(sem("pe_stage"), stage("place_psum"))
                st.do(v.tensor_copy(posx[:, :, 0, :], bk(5, TT, E)))
                st.do(v.tensor_reduce(cnt[:, 0:1], bank[5][:, 2 * E:3 * E], AX_X, ALU.max))
                st.settle()
                st.do(v.scalar_tensor_tensor(posx[:, :, 0, :], posx[:, :, 0, :], 1.0, sel[:, :, :], ALU.add, ALU.mult))
                st.do(v.tensor_scalar(cnt[:, 1:2], cnt[:, 0:1], CAP + 0.5, 1.0, ALU.is_gt, ALU.add))
                st.settle()
                st.do(v.tensor_scalar(cnt[:, 2:3], cnt[:, 1:2], float(E), -1.0, ALU.mult, ALU.add))
                st.do(v.tensor_scalar(posx[:, :, 1, :], posx[:, :, 0, :], -1.0 - CAP, None, ALU.add))
                st.settle()
                v.tensor_copy(npass_i[:, :], cnt[:, 1:3]).then_inc(sem("npass_ready"), 1)
                st.do(v.tensor_scalar(posx[:, :, 0, :], posx[:, :, 0, :], -1.0, None, ALU.add))
                dve.wait_ge(sem("npass_ready"), 1)
                st.settle()
                last = dve.value_load(npass_i[0:1, 1:2], min_val=E - 1, max_val=2 * E - 1)

                def choose(it):
                    v.tensor_copy(poscol[:, :], posx.rearrange("p j a e -> p j (a e)")[:, :, bass.ds(it, 1)].rearrange("p j o -> p (j o)")).then_inc(sem("pos_ready"), 1)
                    dve.wait_ge(sem("pos_ready"), it + 1)
                    v.tensor_scalar(Pm[:, 0, :], const("iota"), poscol[:, 0:1], None, ALU.is_equal)
                    v.tensor_scalar(Pm[:, 1, :], const("iota"), poscol[:, 1:2], None, ALU.is_equal).then_inc(sem("perm_ready"), 1)

                def weigh(it):
                    v.tensor_copy(gcol[:, :], gate.rearrange("p j a e -> p j (a e)")[:, :, bass.ds(it, 1)].rearrange("p j o -> p (j o)")).then_inc(sem("gcol_ready"), 1)
                    dve.wait_ge(sem("gcol_ready"), it + 1)
                    v.tensor_scalar(PG[:, 0, :], Pm[:, 0, :], gcol[:, 0:1], None, ALU.mult)
                    v.tensor_scalar(PG[:, 1, :], Pm[:, 1, :], gcol[:, 1:2], None, ALU.mult).then_inc(sem("pg_ready"), 1)

                def gathered(it):
                    for b in range(2):
                        dve.wait_ge(sem("xg_hi"), it * 2 + b + 1)
                        i = v.tensor_tensor(xg_lo[:, 4 * b:4 * b + 4, :], bk(b, 4, CAP), xg_hi[:, 4 * b:4 * b + 4, :], ALU.subtract)
                    i.then_inc(sem("xg_ready"), 1)

                def add(it):
                    for j in range(TT):
                        for q in range(2):
                            dve.wait_ge(sem("scatter_psum"), it * 4 + 2 * j + q + 1)
                            ys = yacc[:, j, 512 * q:512 * q + 512]
                            v.tensor_tensor(ys, ys, bank[2 * j + q][:, :], ALU.add).then_inc(sem("y_added"), 1)

                def expert(it, is_last):
                    r = it * (MOE_LOADS // RING)
                    dve.wait_ge(sem("perm_ready"), it + 1)
                    weigh(it)
                    dve.wait_ge(sem("pg_ready"), it + 1)
                    if not is_last:
                        choose(it + 1)
                    steps(f, r, lambda: add(it))
                    if not is_last:
                        low(f, MOE_LOADS, r)
                    product(f, f.chunks - 1, r)
                    if not is_last:
                        gathered(it + 1)
                    turned(f, f.chunks - 1, r)
                    if not is_last:
                        low(f, MOE_LOADS + 1, r)
                    dve.wait_ge(ring.used, r * 6 + n_moe + MOE_LOADS)
                    v.tensor_copy(Ysb[:, 512:1024], bank[7][:, :]).then_inc(sem("ysb_ready"), 1)
                    dve.wait_ge(sem("ysb_ready"), it * 2 + 4)
                    v.memset(bank[6][:, :], 0.0)
                    v.memset(bank[7][:, :], 0.0).then_inc(sem("moe_zeroed"), 1)

                choose(0)
                gathered(0)
                st.do(v.tensor_scalar(yacc[:, :, :], x[:, :, :], ALPHA, None, ALU.mult))
                v.memset(PGT[:, :, :], 0.0).then_inc(sem("pgT_ready"), 1)
                v.memset(Ysb[:, 0:512], 0.0).then_inc(sem("ysb_ready"), 1)
                v.memset(Ysb[:, 512:], 0.0).then_inc(sem("ysb_ready"), 1)
                v.memset(bank[6][:, :], 0.0)
                v.memset(bank[7][:, :], 0.0).then_inc(sem("moe_zeroed"), 1)
                st.settle()
                with dve.Fori(0, last) as it:
                    expert(it, False)
                expert(last, True)
                add(last + 1)
                dve.wait_ge(sem("y_added"), last * 4 + 8)

            mixer(0)
            dense(ffn, 0)
            for j in range(TT):
                for q in range(2):
                    xs = x[:, j, 512 * q:512 * q + 512]
                    st.do(v.scalar_tensor_tensor(xs, xs, ALPHA, bank[2 * j + q][:, :], ALU.mult, ALU.add))
            st.settle()
            for m in range(D // FC):
                statistics(x, m)
            layer_norm(1, x)
            xT_out(3)
            mixer(1)
            moe()
            for m in range(D // FC):
                statistics(yacc, m)
            layer_norm(3, yacc)

            def gain(r):
                return lambda t: pcol2[:, r + t:r + t + 1]

            def rms(u, src, dst):
                dve.wait_ge(sem("rms_std"), u + 1)
                st.do(v.reciprocal(r2[:, :], r2[:, :]))
                st.settle()
                for j in range(TT):
                    v.tensor_scalar(dst[:, j, :], src[:, j, :], r2[:, j:j + 1], None, ALU.mult).then_inc(sem("rms_done"), 1)

            def op(ins):
                st.do(ins)
                st.settle()

            def prepare():
                dve.wait_ge(sem("pcol_psum"), 2)
                v.tensor_copy(pcol2[:, 0:ROWS2], bank[4][:, 0:ROWS2]).then_inc(sem("pcol_ready"), 1)
            def lambda_inverse():
                lr, li = pcol2[:, R2_LRE:R2_LRE + NS], pcol2[:, R2_LIM:R2_LIM + NS]
                st.do(v.tensor_tensor(lam2[:, 0, :], lr, lr, ALU.mult))
                op(v.tensor_tensor(lam2[:, 1, :], li, li, ALU.mult))
                op(v.tensor_tensor(lam2[:, 0, :], lam2[:, 0, :], lam2[:, 1, :], ALU.add))
                v.reciprocal(q26[15][:, :], lam2[:, 0, :]).then_inc(sem("dve_stage"), 1)

            def prepare_more():
                tt = v.tensor_tensor
                dve.wait_ge(sem("pool_stage"), stage("blocks_ready"))
                dve.wait_ge(sem("pe_stage"), stage("bc_psum"))
                op(v.tensor_copy(bT[:, :, :, :], bk(5, 2, 2, P)))
                op(v.tensor_copy(cT[:, :, :, :], bk(6, 2, 2, P)))

            def keys_norm():
                tt = v.tensor_tensor
                dve.wait_ge(sem("mkv_ready"), 1)
                mk = mkv[:, :, 0:T]
                op(tt(mk_sq, mk, mk, ALU.mult))
                v.tensor_reduce(ssq[:, 0:TT * MH].rearrange("p (j h) -> p j h", j=TT), mk_sq.rearrange("p j (h d) -> p j h d", d=HD), AX_X, ALU.add).then_inc(sem("dve_stage"), 1)
                dve.wait_ge(sem("act_stage"), stage("mk_std"))
                op(v.reciprocal(rq[:, 0:TT * MH], rq[:, 0:TT * MH]))
                for j in range(TT):
                    m3 = mkv[:, j, 0:T].rearrange("p (h d) -> p h d", d=HD)
                    op(tt(m3, m3, bc(rq[:, MH * j:MH * j + MH], 2, HD), ALU.mult))
                    i = tt(m3, m3, bc(headg[:, 3, :], 1, MH), ALU.mult)
                    if j == 0:
                        op(i)
                i.then_inc(sem("dve_stage"), 1)

            def branches():
                tt = v.tensor_tensor
                dve.wait_ge(sem("proj2_act"), 7)
                st.do(tt(hbuf[:, :, 0:512], qa[:, :, :], qa[:, :, :], ALU.mult))
                st.do(tt(hbuf[:, :, 512:576], kva[:, :, 0:HD], kva[:, :, 0:HD], ALU.mult))
                st.do(tt(hbuf[:, :, 576:832], qm[:, :, :], qm[:, :, :], ALU.mult))
                st.settle()
                v.tensor_reduce(ssq.rearrange("p (j h) -> p j h", j=TT), hbuf[:, :, 0:832].rearrange("p j (h d) -> p j h d", d=HD), AX_X, ALU.add).then_inc(sem("dve_stage"), 1)
                dve.wait_ge(sem("act_stage"), stage("heads_std"))
                op(v.reciprocal(rq[:, :], rq[:, :]))
                for j in range(TT):
                    r = rq[:, 13 * j:13 * j + 13]
                    q3, m3 = (t[:, j, :].rearrange("p (h d) -> p h d", d=HD) for t in (qa, qm))
                    st.do(tt(q3, q3, bc(r[:, 0:8], 2, HD), ALU.mult))
                    st.do(tt(m3, m3, bc(r[:, 9:13], 2, HD), ALU.mult))
                    st.do(v.scalar_tensor_tensor(kd[:, j, 0:HD], kva[:, j, 0:HD], r[:, 8:9], headg[:, 1, :], ALU.mult, ALU.mult))
                    st.settle()
                    st.do(tt(q3, q3, bc(headg[:, 0, :], 1, AH), ALU.mult))
                    st.do(tt(m3, m3, bc(headg[:, 2, :], 1, MH), ALU.mult))
                    i = v.tensor_copy(kd[:, j, HD:], kd[:, j, 0:HD])
                    if j == 0:
                        st.do(i)
                i.then_inc(sem("dve_stage"), 1)
                dve.wait_ge(sem("dve_stage"), stage("heads_normed"))
                dve.wait_ge(sem("idx_rel"), IH)
                parts = (slice(0, P), slice(P, 3 * P))
                for h in range(IH):
                    for j, c in enumerate(parts):
                        w = wi[:, j, h:h + 1]
                        if h == 0:
                            st.do(v.tensor_scalar(score[:, c], rel[:, h, c], w, None, ALU.mult))
                        else:
                            st.do(v.scalar_tensor_tensor(score[:, c], rel[:, h, c], w, score[:, c], ALU.mult, ALU.add))
                    st.settle()
                cap = const("cap")
                st.do(tt(work[:, parts[0]], score[:, parts[0]], cap[:, 0:P], ALU.min))
                st.do(tt(work[:, parts[1]], score[:, parts[1]], cap[:, T:2 * T], ALU.min))
                st.settle()
                for _ in range(TOPK // 8):
                    for j, c in enumerate(parts):
                        st.do(v.max(max8[:, j, :], work[:, c]))
                    st.settle()
                    for j, c in enumerate(parts):
                        st.do(v.match_replace(out=work[:, c], in_to_replace=max8[:, j, :], in_values=work[:, c], imm_value=-3.0e38))
                    st.settle()
                v.tensor_scalar(score, work, -2.5e38, NEG, ALU.is_gt, ALU.mult).then_inc(sem("dve_stage"), 1)
                dve.wait_ge(sem("bu_act"), NS)
                dve.wait_ge(sem("pool_stage"), stage("powers_ready"))
                for sign in (-1, 1):
                    for j in range(NS):
                        c, s, br, bi = Ct[:, j, :], St[:, j, :], bu[:, j, 0, :], bu[:, j, 1, :]
                        t0, t1, t2 = hbuf[:, 0, 0:T], hbuf[:, 0, T:2 * T], hbuf[:, 0, 2 * T:3 * T]
                        st.do(tt(t0, br, s, ALU.mult))
                        st.do(tt(t1, bi, s, ALU.mult))
                        st.do(tt(t2, bi, c, ALU.mult))
                        st.do(tt(br, br, c, ALU.mult))
                        st.settle()
                        st.do(tt(br, br, t1, ALU.add if sign < 0 else ALU.subtract))
                        i = tt(bi, t2, t0, ALU.subtract if sign < 0 else ALU.add)
                        if (sign, j) == (1, NS - 1):
                            i.then_inc(sem("dve_stage"), 1)
                            break
                        st.do(i)
                        st.settle()
                        if sign < 0:
                            m = q26[8][:, j:j + 1].broadcast_to([P, T])
                            st.do(v.tensor_tensor_scan(br, m, br, 0.0, ALU.mult, ALU.add))
                            st.do(v.tensor_tensor_scan(bi, m, bi, 0.0, ALU.mult, ALU.add))
                            st.settle()
                dve.wait_ge(sem("pe_stage"), stage("y_psum"))
                for t in range(2):
                    v.scalar_tensor_tensor(uT[:, t, :], uT[:, t, :], pcol2[:, R2_D + t:R2_D + t + 1], bank[t][:, 0:T], ALU.mult, ALU.add).then_inc(sem("y_read"), 1)
                for h in range(AH + MH):
                    dve.wait_ge(sem("head_scores"), HEADS1 + h + 1)
                    if h >= 2:
                        dve.wait_ge(sem("head_p"), 2 * (HEADS1 + h - 1))
                    if h < AH:
                        dve.wait_ge(sem("bias_ready"), h + 1)
                        v.tensor_tensor(al[h % 2], bk(4 + h % 2, 3 * P), bias[:, h, :], ALU.add).then_inc(sem("head_biased"), 1)
                        dve.wait_ge(sem("head_biased"), HEADS1 + h + 1)
                        st.do(v.tensor_reduce(aneg[:, h, 0:1], al[h % 2][:, 0:P], AX_X, ALU.max, negate=True))
                        v.tensor_reduce(aneg[:, h, 1:2], al[h % 2][:, P:3 * P], AX_X, ALU.max, negate=True).then_inc(sem("head_max"), 1)
                    else:
                        v.tensor_reduce(aneg[:, h, :], bk(4 + h % 2, TT, T), AX_X, ALU.max, negate=True).then_inc(sem("head_max"), 1)
                    if h == AH + 1:
                        op(v.reciprocal(arec[:, 0:AH], asum[:, 0:AH]))
                        dve.wait_ge(sem("head_o"), HEADS1 + AH)
                        for j in range(TT):
                            i = tt(oa[:, j].rearrange("p (h d) -> p h d", d=HD), bk(2 + j, AH, HD), bc(arec[:, 0:AH, j], 2, HD), ALU.mult)
                            if j == 0:
                                st.do(i)
                        i.then_inc(sem("branch_ready"), 1)
                dve.wait_ge(sem("head_p"), 2 * (HEADS1 + AH + MH))
                op(v.reciprocal(arec[:, AH:], asum[:, AH:]))
                dve.wait_ge(sem("head_o"), HEADS1 + AH + MH)
                for j in range(TT):
                    i = tt(om[:, j].rearrange("p (h d) -> p h d", d=HD), bk(j, MH, HD), bc(arec[:, AH:, j], 2, HD), ALU.mult)
                    if j == 0:
                        st.do(i)
                i.then_inc(sem("branch_ready"), 1)
                for m in range(2):
                    dve.wait_ge(ring2.used, N_OA + m + 1)
                    c = slice(512 * m, 512 * m + 512)
                    for j in range(TT):
                        tt(hbuf[:, j, c], bank[2 * m + j][:, :], gates[:, j, c], ALU.mult).then_inc(sem("oa_merged"), 1)
                dve.wait_ge(ring2.used, N_OM + 1)
                for j in range(TT):
                    for q in range(2):
                        g = gates[:, j, 2 * D + 512 * q:2 * D + 512 * q + 512]
                        tt(g, bank[4 + 2 * j + q][:, :], g, ALU.mult).then_inc(sem("om_gated"), 1)
                dve.wait_ge(sem("om_gated"), 4)
                op(tt(hbuf[:, :, :], hbuf[:, :, :], gates[:, :, 2 * D:], ALU.add))
                dve.wait_ge(sem("glu_sig"), 4)
                op(tt(gl[:, :, :], gl[:, :, :], gates[:, :, D:2 * D], ALU.mult))
                dve.wait_ge(ring2.used, N_GLU + 2)
                for j in range(TT):
                    for q in range(2):
                        c = slice(512 * q, 512 * q + 512)
                        st.do(tt(gl2[:, j, c], bank[4 + 2 * j + q][:, :], gl[:, j, c], ALU.mult))
                st.settle()
                tt(hbuf[:, :, :], hbuf[:, :, :], gl2[:, :, :], ALU.add).then_inc(sem("merged_ready"), 1)
                xT_out(T_MERGED)
                for m in range(4):
                    dve.wait_ge(ring2.used, N_OUT2 + m + 1)
                    xs = x[:, :, FC * m:FC * m + FC]
                    i = tt(xs, xs, bk(4 + m, TT, FC), ALU.add)
                    if m < 3:
                        st.do(i)
                i.then_inc(sem("x_mixed"), 1)

            def fed(f, u, late=None):
                dense(f, u, late)
                for j in range(TT):
                    for q in range(2):
                        xs = x[:, j, 512 * q:512 * q + 512]
                        i = v.scalar_tensor_tensor(xs, bank[2 * j + q][:, :], 0.5, xs, ALU.mult, ALU.add)
                        if 2 * j + q < 3:
                            st.do(i)
                i.then_inc(sem("x_fed"), 1)

            prepare()
            dve.wait_ge(sem("pcol_ready"), 2)
            lambda_inverse()
            low(ffn1, 0)
            rms(0, x, hbuf)
            low(ffn1, 1)
            split_xT(T_FFN1, xT2_lo, gain(R2_FFN1))
            fed(ffn1, 1, lambda: rms(1, memx, memx))
            xT_out(T_MEM, gain(R2_MEM), memT, (4, 5, 6, 7))
            rms(2, x, hbuf)
            prepare_more()
            xT_out(T_MIX, gain(R2_MIX))
            keys_norm()
            branches()
            low(ffn2, 0)
            rms(3, x, hbuf)
            low(ffn2, 1)
            split_xT(T_FFN2, xT2_lo, gain(R2_FFN2))
            fed(ffn2, 2)
            dve.wait_ge(sem("final_gain"), 16)
            dve.wait_ge(sem("rms_std"), 5)
            st.do(v.reciprocal(r2[:, :], r2[:, :]))
            st.settle()
            for j in range(TT):
                v.scalar_tensor_tensor(x[:, j, :], x[:, j, :], r2[:, j:j + 1], final_g, ALU.mult, ALU.mult).then_inc(sem("x_done"), 1)


NAMES = """x w_in mix_scale w_out gdn_conv_w gdn_a_log gdn_dt_bias gdn_norm_w cnv_dw_w cnv_dw_b cnv_ln_g cnv_ln_b
fox_f_bias ln_mix_g ln_mix_b ln_ffn_g ln_ffn_b ffn_w1 ffn_w3 ffn_w2 moe_router moe_w1 moe_w3 moe_w2 mem_2 ffn1_norm_2
ffn1_w_in_2 ffn1_w_out_2 mix_norm_2 w_in_2 a_q_gain_2 a_k_gain_2 rel_bias_2 w_o_a_2 ssm_lambda_re_2 ssm_lambda_im_2
ssm_log_dt_2 ssm_b_re_2 ssm_b_im_2 ssm_c_re_2 ssm_c_im_2 ssm_d_2 w_glu_2 mem_norm_2 w_mem_kv_2 m_q_gain_2 m_k_gain_2
w_o_m_2 w_out_2 ffn2_norm_2 ffn2_w_in_2 ffn2_w_out_2 final_norm_2""".split()


def kernel(**inputs):
    import concourse.bacc as bacc
    from concourse.bass_utils import run_bass_kernel_spmd

    nc = bacc.Bacc("TRN2", target_bir_lowering=False, num_devices=1)
    arrays, args = {}, {}
    laid = {k: np.ascontiguousarray(inputs[k]) for k in NAMES}
    laid["consts"] = np.concatenate(list(shape_constants().values()), 1)
    for name, v in laid.items():
        arrays[f"in_{name}"] = v
        args[name] = nc.dram_tensor(f"in_{name}", v.shape, mybir.dt.from_np(v.dtype), kind="ExternalInput").ap()
    out = nc.dram_tensor("out", (1, T, D), F32, kind="ExternalOutput").ap()
    two_block_kernel(nc, args, out)
    r = run_bass_kernel_spmd(nc, [arrays], core_ids=[0])
    return r.results[0]["out"]
```
